# Optimizing a Trainium2 kernel written in Bass

```python
import jax
import jax.numpy as jnp
from jax import lax
import numpy as np

D_MODEL = 1024
BATCH = 1
SEQ = 512
DEPTH = 2
DEC_BATCH = 1
DEC_SEQ = 32
PAST_LEN = 256

CHUNK = 64
N_META = 16
A_HEADS = 8
A_NOPE = 64
A_ROPE = 32
A_V = 64
A_LORA = 256
ROPE_THETA = 10000.0
B_QHEADS = 8
B_KVHEADS = 2
B_G = B_QHEADS // B_KVHEADS
B_HD = 64
B_WINDOW = 128
B_WCHUNKS = B_WINDOW // CHUNK
C_HEADS = 4
C_DK = 128
C_DV = 256
C_LOWRANK = 16
C_TAU = 16.0
C_BLOCK = 16
D_FF = 4 * D_MODEL
N_BRANCH = 3
Q_BLOCK = 128
EPS = 1e-6
NEG = -1e30
SPLITS = (A_HEADS * A_NOPE, A_HEADS * A_ROPE, A_LORA, A_ROPE,
          B_QHEADS * B_HD, B_KVHEADS * B_HD, B_KVHEADS * B_HD,
          C_HEADS * C_DK, C_HEADS * C_DK, C_HEADS * C_DV, C_LOWRANK, C_HEADS * C_DV,
          N_BRANCH * D_MODEL)
D_IN = sum(SPLITS)

kernel_name = 'hybrid_mla_swa_gla_stream_step'

def _rmsnorm(x, g):
    xf = x.astype(jnp.float32)
    y = xf * lax.rsqrt(jnp.mean(xf * xf, axis=-1, keepdims=True) + EPS)
    return (y * g.astype(jnp.float32)).astype(x.dtype)

def _split_cols(z):
    return jnp.split(z, [int(i) for i in np.cumsum(SPLITS)[:-1]], axis=-1)

def _rope(x, pos):
    half = A_ROPE // 2
    inv = ROPE_THETA ** (-jnp.arange(half, dtype=jnp.float32) / half)
    ang = pos.astype(jnp.float32)[:, None] * inv[None, :]
    ang = ang.reshape((ang.shape[0],) + (1,) * (x.ndim - 3) + (half,))
    cos = jnp.cos(ang).astype(x.dtype)
    sin = jnp.sin(ang).astype(x.dtype)
    x1, x2 = x[..., :half], x[..., half:]
    return jnp.concatenate([x1 * cos - x2 * sin, x1 * sin + x2 * cos], axis=-1)

def _alibi_slopes():
    h = jnp.arange(1, B_QHEADS + 1, dtype=jnp.float32)
    return (2.0 ** (-8.0 * h / B_QHEADS)).reshape(B_KVHEADS, B_G)

def _mla_expand(c, w_uk, w_uv):
    return (jnp.einsum('btc,chd->bthd', c, w_uk), jnp.einsum('btc,chd->bthd', c, w_uv))

def _mla_attend(qn, qr_rot, qr_raw, qpos, mkn, mkr, mv, kn, kr, v, kpos):
    scale = (A_NOPE + A_ROPE) ** -0.5
    s_meta = (jnp.einsum('bqhd,bmhd->bhqm', qn, mkn)
              + jnp.einsum('bqhr,bmr->bhqm', qr_raw, mkr)).astype(jnp.float32) * scale
    s_fr = (jnp.einsum('bqhd,bkhd->bhqk', qn, kn)
            + jnp.einsum('bqhr,bkr->bhqk', qr_rot, kr)).astype(jnp.float32) * scale
    visible = (kpos[None, :] // CHUNK) <= (qpos[:, None] // CHUNK)
    s_fr = jnp.where(visible, s_fr, NEG)
    prob = jax.nn.softmax(jnp.concatenate([s_meta, s_fr], axis=-1), axis=-1).astype(v.dtype)
    m = mkn.shape[1]
    return (jnp.einsum('bhqm,bmhv->bqhv', prob[..., :m], mv)
            + jnp.einsum('bhqk,bkhv->bqhv', prob[..., m:], v))

def _mla_blocked(qn, qr_rot, qr_raw, qpos, keys):
    t = qn.shape[1]
    if t <= Q_BLOCK:
        return _mla_attend(qn, qr_rot, qr_raw, qpos, *keys)
    nb = t // Q_BLOCK

    def blocks(a):
        return jnp.swapaxes(a.reshape((a.shape[0], nb, Q_BLOCK) + a.shape[2:]), 0, 1)

    out = lax.map(lambda a: _mla_attend(a[0], a[1], a[2], a[3], *keys),
                  (blocks(qn), blocks(qr_rot), blocks(qr_raw), qpos.reshape(nb, Q_BLOCK)))
    out = jnp.swapaxes(out, 0, 1)
    return out.reshape((out.shape[0], t) + out.shape[3:])

def _swa_attend(q, k, v, qpos, kpos, mk, mv, sinks, slopes):
    scale = B_HD ** -0.5
    s_meta = jnp.einsum('bnqhgd,bmhd->bnhgqm', q, mk).astype(jnp.float32) * scale
    s_fr = jnp.einsum('bnqhgd,bnkhd->bnhgqk', q, k).astype(jnp.float32) * scale
    dist = jnp.abs(qpos[:, :, None] - kpos[:, None, :]).astype(jnp.float32)
    cq = qpos[:, :, None] // CHUNK
    ck = kpos[:, None, :] // CHUNK
    visible = (kpos[:, None, :] >= 0) & (ck <= cq) & (ck > cq - B_WCHUNKS)
    s_fr = jnp.where(visible[None, :, None, None],
                     s_fr - slopes[:, :, None, None] * dist[None, :, None, None], NEG)
    sink = jnp.broadcast_to(sinks.astype(jnp.float32)[:, :, None, None], s_meta.shape[:-1] + (1,))
    prob = jax.nn.softmax(jnp.concatenate([sink, s_meta, s_fr], axis=-1), axis=-1).astype(v.dtype)
    m = mk.shape[1]
    return (jnp.einsum('bnhgqm,bmhd->bnqhgd', prob[..., 1:1 + m], mv)
            + jnp.einsum('bnhgqk,bnkhd->bnqhgd', prob[..., 1 + m:], v))

def _chunk_band(a):
    nc = a.shape[1]
    parts = []
    for j in range(B_WCHUNKS - 1, -1, -1):
        pads = ((0, 0), (j, 0)) + ((0, 0),) * (a.ndim - 2)
        parts.append(jnp.pad(a, pads)[:, :nc])
    return jnp.concatenate(parts, axis=2)

def _gla_scan(q, k, v, loga, s0):
    b_sz, t = q.shape[:2]
    pad = (-t) % C_BLOCK

    def prep(a):
        a = jnp.pad(a, ((0, 0), (0, pad)) + ((0, 0),) * (a.ndim - 2))
        return jnp.moveaxis(a.reshape((b_sz, -1, C_BLOCK) + a.shape[2:]), 1, 0)

    tri = jnp.tril(jnp.ones((C_BLOCK, C_BLOCK), dtype=bool))

    def step(s, blk):
        qb, kb, vb, lb = blk
        qf, kf, vf = qb.astype(jnp.float32), kb.astype(jnp.float32), vb.astype(jnp.float32)
        b = jnp.cumsum(lb, axis=1)
        bl = b[:, -1]
        diff = b[:, :, None] - b[:, None, :]
        decay = jnp.exp(jnp.where(tri[None, :, :, None, None], diff, NEG))
        attn = jnp.einsum('bthd,bshd,btshd->bhts', qf, kf, decay)
        o = (jnp.einsum('bhts,bshv->bthv', attn, vf)
             + jnp.einsum('bthd,bhdv->bthv', qf * jnp.exp(b), s))
        s = jnp.exp(bl)[..., None] * s + jnp.einsum('bshd,bshv->bhdv', kf * jnp.exp(bl[:, None] - b), vf)
        return s, o

    s, o = lax.scan(step, s0.astype(jnp.float32), (prep(q), prep(k), prep(v), prep(loga)))
    o = jnp.moveaxis(o, 0, 1)
    o = o.reshape((b_sz, -1) + o.shape[3:])[:, :t]
    return o.astype(v.dtype), s.astype(s0.dtype)

def _gla_branch(qc, kc, vc, alr, gc, s0, p):
    b_sz, t = qc.shape[:2]
    q = qc.reshape(b_sz, t, C_HEADS, C_DK) * (C_DK ** -0.5)
    k = kc.reshape(b_sz, t, C_HEADS, C_DK)
    v = vc.reshape(b_sz, t, C_HEADS, C_DV)
    loga = (jax.nn.log_sigmoid((alr @ p['w_alpha'] + p['b_alpha']).astype(jnp.float32))
            / C_TAU).reshape(b_sz, t, C_HEADS, C_DK)
    o, s = _gla_scan(q, k, v, loga, s0)
    o = _rmsnorm(o, p['g_gla']) * jax.nn.silu(gc.reshape(b_sz, t, C_HEADS, C_DV))
    return o.reshape(b_sz, t, C_HEADS * C_DV), s

def _merge(oa, ob, oc, gate, p):
    g = jax.nn.sigmoid(gate).reshape(gate.shape[:-1] + (N_BRANCH, D_MODEL))
    y = (g[..., 0, :] * (oa @ p['w_up_a']) + g[..., 1, :] * (ob @ p['w_up_b'])
         + g[..., 2, :] * (oc @ p['w_up_c']))
    return y @ p['w_out']

def _residual(x, mix, p):
    x = x + _rmsnorm(mix, p['g_post_mix'])
    f = jnp.square(jax.nn.relu(_rmsnorm(x, p['g_pre_mlp']) @ p['w_ff1'])) @ p['w_ff2']
    return x + _rmsnorm(f, p['g_post_mlp'])

def _prompt_layer(x, pos, p):
    m = N_META
    b_sz, t, _ = x.shape
    s_len = t - m
    h = _rmsnorm(x, p['g_pre_mix'])
    (qn, qr, ckv, kr, qb, kb, vb, qc, kc, vc, alr, gc, gate) = _split_cols(h @ p['w_in'])
    zpos = jnp.zeros((m,), jnp.int32)
    qn = qn.reshape(b_sz, t, A_HEADS, A_NOPE)
    qr = qr.reshape(b_sz, t, A_HEADS, A_ROPE)
    c = _rmsnorm(ckv, p['g_kv'])
    kn, va = _mla_expand(c, p['w_uk'], p['w_uv'])
    kr_f = _rope(kr[:, m:], pos)
    meta_a = (kn[:, :m], kr[:, :m], va[:, :m])
    oa_m = _mla_attend(qn[:, :m], qr[:, :m], qr[:, :m], zpos, *meta_a,
                       kn[:, :0], kr_f[:, :0], va[:, :0], pos[:0])
    oa_f = _mla_blocked(qn[:, m:], _rope(qr[:, m:], pos), qr[:, m:], pos,
                        meta_a + (kn[:, m:], kr_f, va[:, m:], pos))
    oa = jnp.concatenate([oa_m, oa_f], axis=1).reshape(b_sz, t, A_HEADS * A_V)
    sinks = p['b_sinks'].reshape(B_KVHEADS, B_G)
    slopes = _alibi_slopes()
    qb = qb.reshape(b_sz, t, B_KVHEADS, B_G, B_HD)
    kb = kb.reshape(b_sz, t, B_KVHEADS, B_HD)
    vb = vb.reshape(b_sz, t, B_KVHEADS, B_HD)
    mk, mv = kb[:, :m], vb[:, :m]
    ob_m = _swa_attend(qb[:, None, :m], kb[:, None, :0], vb[:, None, :0], zpos[None],
                       jnp.zeros((1, 0), jnp.int32), mk, mv, sinks, slopes)
    nc = s_len // CHUNK
    qpos_c = pos.reshape(nc, CHUNK)
    kpos_band = jnp.concatenate([qpos_c - j * CHUNK for j in range(B_WCHUNKS - 1, -1, -1)], axis=-1)
    kf = kb[:, m:].reshape(b_sz, nc, CHUNK, B_KVHEADS, B_HD)
    vf = vb[:, m:].reshape(b_sz, nc, CHUNK, B_KVHEADS, B_HD)
    ob_f = _swa_attend(qb[:, m:].reshape(b_sz, nc, CHUNK, B_KVHEADS, B_G, B_HD),
                       _chunk_band(kf), _chunk_band(vf), qpos_c, kpos_band, mk, mv, sinks, slopes)
    ob = jnp.concatenate([ob_m.reshape(b_sz, m, -1), ob_f.reshape(b_sz, s_len, -1)], axis=1)
    s0 = jnp.zeros((b_sz, C_HEADS, C_DK, C_DV), x.dtype)
    oc, s_c = _gla_branch(qc, kc, vc, alr, gc, s0, p)
    x = _residual(x, _merge(oa, ob, oc, gate, p), p)
    w = min(B_WINDOW, s_len)
    new_state = (c[:, m:], kr_f, c[:, :m], kr[:, :m], kb[:, t - w:], vb[:, t - w:], mk, mv, s_c)
    return x, new_state

def _sample_layer(x, pos, p, c_ckv, c_kr, c_mckv, c_mkr, c_bk, c_bv, c_mbk, c_mbv, s_c):
    b_sz, t, _ = x.shape
    past = c_ckv.shape[1]
    h = _rmsnorm(x, p['g_pre_mix'])
    (qn, qr, ckv, kr, qb, kb, vb, qc, kc, vc, alr, gc, gate) = _split_cols(h @ p['w_in'])
    qn = qn.reshape(b_sz, t, A_HEADS, A_NOPE)
    qr = qr.reshape(b_sz, t, A_HEADS, A_ROPE)
    c = _rmsnorm(ckv, p['g_kv'])
    kr_r = _rope(kr, pos)
    c_all = jnp.concatenate([c_ckv, c], axis=1)
    kr_all = jnp.concatenate([c_kr, kr_r], axis=1)
    kn, va = _mla_expand(c_all, p['w_uk'], p['w_uv'])
    mkn, mva = _mla_expand(c_mckv, p['w_uk'], p['w_uv'])
    kpos = jnp.arange(past + t, dtype=jnp.int32)
    oa = _mla_blocked(qn, _rope(qr, pos), qr, pos,
                      (mkn, c_mkr, mva, kn, kr_all, va, kpos)).reshape(b_sz, t, A_HEADS * A_V)
    sinks = p['b_sinks'].reshape(B_KVHEADS, B_G)
    slopes = _alibi_slopes()
    qb = qb.reshape(b_sz, t, B_KVHEADS, B_G, B_HD)
    k_all = jnp.concatenate([c_bk, kb.reshape(b_sz, t, B_KVHEADS, B_HD)], axis=1)
    v_all = jnp.concatenate([c_bv, vb.reshape(b_sz, t, B_KVHEADS, B_HD)], axis=1)
    w = c_bk.shape[1]
    kpos_b = jnp.arange(past - w, past + t, dtype=jnp.int32)
    ob = _swa_attend(qb[:, None], k_all[:, None], v_all[:, None], pos[None], kpos_b[None],
                     c_mbk, c_mbv, sinks, slopes).reshape(b_sz, t, B_QHEADS * B_HD)
    oc, s_new = _gla_branch(qc, kc, vc, alr, gc, s_c, p)
    x = _residual(x, _merge(oa, ob, oc, gate, p), p)
    return x, (c, kr_r, k_all[:, -w:], v_all[:, -w:], s_new)

def setup_inputs(seed: int = 0) -> dict:
    key = jax.random.key(seed)
    ks = iter(jax.random.split(key, 32))

    def nrm(shape, scale=1.0):
        return scale * jax.random.normal(next(ks), shape, jnp.float32)

    def gain(shape):
        return 1.0 + 0.05 * jax.random.normal(next(ks), shape, jnp.float32)

    win = min(B_WINDOW, PAST_LEN)
    return {
        'x_prompt': nrm((BATCH, SEQ, D_MODEL)),
        'x_sample': nrm((DEC_BATCH, DEC_SEQ, D_MODEL)),
        'cache_A_ckv': nrm((DEPTH, DEC_BATCH, PAST_LEN, A_LORA)),
        'cache_A_krope': nrm((DEPTH, DEC_BATCH, PAST_LEN, A_ROPE)),
        'cache_A_meta_ckv': nrm((DEPTH, DEC_BATCH, N_META, A_LORA)),
        'cache_A_meta_krope': nrm((DEPTH, DEC_BATCH, N_META, A_ROPE)),
        'cache_B_k': nrm((DEPTH, DEC_BATCH, win, B_KVHEADS, B_HD)),
        'cache_B_v': nrm((DEPTH, DEC_BATCH, win, B_KVHEADS, B_HD)),
        'cache_B_meta_k': nrm((DEPTH, DEC_BATCH, N_META, B_KVHEADS, B_HD)),
        'cache_B_meta_v': nrm((DEPTH, DEC_BATCH, N_META, B_KVHEADS, B_HD)),
        'state_C': nrm((DEPTH, DEC_BATCH, C_HEADS, C_DK, C_DV), 0.5),
        'meta_tokens': nrm((N_META, D_MODEL)),
        'g_pre_mix': gain((DEPTH, D_MODEL)),
        'w_in': nrm((DEPTH, D_MODEL, D_IN), D_MODEL ** -0.5),
        'g_kv': gain((DEPTH, A_LORA)),
        'w_uk': nrm((DEPTH, A_LORA, A_HEADS, A_NOPE), A_LORA ** -0.5),
        'w_uv': nrm((DEPTH, A_LORA, A_HEADS, A_V), A_LORA ** -0.5),
        'b_sinks': nrm((DEPTH, B_QHEADS), 0.5),
        'w_alpha': nrm((DEPTH, C_LOWRANK, C_HEADS * C_DK), C_LOWRANK ** -0.5),
        'b_alpha': nrm((DEPTH, C_HEADS * C_DK), 0.1),
        'g_gla': gain((DEPTH, C_DV)),
        'w_up_a': nrm((DEPTH, A_HEADS * A_V, D_MODEL), (A_HEADS * A_V) ** -0.5),
        'w_up_b': nrm((DEPTH, B_QHEADS * B_HD, D_MODEL), (B_QHEADS * B_HD) ** -0.5),
        'w_up_c': nrm((DEPTH, C_HEADS * C_DV, D_MODEL), (C_HEADS * C_DV) ** -0.5),
        'w_out': nrm((DEPTH, D_MODEL, D_MODEL), D_MODEL ** -0.5),
        'g_post_mix': gain((DEPTH, D_MODEL)),
        'g_pre_mlp': gain((DEPTH, D_MODEL)),
        'w_ff1': nrm((DEPTH, D_MODEL, D_FF), D_MODEL ** -0.5),
        'w_ff2': nrm((DEPTH, D_FF, D_MODEL), D_FF ** -0.5),
        'g_post_mlp': gain((DEPTH, D_MODEL)),
    }

def reference(x_prompt, x_sample, cache_A_ckv, cache_A_krope, cache_A_meta_ckv, cache_A_meta_krope,
              cache_B_k, cache_B_v, cache_B_meta_k, cache_B_meta_v, state_C,
              meta_tokens, g_pre_mix, w_in, g_kv, w_uk, w_uv, b_sinks, w_alpha, b_alpha, g_gla,
              w_up_a, w_up_b, w_up_c, w_out, g_post_mix, g_pre_mlp, w_ff1, w_ff2, g_post_mlp):
    b_sz, s_len, _ = x_prompt.shape
    xp = jnp.concatenate([jnp.broadcast_to(meta_tokens[None].astype(x_prompt.dtype),
                                           (b_sz, N_META, D_MODEL)), x_prompt], axis=1)
    pos_p = jnp.arange(s_len, dtype=jnp.int32)
    xs = x_sample
    past = cache_A_ckv.shape[2]
    pos_s = past + jnp.arange(x_sample.shape[1], dtype=jnp.int32)
    st_p = [[] for _ in range(9)]
    st_s = [[] for _ in range(5)]
    for l in range(DEPTH):
        p = {'g_pre_mix': g_pre_mix[l], 'w_in': w_in[l], 'g_kv': g_kv[l], 'w_uk': w_uk[l],
             'w_uv': w_uv[l], 'b_sinks': b_sinks[l], 'w_alpha': w_alpha[l], 'b_alpha': b_alpha[l],
             'g_gla': g_gla[l], 'w_up_a': w_up_a[l], 'w_up_b': w_up_b[l], 'w_up_c': w_up_c[l],
             'w_out': w_out[l], 'g_post_mix': g_post_mix[l], 'g_pre_mlp': g_pre_mlp[l],
             'w_ff1': w_ff1[l], 'w_ff2': w_ff2[l], 'g_post_mlp': g_post_mlp[l]}
        xp, new_p = _prompt_layer(xp, pos_p, p)
        xs, new_s = _sample_layer(xs, pos_s, p, cache_A_ckv[l], cache_A_krope[l], cache_A_meta_ckv[l],
                                  cache_A_meta_krope[l], cache_B_k[l], cache_B_v[l], cache_B_meta_k[l],
                                  cache_B_meta_v[l], state_C[l])
        for lst, a in zip(st_p, new_p):
            lst.append(a)
        for lst, a in zip(st_s, new_s):
            lst.append(a)
    y_prompt = xp[:, N_META:]
    return (y_prompt, xs,
            jnp.stack(st_p[0]), jnp.stack(st_p[1]), jnp.stack(st_p[2]), jnp.stack(st_p[3]),
            jnp.stack(st_p[4]), jnp.stack(st_p[5]), jnp.stack(st_p[6]), jnp.stack(st_p[7]),
            jnp.stack(st_p[8]),
            jnp.stack(st_s[0]), jnp.stack(st_s[1]), jnp.stack(st_s[2]), jnp.stack(st_s[3]),
            jnp.stack(st_s[4]))


_drawn_inputs = setup_inputs


def setup_inputs(seed=0):
    import zlib

    import numpy as np

    out = dict(_drawn_inputs(seed))
    spreads = {}
    factors = {'b_sinks': 8.0}
    for name, (base, spread) in spreads.items():
        noise = np.random.default_rng([zlib.crc32(name.encode()), seed]).standard_normal(out[name].shape)
        drawn = base * np.exp(spread * noise) if base else spread * noise
        out[name] = jnp.asarray(drawn.astype(out[name].dtype))
    for name, factor in factors.items():
        out[name] = (out[name] * factor).astype(out[name].dtype)
    return out
```

```python
import concourse.bass as bass
from concourse import mybir
from contextlib import ExitStack
import numpy as np

F32 = mybir.dt.float32
F32R = mybir.dt.float32r
ALU = mybir.AluOpType
ACT = mybir.ActivationFunctionType
AX = mybir.AxisListType

P = 128
D = 1024
KD = D // P
SEQ, META, DEC = 512, 16, 32
T = SEQ + META + DEC
HALF = T // 2
DEPTH = 2
CHUNK = 64
PAST = 256
LORA, KL = 256, 2
A_HEADS, A_NOPE, A_ROPE, A_V = 8, 64, 32, 64
B_HEADS, B_KV, B_HD = 8, 2, 64
B_G = B_HEADS // B_KV
WIN = 128
C_HEADS, C_DK, C_DV, C_LR = 4, 128, 256, 16
D_FF = 4 * D
BLK = 16
EPS = 1e-6
A_SCALE = float((A_NOPE + A_ROPE) ** -0.5)
B_SCALE = float(B_HD ** -0.5)
META0, SAMP0 = SEQ, SEQ + META
MIXED = META + DEC
CKEYS = PAST + META
NBLK = T // BLK
SBS = 128 // BLK
NEG = -1e30
WSLOTS = 3

SUPER = [(META0, META)] + [(128 * i, 128) for i in range(SEQ // 128)] + [(SAMP0, DEC)]


def plan_units():
    units = [("kralr", 0)]
    for h in range(C_HEADS):
        units += [("cq", h), ("ck", h), ("cv", 2 * h), ("cv", 2 * h + 1), ("cg", 2 * h), ("cg", 2 * h + 1)]
    units += [("ckv", n) for n in range(2)] + [("qn", n) for n in range(4)] + [("qr", n) for n in range(2)]
    for n in range(KD):
        units += [("gate_c", n), ("up_c", n)]
    units += [("kb", 0), ("vb", 0)] + [("qb", n) for n in range(4)]
    for b in "ab":
        for n in range(0, KD, 2):
            units += [("gate_" + b, n), ("gate_" + b, n + 1), ("up_" + b, n)]
    units += [("out", n) for n in range(KD)]
    ff1 = [[("ff1", 8 * g + n) for n in range(8)] for g in range(4)]
    ff2 = [[("ff2", 8 * g + n) for n in range(8)] for g in range(4)]
    units += ff1[0] + ff1[1] + ff2[0] + ff1[2] + ff2[1] + ff1[3] + ff2[2] + ff2[3]
    return units


UNITS = plan_units()
NU = len(UNITS)
UIDX = {u: n for n, u in enumerate(UNITS)}


def outs_of(kind):
    return (2, 4) if kind in ("up_a", "up_b") else (1, KD)


CONST = {}
_at = 0
for _name, _w in (("ident", 128), ("ones_d", 128), ("ones_v", 128), ("perm", 128), ("selrep", 144),
                  ("blockmask", 128), ("cos", T), ("sin", T), ("dist", 208), ("mask_s", 320),
                  ("dist_s", 192), ("rows", 128), ("neg", 64), ("ones", 128), ("zeros", 128), ("eps", 1)):
    CONST[_name] = (_at, _w)
    _at += _w
NCONST = _at
PARAM = {}
_at = 0
for _name, _w in (("g_pre_mix", 8), ("g_post_mix", 8), ("g_pre_mlp", 8), ("g_post_mlp", 8), ("g_kv", 2),
                  ("g_gla", 2), ("b_alpha", 4), ("sinks", 8)):
    PARAM[_name] = (_at, _w)
    _at += _w
NPARAM = _at


class Steps:

    def __init__(self, known):
        self.count = {e: 0 for e in ("pe", "act", "dve", "pool")}
        self.known = known
        self.seen = {}

    def done(self, engine, name=None):
        self.count[engine] += 1
        if name is not None:
            assert (engine, name) not in self.seen, name
            self.seen[engine, name] = self.count[engine]
        return 1

    def at(self, engine, name):
        if self.known is None:
            return 1
        return self.known[engine, name]


def build(nc, io, known):
    st = Steps(known)
    ctx = ExitStack()
    with ctx:
        def sem(name):
            return ctx.enter_context(nc.semaphore(name))

        base = 16512
        place = {"next": base}

        def at(name, shape, dt, offset):
            size = 4 * int(np.prod(shape[1:]))
            assert offset + size <= 229344, (name, offset + size)
            return nc.alloc_sbuf_tensor_at(name, shape, dt, offset=offset)

        def region(size):
            off = place["next"]
            place["next"] += (size + 31) // 32 * 32
            return off

        row = 4 * T
        r_w = [region(8192) for _ in range(WSLOTS)]
        r_h = region(16 * row)
        r_oc = region(16 * row)
        r_x = region(8 * row)
        r_sig = region(2 * row)
        r_r = region(row)
        r_const = region(4 * NCONST)
        r_par = region(4 * NPARAM)
        work = place["next"]

        wraw = [at(f"wraw{s}", [P, 1024], F32, r_w[s]) for s in range(WSLOTS)]
        wlo = [at(f"wlo{s}", [P, 1024], F32R, r_w[s]) for s in range(WSLOTS)]
        whi = [at(f"whi{s}", [P, 1024], F32R, r_w[s] + 4096) for s in range(WSLOTS)]

        def split_set(name, n, off):
            return (at(name + "_raw", [P, n, T], F32, off), at(name + "_lo", [P, n, T], F32R, off),
                    at(name + "_hi", [P, n, T], F32R, off + n * row))

        h_raw, h_lo, h_hi = split_set("h", KD, r_h)
        oc_raw, oc_lo, oc_hi = split_set("oc", KD, r_oc)
        hid0 = split_set("hid0", KD, r_oc)
        hid1 = split_set("hid1", KD, work)
        hid = [hid0, hid1]
        mix = at("mix", [P, KD, T], F32, r_oc)
        sq = at("sq", [P, KD, T], F32, r_oc + KD * row)
        facc = at("facc", [P, KD, T], F32, work + 16 * row)
        x = at("x", [P, KD, T], F32, r_x)
        y = at("y", [P, KD, T], F32, r_x)
        sig = at("sig", [P, 2, T], F32, r_sig)
        rstd = at("rstd", [P, T], F32, r_r)
        const = at("const", [P, NCONST], F32, r_const)
        par = at("par", [P, NPARAM], F32, r_par)

        def c_(name, rows=P):
            a, w = CONST[name]
            return const[0:rows, a:a + w]

        w_alpha = const[:, CONST["mask_s"][0]:CONST["mask_s"][0] + 512]

        def p_(name, n=0, w=1, rows=P, r0=0):
            a = PARAM[name][0] + n
            return par[r0:r0 + rows, a:a + w]

        wk = {"next": work}

        def wt(name, shape, dt=F32, off=None):
            size = 4 * int(np.prod(shape[1:]))
            if off is None:
                off = wk["next"]
                wk["next"] += (size + 31) // 32 * 32
            return at(name, shape, dt, off), off

        kra, _ = wt("kra", [P, T])
        keep = wk["next"]
        cproj = [wt(f"cproj{i}", [P, 6, T])[0] for i in range(2)]
        bcum, _ = wt("bcum", [P, T])
        ediag, ediag_off = wt("ediag", [P, NBLK * BLK * (BLK + 1) // 2])
        kfar, _ = wt("kfar", [P, 64 * 28])
        zlog = at("zlog", [P, T], F32, ediag_off)
        ztmp = at("ztmp", [P, T], F32, ediag_off + row)
        lsig = at("lsig", [P, T], F32, ediag_off + 2 * row)
        kfar_s, _ = wt("kfar_s", [P, BLK])
        qfar, _ = wt("qfar", [P, 4 * 112])
        qfar_s, _ = wt("qfar_s", [P, BLK])
        kend, _ = wt("kend", [P, T])
        ebl, _ = wt("ebl", [P, T])
        amat, _ = wt("amat", [P, T])
        ktok, _ = wt("ktok", [P, 6, 128])
        state, _ = wt("state", [P, 8, C_DV])
        assert wk["next"] <= 229344, wk["next"]
        gsq = at("gsq", [P, 2, T], F32, r_x)
        oh = at("oh", [P, 2, T], F32, r_x + 2 * row)
        vtok = at("vtok", [P, 6, 256], F32, r_x + 4 * row)
        qe = at("qe", [P, T], F32, r_x + 4 * row + 6144)
        gsig = sig
        cksq = at("cksq", [P, 2, T], F32, r_sig)
        wk["next"] = keep
        oa_raw, oa_lo, oa_hi = split_set("oa", 4, keep)
        qn = at("qn", [P, 4, T], F32, keep)
        wk["next"] = keep + 8 * row
        a_tmp = keep + 4 * row
        ckv = at("ckv", [P, KL, T], F32, a_tmp)
        cct = at("cct", [P, KL, CKEYS], F32, a_tmp + 2 * row)
        qr, _ = wt("qr", [P, 2, T])
        qrot, _ = wt("qrot", [P, 2, T])
        kn, _ = wt("kn", [P, 4, T])
        krot, _ = wt("krot", [P, T])
        va, _ = wt("va", [P, 4, 512])
        va_pm, _ = wt("va_pm", [META, 512])
        va_new, _ = wt("va_new", [DEC, 512])
        kn_c, _ = wt("kn_c", [P, 4, CKEYS])
        va_c, _ = wt("va_c", [P, 2, 512])
        va_cm, _ = wt("va_cm", [META, 512])
        kr_c, _ = wt("kr_c", [P, CKEYS])
        p_off = wk["next"]
        prob = [wt(f"prob{i}", [P, 1056])[0] for i in range(2)]
        wuk = at("wuk", [P, KL, 512], F32, p_off)
        wuv = at("wuv", [P, KL, 512], F32, p_off + 4096)
        ptf_off = wk["next"]
        ptf, _ = wt("ptf", [P, 2, 512])
        ptm, _ = wt("ptm", [META, 512])
        stat, _ = wt("stat", [P, 2, 24])
        a_end = wk["next"]
        assert a_end <= 229344, a_end
        wk["next"] = keep + 8 * row
        ob_raw, ob_lo, ob_hi = split_set("ob", 4, wk["next"])
        wk["next"] += 8 * row
        qb = at("qb", [P, 4, T], F32, wk["next"])
        wk["next"] += 4 * row
        kb, _ = wt("kb", [P, T])
        vb, _ = wt("vb", [P, T])
        v_own, _ = wt("v_own", [P, 4, 128])
        v_prev, _ = wt("v_prev", [64, 3, 128])
        v_pm, _ = wt("v_pm", [META, 128])
        v_new, _ = wt("v_new", [DEC, 128])
        kb_c, _ = wt("kb_c", [P, WIN + META])
        vb_c, _ = wt("vb_c", [P, 128])
        vb_cm, _ = wt("vb_cm", [META, 128])
        assert wk["next"] <= p_off, (wk["next"], p_off)

        dps = [ctx.enter_context(nc.psum_tensor(f"dense{i}", [P, 512], F32)) for i in range(2)]
        ps = ctx.enter_context(nc.psum_tensor("att", [P, 6, 512], F32))
        S0, S1, M_, T0, T1, O_ = range(6)
        PAIRS = [slice(0, 2), slice(3, 5)]

        pe_done, act_done, dve_done, pool_done = (sem(n) for n in ("pe_done", "act_done", "dve_done", "pool_done"))
        w_loaded = [sem(f"w_loaded{s}") for s in range(WSLOTS)]
        par_loaded = sem("par_loaded")
        spilled = sem("x_spilled")
        x_back = sem("x_back")
        a_loaded = sem("a_cache_loaded")
        b_loaded = sem("b_cache_loaded")
        state_loaded = sem("state_loaded")
        stored = sem("outputs_stored")
        block_sems = [pe_done, act_done, dve_done, pool_done, *w_loaded, par_loaded, spilled, x_back, a_loaded,
                      b_loaded, state_loaded, stored]
        first_loaded = sem("first_loaded")
        last_stored = sem("last_stored")

        rtmp = at("rtmp", [P, T], F32, ptf_off)
        eps = c_("eps")
        zero_l = c_("zeros")
        STATE_IN = [0, 1, 2, 3, 4, 6]
        STATE_OUT = [1, 2, 3, 4, 5, 7]
        VA_TILES = [
            [(ckv, 0, 128, va[:, 0, :]), (ckv, 128, 128, va[:, 1, :])],
            [(ckv, 256, 128, va[:, 2, :]), (ckv, 384, 128, va[:, 3, :])],
            [(cct, 0, 128, va_c[:, 0, :]), (cct, 128, 128, va_c[:, 1, :])],
            [(cct, PAST, META, va_cm[:, :]), (ckv, META0, META, va_pm[:, :])],
            [(ckv, SAMP0, DEC, va_new[:, :])],
        ]
        PREP_A_OVER = [("act", "prep a 14"), ("dve", "prep a 13"), ("dve", "krot"), ("dve", "qrot 1")]

        def ediag_of(j):
            a = NBLK * (BLK * j - j * (j - 1) // 2)
            return ediag[:, a:a + NBLK * (BLK - j)]

        def kfar_of(i):
            a = 32 * i * (i - 1)
            return kfar[:, a:a + 64 * i]

        def prep_evac(s):
            if s == 0:
                return "act"
            if s < 4:
                return "dve"
            return "act" if s % 2 == 0 else "dve"

        with nc.Block() as block:
            @block.sync
            def _(sp):
                sp.dma_start(const[:, :], io["const"]).then_inc(first_loaded, 16)
                sp.dma_start(x[:, :, :], io["x"].rearrange("(k p) t -> p k t", p=P)).then_inc(first_loaded, 16)
                sp.wait_ge(first_loaded, 32)

            @block.scalar
            def _(act):
                act.preload_act_table_set("natural_log_exp_and_others")

        def layer(l, block):
            H = (slice(0, HALF), slice(HALF, T))
            def A(e, n):
                return st.at(e, n)

            moving = {"h": (h_hi, h_lo), "oc": (oc_hi, oc_lo), "oa": (oa_hi, oa_lo), "ob": (ob_hi, ob_lo),
                      "y": (h_hi, h_lo), "h2": (h_hi, h_lo), "hid0": (hid0[2], hid0[1]), "hid1": (hid1[2], hid1[1])}

            def source(kind, n):
                if kind == "up_c":
                    return "oc"
                if kind == "up_a":
                    return "oa"
                if kind == "up_b":
                    return "ob"
                if kind == "out":
                    return "y"
                if kind == "ff1":
                    return "h2"
                if kind == "ff2":
                    return "hid%d" % (n // 8 % 2)
                return "h"

            def ready_names(kind, n, k):
                s = source(kind, n)
                if s.startswith("hid"):
                    g = n // 8
                    return ("act", f"hid hi {8 * g + k}"), ("pool", f"hid lo {8 * g + k}")
                return ("act", f"{s} hi {k}"), ("pool", f"{s} lo {k}")

            halves_done = []
            for u, (kind, n) in enumerate(UNITS):
                for o in range(outs_of(kind)[0]):
                    for hf in range(2):
                        halves_done.append((u, o, hf))
            bank_of = {key: i % 2 for i, key in enumerate(halves_done)}
            before = {key: halves_done[i - 2] for i, key in enumerate(halves_done) if i >= 2}

            def evac_engine(kind):
                return "act" if kind in ("ck", "cg", "gate_a", "gate_b", "gate_c", "out", "ff1", "vb") else "dve"

            order = []
            dn = iter(range(NU))

            def dense(k=1):
                for _ in range(k):
                    order.append(("dense", next(dn)))

            order.append(("norm", "pre_mix"))
            dense(1)
            dense(6)
            def gla_steps(*steps):
                for h, what in steps:
                    order.append(("gla", h, what))

            for h in range(C_HEADS):
                gla_steps((h, "p z"), (h, "v decay"))
                dense()
                if h > 0:
                    gla_steps((h - 1, "p ms"), (h - 1, "v out"))
                gla_steps((h, "v diag 0"), (h, "v diag 1"))
                dense()
                gla_steps((h, "p vtok"), (h, "p diag 0"), (h, "p diag 1"), (h, "v vtok"), (h, "v diag 2"), (h, "v diag 3"), (h, "v farq"))
                dense()
                gla_steps((h, "v far"), (h, "v kend"), (h, "p diag 2"), (h, "p diag 3"))
                dense()
                gla_steps((h, "p ktok"), (h, "p far"), (h, "v ktok"), (h, "v amat"))
                dense()
                gla_steps((h, "p kv"), (h, "v state"), (h, "v silu"))
                dense()
                gla_steps((h, "p o"), (h, "v o"))
            gla_steps((C_HEADS - 1, "p ms"), (C_HEADS - 1, "v out"))
            dense(2)
            for s in range(len(VA_TILES) + 10):
                order.append(("prep_a", s))
            jobs = [("a", t, i) for t in range(4) for i in range(5)]
            for j in range(len(jobs) + 2):
                order.append(("att", "a", j))
                if j < 16:
                    dense()
            dense(6)
            order.append(("prep_b", 0))
            order.append(("prep_b", 1))
            jobs_b = [("b", kv, i) for kv in range(2) for i in range(5)]
            for j in range(len(jobs_b) + 2):
                order.append(("att", "b", j))
                dense()
            while True:
                try:
                    u = next(dn)
                except StopIteration:
                    break
                if UNITS[u] == ("out", 0):
                    order.append(("split_y",))
                if UNITS[u] == ("ff1", 0):
                    order += [("norm", "post_mix"), ("norm", "pre_mlp")]
                order.append(("dense", u))
            order.append(("norm", "post_mlp"))
            JOBS = {"a": jobs, "b": jobs_b}

            norm_src = {"pre_mix": x, "post_mix": mix, "pre_mlp": x, "post_mlp": facc}

            def sig_free(b, n):
                if b == "c":
                    return (dve_done, A("dve", f"evac {UIDX['up_c', n - 2]} 0 1")) if n >= 2 else (pe_done, A("pe", "prep a 0"))
                if b == "a" and n < 2:
                    return dve_done, A("dve", f"evac {UIDX['up_c', n + 6]} 0 1")
                return pool_done, A("pool", f"y a {n + 6}" if n < 2 else f"y {b} {n - 2}")

            def key_count(br, i):
                if br == "a":
                    return 128 * (i + 1) + META if i < 4 else 320
                return (144 if i == 0 else 208) if i < 4 else 192

            def prob_view(br, j):
                _, t, i = JOBS[br][j]
                nk = key_count(br, i)
                if br == "a":
                    return prob[j % 2][:, 0:2 * nk].rearrange("p (a n) -> p a n", a=2)
                return prob[j % 2][:, 0:4 * (nk + 1)].rearrange("p (a n) -> p a n", a=4)

            @block.sync
            def _(sp):
                sp.dma_start(par[:, :], io["par"][bass.ds(l, 1), :, :].rearrange("a p n -> (a p) n")).then_inc(par_loaded, 16)
                sp.dma_start(w_alpha[96:112, :], io["w_alpha"][bass.ds(l, 1), :, :].rearrange("a p n -> (a p) n")).then_inc(par_loaded, 16)

                def load(slot, u):
                    sp.dma_start(wraw[slot][:, :], io["w"][bass.ds(l * NU + u, 1), :, :].rearrange("a p n -> (a p) n")
                                 ).then_inc(w_loaded[slot], 16)

                for u in range(WSLOTS):
                    load(u, u)
                for u in range(WSLOTS, NU):
                    sp.wait_ge(pe_done, A("pe", f"dense {u - WSLOTS}"))
                    load(u % WSLOTS, u)

            @block.tensor
            def _(pe):
                first_use = set()

                def dense_unit(u):
                    kind, n = UNITS[u]
                    nout, kt = outs_of(kind)
                    slot = u % WSLOTS
                    hi_w = whi[slot][:, :].rearrange("p (k m) -> p k m", k=kt)
                    lo_w = wlo[slot][:, :].rearrange("p (k m) -> p k m", k=kt)
                    src = source(kind, n)
                    hi_x, lo_x = moving[src]
                    key = (src, n // 8) if kind == "ff2" else src
                    fresh = key not in first_use
                    first_use.add(key)
                    pe.wait_ge(act_done, A("act", f"w hi {u}"))
                    pe.wait_ge(pool_done, A("pool", f"w lo {u}"))
                    m = 112 if kind == "kralr" else 128
                    for o in range(nout):
                        for hf in range(2):
                            bank = dps[bank_of[u, o, hf]]
                            if (u, o, hf) in before:
                                pu, po, ph = before[u, o, hf]
                                pe.wait_ge(act_done if evac_engine(UNITS[pu][0]) == "act" else dve_done,
                                           A(evac_engine(UNITS[pu][0]), f"evac {pu} {po} {ph}"))
                            for k in range(kt):
                                if fresh and o == 0 and hf == 0:
                                    for e, name in ready_names(kind, n, k):
                                        pe.wait_ge({"act": act_done, "pool": pool_done}[e], A(e, name))
                                for i, (a, b) in enumerate(((hi_w, hi_x), (lo_w, hi_x), (hi_w, lo_x))):
                                    mm = pe.matmul(bank[0:m, 0:HALF], a[:, k, o * 128:o * 128 + m], b[:, k, H[hf]],
                                                   start=(k == 0 and i == 0), stop=(k == kt - 1 and i == 2))
                            last = o == nout - 1 and hf == 1
                            mm.then_inc(pe_done, st.done("pe", f"half {u} {o} {hf}"))
                    st.seen["pe", f"dense {u}"] = st.count["pe"]

                def norm(which):
                    for k in range(KD):
                        e = "act" if k % 2 == 0 else "dve"
                        pe.wait_ge(act_done if e == "act" else dve_done, A(e, f"sq {which} {k}"))
                        for hf in range(2):
                            mm = pe.matmul(ps[:, PAIRS[0].start + hf, 0:HALF], c_("ones_d"), sq[:, k, H[hf]],
                                           start=(k == 0), stop=(k == KD - 1))
                    mm.then_inc(pe_done, st.done("pe", f"ms {which}"))

                def gla(h, s):
                    pr = cproj[h % 2]
                    q, kk = pr[:, 0, :], pr[:, 1, :]
                    if s == "p z":
                        if h == 0:
                            pe.wait_ge(dve_done, A("dve", f"evac {UIDX['kralr', 0]} 0 1"))
                            pe.wait_ge(par_loaded, 32)
                        else:
                            pe.wait_ge(dve_done, A("dve", f"gla state {h - 1}"))
                        for hf in range(2):
                            mm = pe.matmul(ps[:, S0 + hf, 0:HALF], w_alpha[96:112, 128 * h:128 * h + 128],
                                           kra[96:112, H[hf]], start=True, stop=True)
                        mm.then_inc(pe_done, st.done("pe", f"gla z {h}"))
                    if s.startswith("p diag"):
                        if s == "p diag 0":
                            pe.wait_ge(act_done, A("act", f"gla z {h}"))
                            if h > 0:
                                pe.wait_ge(act_done, A("act", f"gla rstd {h - 1}"))
                        for j in range(4 * int(s[-1]), 4 * int(s[-1]) + 4):
                            w = BLK - j
                            pe.wait_ge(dve_done, A("dve", f"gla e {h} {j}"))
                            a0 = CONST["selrep"][0] + 15 - j
                            e = ediag_of(j).rearrange("p (b t) -> p b t", t=w)
                            out0 = ps[:, S0, :].rearrange("p (b t) -> p b t", t=BLK)
                            out1 = ps[:, S1, 0:48].rearrange("p (b t) -> p b t", t=BLK)
                            pe.matmul(out0[:, :, j:], const[:, a0:a0 + 128], e[:, 0:32, :],
                                      start=(j == 0), stop=(j == 15))
                            mm = pe.matmul(out1[:, :, j:], const[:, a0:a0 + 128], e[:, 32:35, :],
                                           start=(j == 0), stop=(j == 15))
                            mm.then_inc(pe_done, st.done("pe", f"gla diag {h} {j}"))
                    if s == "p vtok":
                        for sb in range(6):
                            a, n = SUPER[sb]
                            bank = (M_, O_)[sb % 2]
                            if sb == 0:
                                pe.wait_ge(dve_done, A("dve", f"evac {UIDX['cv', 2 * h + 1]} 0 1"))
                                if h > 0:
                                    pe.wait_ge(act_done, A("act", f"gla oevac {h - 1}"))
                            if sb >= 2:
                                pe.wait_ge(act_done, A("act", f"gla vtok {h} {sb - 2}"))
                            for i in range(2):
                                mm = pe.transpose(ps[0:n, bank, 128 * i:128 * i + 128], pr[:, 2 + i, a:a + n],
                                                  c_("ident"))
                            mm.then_inc(pe_done, st.done("pe", f"gla vtok {h} {sb}"))
                    if s == "p far":
                        for bank, n in ((T0, 512), (T1, 32)):
                            pe.matmul(ps[:, bank, 0:n], zero_l, c_("cos")[:, 0:n], start=True, stop=False,
                                      skip_group_check=True)
                        pe.wait_ge(dve_done, A("dve", f"gla far s {h}"))
                        pe.matmul(ps[0:16, T1, 16:32], kfar_s[:, :], qfar_s[:, :], start=False, stop=True,
                                  skip_group_check=True)
                        for i in range(1, 8):
                            pe.wait_ge(dve_done, A("dve", f"gla far {h} {i}"))
                            kf = kfar_of(i).rearrange("p (b s) -> p b s", b=4)
                            qf = qfar[:, :].rearrange("p (b i t) -> p b i t", b=4, t=BLK)
                            for sb in range(4):
                                mm = pe.matmul(ps[0:16 * i, T0, 128 * sb + 16 * i:128 * sb + 16 * i + 16],
                                               kf[:, sb, :], qf[:, sb, i - 1, :], start=False, stop=True,
                                               skip_group_check=True)
                            mm.then_inc(pe_done, st.done("pe", f"gla far {h} {i}"))
                    if s == "p ktok":
                        pe.wait_ge(dve_done, A("dve", f"gla kend {h}"))
                        pe.wait_ge(act_done, A("act", f"gla vtok {h} 5"))
                        for g, bank in ((0, M_), (1, O_)):
                            for i in range(3):
                                a, n = SUPER[3 * g + i]
                                mm = pe.transpose(ps[0:n, bank, 128 * i:128 * i + 128], kend[:, a:a + n], c_("ident"))
                            mm.then_inc(pe_done, st.done("pe", f"gla ktok {h} {g}"))
                    if s == "p kv":
                        pe.wait_ge(dve_done, A("dve", f"gla amat {h}"))
                        pe.wait_ge(act_done, A("act", f"gla ktok {h} 1"))
                        for sb in range(6):
                            a, n = SUPER[sb]
                            bank = (S0, S1, T0)[sb // 2]
                            mm = pe.matmul(ps[:, bank, 256 * (sb % 2):256 * (sb % 2) + 256], ktok[0:n, sb, :],
                                           vtok[0:n, sb, :], start=(sb % 2 == 0), stop=True, skip_group_check=True)
                        mm.then_inc(pe_done, st.done("pe", f"gla kv {h}"))
                    if s == "p o":
                        pe.wait_ge(dve_done, A("dve", f"gla state {h}"))
                        for vt in range(2):
                            for sb in range(6):
                                a, n = SUPER[sb]
                                if n == 128:
                                    dst = ps[:, (M_, O_)[vt], a:a + n]
                                else:
                                    dst = ps[:, T1, 48 * vt + a - SEQ:48 * vt + a - SEQ + n]
                                first = (sb == 1) or (vt == 0 and sb == 0)
                                pe.matmul(dst, vtok[0:n, sb, 128 * vt:128 * vt + 128], amat[0:n, a:a + n],
                                          start=first, stop=False, skip_group_check=True)
                                mm = pe.matmul(dst, state[:, STATE_IN[sb], 128 * vt:128 * vt + 128],
                                               qe[:, a:a + n], start=False, stop=True, skip_group_check=True)
                        mm.then_inc(pe_done, st.done("pe", f"gla o {h}"))
                    if s == "p ms":
                        pe.wait_ge(act_done, A("act", f"gla sq {h}"))
                        if h + 1 < C_HEADS:
                            pe.wait_ge(act_done, A("act", f"gla z {h + 1}"))
                        for i in range(2):
                            for hf in range(2):
                                mm = pe.matmul(ps[:, S0 + hf, 0:HALF], c_("ones_v"), gsq[:, i, H[hf]],
                                               start=(i == 0), stop=(i == 1))
                        mm.then_inc(pe_done, st.done("pe", f"gla ms {h}"))

                def prep_a(s):
                    pair = PAIRS[s % 2].start
                    if s >= 2:
                        e = prep_evac(s - 2)
                        pe.wait_ge(act_done if e == "act" else dve_done, A(e, f"prep a {s - 2}"))
                    elif s == 0:
                        pe.wait_ge(act_done, A("act", f"gla rstd {C_HEADS - 1}"))
                        pe.wait_ge(dve_done, A("dve", f"gla state {C_HEADS - 1}"))
                    if s == 0:
                        pe.wait_ge(act_done, A("act", "ckv sq"))
                        for k in range(KL):
                            for hf in range(2):
                                mm = pe.matmul(ps[:, pair + hf, 0:HALF], c_("ones_v"), cksq[:, k, H[hf]],
                                               start=(k == 0), stop=(k == KL - 1))
                    elif s == 1:
                        for hf in range(2):
                            mm = pe.matmul(ps[0:96, pair + hf, 0:HALF], const[0:96, CONST["perm"][0]:CONST["perm"][0] + 96],
                                           kra[0:96, H[hf]], start=True, stop=True)
                    elif s in (2, 3):
                        u = UIDX["qr", s - 2]
                        pe.wait_ge(dve_done, A("dve", f"evac {u} 0 1"))
                        for hf in range(2):
                            mm = pe.matmul(ps[:, pair + hf, 0:HALF], c_("perm"), qr[:, s - 2, H[hf]],
                                           start=True, stop=True)
                    elif s in (4, 5, 6, 7):
                        if s == 4:
                            pe.wait_ge(dve_done, A("dve", "c 1"))
                            pe.wait_ge(a_loaded, 64)
                        for hf in range(2):
                            for k in range(KL):
                                mm = pe.matmul(ps[:, pair + hf, 0:HALF], wuk[:, k, 128 * (s - 4):128 * (s - 4) + 128],
                                               ckv[:, k, H[hf]], start=(k == 0), stop=(k == KL - 1))
                    elif s in (8, 9):
                        for i in range(2):
                            n = 2 * (s - 8) + i
                            for k in range(KL):
                                mm = pe.matmul(ps[:, pair + i, 0:CKEYS], wuk[:, k, 128 * n:128 * n + 128],
                                               cct[:, k, :], start=(k == 0), stop=(k == KL - 1))
                    else:
                        for i, (src, a, n, _) in enumerate(VA_TILES[s - 10]):
                            for k in range(KL):
                                mm = pe.matmul(ps[0:n, pair + i, 0:512], src[:, k, a:a + n], wuv[:, k, :],
                                               start=(k == 0), stop=(k == KL - 1))
                    mm.then_inc(pe_done, st.done("pe", f"prep a {s}"))

                def scores(br, j):
                    _, t, i = JOBS[br][j]
                    if br == "a":
                        if j >= 1:
                            pe.wait_ge(dve_done, A("dve", f"a shift {j - 1}"))
                        if j == 0:
                            for e, name in PREP_A_OVER:
                                pe.wait_ge({"act": act_done, "dve": dve_done, "pool": pool_done}[e], A(e, name))
                        for a in range(2):
                            h = 2 * t + a
                            r64, r32 = slice(64 * a, 64 * a + 64), slice(32 * (h % 4), 32 * (h % 4) + 32)
                            if i < 4:
                                qc, nk = slice(128 * i, 128 * i + 128), 128 * (i + 1)
                                pe.matmul(ps[:, S0 + a, 0:nk], qn[r64, t, qc], kn[r64, t, 0:nk], start=True, stop=False,
                                          skip_group_check=True)
                                pe.matmul(ps[:, S0 + a, 0:nk], qrot[r32, h // 4, qc], krot[r32, 0:nk], start=False, stop=True,
                                          skip_group_check=True)
                                r1 = slice(r32.start, r32.start + 1)
                                pe.matmul(ps[:, S0 + a, nk - 64:nk], c_("rows")[r1], c_("neg")[r1], start=False, stop=True,
                                          skip_group_check=True)
                                mdst = ps[:, S0 + a, nk:nk + META] if i < 3 else ps[:, M_, 16 * a:16 * a + 16]
                                pe.matmul(mdst, qn[r64, t, qc], kn[r64, t, META0:META0 + META],
                                          start=(i == 3 and a == 0), stop=False, skip_group_check=True)
                                mm = pe.matmul(mdst, qr[r32, h // 4, qc],
                                               krot[r32, META0:META0 + META], start=False, stop=True, skip_group_check=True)
                                if i == 3 and a == 0:
                                    mm.then_inc(pe_done, st.done("pe"))
                                    pe.wait_ge(pe_done, st.count["pe"])
                            else:
                                qc = slice(META0, T)
                                first = True
                                for c0, n, kk_, kr_, rope in ((0, PAST, kn_c[r64, t, 0:PAST], kr_c[r32, 0:PAST], qrot),
                                                              (256, DEC, kn[r64, t, SAMP0:T], krot[r32, SAMP0:T], qrot),
                                                              (288, META, kn_c[r64, t, PAST:CKEYS], kr_c[r32, PAST:CKEYS], qr),
                                                              (304, META, kn[r64, t, META0:SAMP0], krot[r32, META0:SAMP0], qr)):
                                    dst = ps[0:MIXED, S0 + a, c0:c0 + n]
                                    pe.matmul(dst, qn[r64, t, qc], kk_, start=first, stop=False, skip_group_check=True)
                                    mm = pe.matmul(dst, rope[r32, h // 4, qc], kr_, start=False, stop=True,
                                                   skip_group_check=True)
                                    first = False
                    else:
                        if j >= 1:
                            pe.wait_ge(dve_done, A("dve", f"b bias {j - 1}"))
                        else:
                            pe.wait_ge(act_done, A("act", "b vtok"))
                            pe.wait_ge(dve_done, A("dve", "b vtok"))
                            pe.wait_ge(dve_done, A("dve", f"evac {UIDX['qb', 3]} 0 1"))
                            pe.wait_ge(b_loaded, 48)
                        r64 = slice(64 * t, 64 * t + 64)
                        for g in range(B_G):
                            if i < 4:
                                c0 = 208 * (g % 2)
                                qc = slice(128 * i, 128 * i + 128)
                                parts = [(64, META, kb[r64, META0:SAMP0]), (80, 128, kb[r64, qc])]
                                if i > 0:
                                    parts.append((0, 64, kb[r64, 128 * i - 64:128 * i]))
                                rows = P
                            else:
                                c0 = 192 * (g % 2)
                                qc = slice(META0, T)
                                parts = [(0, WIN, kb_c[r64, 0:WIN]), (128, DEC, kb[r64, SAMP0:T]),
                                         (160, META, kb_c[r64, WIN:WIN + META]), (176, META, kb[r64, META0:SAMP0])]
                                rows = MIXED
                            for n_, (o, w, key) in enumerate(parts):
                                mm = pe.matmul(ps[0:rows, S0 + g // 2, c0 + o:c0 + o + w], qb[r64, g, qc], key,
                                               start=(g % 2 == 0 and n_ == 0), stop=True, skip_group_check=True)
                    mm.then_inc(pe_done, st.done("pe", f"{br} scores {j}"))

                def turn(br, j):
                    _, t, i = JOBS[br][j]
                    pe.wait_ge(pool_done, A("pool", f"{br} prob {j}"))
                    if j >= 1:
                        pe.wait_ge(dve_done, A("dve", f"{br} turned {j - 1}"))
                    if j >= 2:
                        pe.wait_ge(dve_done, A("dve", f"{br} o {j - 2}"))
                    nk = key_count(br, i)
                    pb = prob_view(br, j)
                    if br == "a":
                        for a in range(2):
                            if i < 4:
                                for kt in range(i + 1):
                                    pe.transpose(ps[:, T0 + a, 128 * kt:128 * kt + 128], pb[:, a, 128 * kt:128 * kt + 128],
                                                 c_("ident"))
                                mm = pe.transpose(ps[0:META, O_, 256 + 128 * a:384 + 128 * a],
                                                  pb[:, a, nk - META:nk], c_("ident"))
                            else:
                                idn = const[0:MIXED, 0:MIXED]
                                for n_, (c0, w) in enumerate(((0, 128), (128, 128), (256, DEC), (288, META), (304, META))):
                                    mm = pe.transpose(ps[0:w, T0 + a, 48 * n_:48 * n_ + 48], pb[0:MIXED, a, c0:c0 + w], idn)
                    else:
                        for g in range(B_G):
                            if i < 4:
                                o = 0 if i > 0 else -64
                                c = slice(128 * g, 128 * g + 128)
                                if i > 0:
                                    pe.transpose(ps[0:64, T1, c], pb[:, g, 0:64], c_("ident"))
                                pe.transpose(ps[:, T0, c], pb[:, g, 80 + o:208 + o], c_("ident"))
                                mm = pe.transpose(ps[0:META, M_, c], pb[:, g, 64 + o:80 + o], c_("ident"))
                            else:
                                idn = const[0:MIXED, 0:MIXED]
                                c = slice(48 * g, 48 * g + 48)
                                pe.transpose(ps[:, T0, c], pb[0:MIXED, g, 0:WIN], idn)
                                pe.transpose(ps[0:DEC, T1, c], pb[0:MIXED, g, WIN:WIN + DEC], idn)
                                pe.transpose(ps[0:META, M_, c], pb[0:MIXED, g, 160:176], idn)
                                mm = pe.transpose(ps[0:META, M_, 192 + 48 * g:240 + 48 * g], pb[0:MIXED, g, 176:192], idn)
                    mm.then_inc(pe_done, st.done("pe", f"{br} turn {j}"))

                def values(br, j):
                    _, t, i = JOBS[br][j]
                    pe.wait_ge(dve_done, A("dve", f"{br} turned {j}"))
                    if j >= 1:
                        pe.wait_ge(dve_done, A("dve", f"{br} o {j - 1}"))
                    if br == "a":
                        for a in range(2):
                            hc = slice(64 * (2 * t + a), 64 * (2 * t + a) + 64)
                            if i < 4:
                                dst = ps[64 * a:64 * a + 64, O_, 0:128]
                                for kt in range(i + 1):
                                    pe.matmul(dst, va[:, kt, hc], ptf[:, a, 128 * kt:128 * kt + 128],
                                              start=(kt == 0), stop=False)
                                mm = pe.matmul(dst, va_pm[:, hc], ptm[:, 128 * a:128 * a + 128], start=False, stop=True)
                            else:
                                dst = ps[64 * a:64 * a + 64, O_, 0:MIXED]
                                pe.matmul(dst, va_c[:, 0, hc], ptf[:, a, 0:48], start=True, stop=False)
                                pe.matmul(dst, va_c[:, 1, hc], ptf[:, a, 48:96], start=False, stop=False)
                                pe.matmul(dst, va_new[:, hc], ptf[0:DEC, a, 96:144], start=False, stop=False)
                                pe.matmul(dst, va_cm[:, hc], ptf[0:META, a, 144:192], start=False, stop=False)
                                mm = pe.matmul(dst, va_pm[:, hc], ptf[0:META, a, 192:240], start=False, stop=True)
                    else:
                        hc = slice(64 * t, 64 * t + 64)
                        if i < 4:
                            dst = ps[64 * t:64 * t + 64, O_, 0:512]
                            pe.matmul(dst, v_own[:, i, hc], ptf[:, 0, :], start=True, stop=False)
                            if i > 0:
                                pe.matmul(dst, v_prev[:, i - 1, hc], ptf[0:64, 1, :], start=False, stop=False)
                            mm = pe.matmul(dst, v_pm[:, hc], ptm[:, :], start=False, stop=True)
                        else:
                            dst = ps[64 * t:64 * t + 64, O_, 0:192]
                            pe.matmul(dst, vb_c[:, hc], ptf[:, 0, 0:192], start=True, stop=False)
                            pe.matmul(dst, v_new[:, hc], ptf[0:DEC, 1, 0:192], start=False, stop=False)
                            pe.matmul(dst, vb_cm[:, hc], ptm[:, 0:192], start=False, stop=False)
                            mm = pe.matmul(dst, v_pm[:, hc], ptm[:, 192:384], start=False, stop=True)
                    mm.then_inc(pe_done, st.done("pe", f"{br} values {j}"))

                def prep_b(s):
                    if s == 0:
                        pe.wait_ge(act_done, A("act", f"evac {UIDX['vb', 0]} 0 1"))
                        pe.wait_ge(dve_done, A("dve", f"a o {len(jobs) - 1}"))
                        for i in range(4):
                            pe.transpose(ps[:, T0, 128 * i:128 * i + 128], vb[:, 128 * i:128 * i + 128], c_("ident"))
                        for i in range(1, 4):
                            pe.transpose(ps[0:64, T1, 128 * i - 128:128 * i], vb[:, 128 * i - 64:128 * i], c_("ident"))
                        pe.transpose(ps[0:META, M_, 0:128], vb[:, META0:SAMP0], c_("ident"))
                        mm = pe.transpose(ps[0:DEC, M_, 128:256], vb[:, SAMP0:T], c_("ident"))
                        mm.then_inc(pe_done, st.done("pe", "b vtok"))

                for step in order:
                    if step[0] == "dense":
                        dense_unit(step[1])
                    elif step[0] == "norm":
                        norm(step[1])
                    elif step[0] == "gla":
                        gla(step[1], step[2])
                    elif step[0] == "prep_a":
                        prep_a(step[1])
                    elif step[0] == "prep_b":
                        prep_b(step[1])
                    elif step[0] == "att":
                        br, j = step[1], step[2]
                        n = len(JOBS[br])
                        if 1 <= j <= n:
                            turn(br, j - 1)
                        if j >= 2:
                            values(br, j - 2)
                        if j < n:
                            scores(br, j)

            @block.scalar
            def _(act):
                def store(dst, src, e, name):
                    act.wait_ge({"act": act_done, "dve": dve_done}[e], A(e, name))
                    act.dma_start(dst, src).then_inc(stored, 16)
                    count["stored"] += 16

                count = {"stored": 0}

                def w_hi(u):
                    slot = u % WSLOTS
                    act.wait_ge(w_loaded[slot], 16 * (u // WSLOTS + 1))
                    act.activation(whi[slot][:, :], wraw[slot][:, :], ACT.Copy).then_inc(act_done, st.done("act", f"w hi {u}"))

                def round_tile(dst, src, wait, name):
                    act.wait_ge(*wait)
                    act.activation(dst, src, ACT.Copy).then_inc(act_done, st.done("act", name))

                def link(ins, name=None):
                    ins.then_inc(act_done, st.done("act", name))
                    act.wait_ge(act_done, st.count["act"])

                def evac(u):
                    kind, n = UNITS[u]
                    if evac_engine(kind) != "act":
                        return
                    for hf in range(2):
                        src = dps[bank_of[u, 0, hf]][:, 0:HALF]
                        act.wait_ge(pe_done, A("pe", f"half {u} 0 {hf}"))
                        if kind == "ck":
                            if hf == 0 and n >= 2:
                                act.wait_ge(dve_done, A("dve", f"gla kend {n - 2}"))
                            ins = act.activation(cproj[n % 2][:, 1, H[hf]], src, ACT.Copy)
                        elif kind == "cg":
                            h, i = n // 2, n % 2
                            if hf == 0 and h >= 2:
                                act.wait_ge(dve_done, A("dve", f"gla silu {h - 2}"))
                            ins = act.activation(cproj[h % 2][:, 4 + i, H[hf]], src, ACT.Copy)
                        elif kind == "vb":
                            if hf == 0:
                                act.wait_ge(dve_done, A("dve", f"a o {len(jobs) - 1}"))
                                act.wait_ge(pe_done, A("pe", f"a values {len(jobs) - 1}"))
                            ins = act.activation(vb[:, H[hf]], src, ACT.Copy)
                        elif kind == "out":
                            if hf == 0 and n == 0:
                                act.wait_ge(pe_done, A("pe", f"dense {UIDX['up_c', KD - 1]}"))
                            ins = act.activation(mix[:, n, H[hf]], src, ACT.Copy)
                        elif kind == "ff1":
                            g = n // 8
                            if hf == 0:
                                if g >= 2 and n % 8 == 0:
                                    act.wait_ge(pe_done, A("pe", f"dense {UIDX['ff2', 8 * (g - 2) + 7]}"))
                                if g == 0 and n == 0:
                                    act.wait_ge(dve_done, A("dve", "h raw pre_mlp 7"))
                                    act.wait_ge(pe_done, A("pe", "ms pre_mlp"))
                                if g == 1 and n == 8:
                                    act.wait_ge(pe_done, A("pe", f"dense {UIDX['up_b', 6]}"))
                            ins = act.activation(hid[g % 2][0][:, n % 8, H[hf]], src, ACT.Relu)
                        else:
                            if hf == 0:
                                b = kind[-1]
                                act.wait_ge(*sig_free(b, n))
                            ins = act.activation(sig[:, n % 2, H[hf]], src, ACT.Exp, scale=-1.0)
                        ins.then_inc(act_done, st.done("act", f"evac {u} 0 {hf}"))

                def after_evac(u):
                    kind, n = UNITS[u]
                    if kind == "ff1":
                        g = n // 8
                        round_tile(hid[g % 2][2][:, n % 8, :], hid[g % 2][0][:, n % 8, :],
                                   (dve_done, A("dve", f"hid {n}")), f"hid hi {n}")

                def norm(which):
                    src = norm_src[which]
                    for k in range(0, KD, 2):
                        if which == "pre_mix":
                            if k == 0:
                                act.wait_ge(par_loaded, 32)
                        elif which == "post_mix":
                            act.wait_ge(act_done, A("act", f"evac {UIDX['out', k]} 0 1"))
                        elif which == "pre_mlp":
                            act.wait_ge(dve_done, A("dve", f"x post_mix {k}"))
                        else:
                            act.wait_ge(dve_done, A("dve", f"evac {UIDX['ff2', 24 + k]} 0 1"))
                            if k == 0:
                                act.wait_ge(pe_done, A("pe", f"dense {UIDX['ff2', 23]}"))
                        act.activation(sq[:, k, :], src[:, k, :], ACT.Square).then_inc(act_done, st.done("act", f"sq {which} {k}"))
                    act.wait_ge(pe_done, A("pe", f"ms {which}"))
                    if which == "pre_mlp":
                        act.wait_ge(dve_done, A("dve", "x post_mix 7"))
                    link(act.activation(rstd[:, :].rearrange("p (a n) -> p a n", a=2), ps[:, 0:2, 0:HALF], ACT.Ln,
                                        bias=eps[:, 0:1]))
                    act.activation(rstd[:, :], rstd[:, :], ACT.Exp, scale=-0.5).then_inc(act_done, st.done("act", f"rstd {which}"))
                    if which in ("pre_mix", "pre_mlp"):
                        name = "h" if which == "pre_mix" else "h2"
                        for k in range(KD):
                            round_tile(h_hi[:, k, :], h_raw[:, k, :], (dve_done, A("dve", f"h raw {which} {k}")), f"{name} hi {k}")
                    if which == "pre_mix":
                        act.wait_ge(dve_done, A("dve", "h raw pre_mix 7"))
                        act.dma_start(io["x_spill"], x[:, :, :]).then_inc(spilled, 16)

                def gla(h, s):
                    pr = cproj[h % 2]
                    if s == "v decay":
                        if h > 0:
                            act.wait_ge(dve_done, A("dve", f"gla state {h - 1}"))
                            act.wait_ge(pe_done, A("pe", f"gla o {h - 1}"))
                            act.wait_ge(pe_done, A("pe", f"gla diag {h - 1} 15"))
                        act.dma_start(state[:, 6, :], io["state"][bass.ds(l * C_HEADS + h, 1), :, :].rearrange("a p n -> (a p) n")).then_inc(state_loaded, 16)
                        act.wait_ge(pe_done, A("pe", f"gla z {h}"))
                        zz = zlog[:, :]
                        link(act.activation(zz.rearrange("p (a n) -> p a n", a=2), ps[:, S0:S1 + 1, 0:HALF], ACT.Identity,
                                            bias=p_("b_alpha", h)), f"gla z {h}")
                        link(act.activation(ztmp[:, :], zz, ACT.Abs))
                        link(act.activation(ztmp[:, :], ztmp[:, :], ACT.Exp, scale=-1.0))
                        act.activation(ztmp[:, :], ztmp[:, :], ACT.Ln, bias=1.0).then_inc(act_done, st.done("act", f"gla ln {h}"))
                    if s.startswith("v diag"):
                        for j in range(4 * int(s[-1]), 4 * int(s[-1]) + 4):
                            e = ediag_of(j)
                            act.wait_ge(pool_done, A("pool", f"gla d {h} {j}"))
                            act.activation(e, e, ACT.Exp, scale=1.0 / 16).then_inc(act_done, st.done("act", f"gla e {h} {j}"))
                    if s == "v vtok":
                        act.wait_ge(spilled, 16)
                        if h > 0:
                            act.wait_ge(pe_done, A("pe", f"gla o {h - 1}"))
                        for sb in range(6):
                            n = SUPER[sb][1]
                            bank = (M_, O_)[sb % 2]
                            act.wait_ge(pe_done, A("pe", f"gla vtok {h} {sb}"))
                            act.activation(vtok[0:n, sb, :], ps[0:n, bank, 0:256], ACT.Copy).then_inc(act_done, st.done("act", f"gla vtok {h} {sb}"))
                    if s == "v farq":
                        act.wait_ge(pool_done, A("pool", f"gla far q {h}"))
                        act.activation(qfar[:, :], qfar[:, :], ACT.Exp, scale=1.0 / 16).then_inc(act_done, st.done("act"))
                        act.activation(qfar_s[:, :], qfar_s[:, :], ACT.Exp, scale=1.0 / 16).then_inc(act_done, st.done("act"))
                        act.activation(kfar_s[:, :], kfar_s[:, :], ACT.Exp, scale=1.0 / 16).then_inc(act_done, st.done("act", f"gla far q {h}"))
                    if s == "v far":
                        for i in range(1, 8):
                            act.wait_ge(pool_done, A("pool", f"gla far {h} {i}"))
                            kf = kfar_of(i)
                            act.activation(kf, kf, ACT.Exp, scale=1.0 / 16).then_inc(act_done, st.done("act", f"gla far {h} {i}"))
                    if s == "v kend":
                        act.wait_ge(dve_done, A("dve", f"gla scan {h}"))
                        if h > 0:
                            act.wait_ge(dve_done, A("dve", f"gla state {h - 1}"))
                        act.activation(ebl[:, :], bcum[:, :], ACT.Exp, scale=1.0 / 16).then_inc(act_done, st.done("act", f"gla eb {h}"))
                        act.wait_ge(pool_done, A("pool", f"gla kend {h}"))
                        act.activation(kend[:, :], kend[:, :], ACT.Exp, scale=1.0 / 16).then_inc(act_done, st.done("act", f"gla kend {h}"))
                    if s == "v ktok":
                        for g in range(2):
                            bank = (M_, O_)[g]
                            act.wait_ge(pe_done, A("pe", f"gla ktok {h} {g}"))
                            for i in range(3):
                                n = SUPER[3 * g + i][1]
                                ins = act.activation(ktok[0:n, 3 * g + i, :], ps[0:n, bank, 128 * i:128 * i + 128], ACT.Copy)
                                ins.then_inc(act_done, st.done("act", f"gla ktok {h} {g}" if i == 2 else None))
                    if s == "v silu":
                        act.wait_ge(act_done, A("act", f"evac {UIDX['cg', 2 * h + 1]} 0 1"))
                        if h >= 1:
                            act.wait_ge(dve_done, A("dve", f"gla out {h - 1} 1"))
                        act.activation(gsig[:, :, :], pr[:, 4:6, :], ACT.Exp, scale=-1.0).then_inc(act_done, st.done("act", f"gla gate {h}"))
                    if s == "v o":
                        act.wait_ge(pe_done, A("pe", f"gla o {h}"))
                        act.wait_ge(spilled, 16)
                        if h > 0:
                            act.wait_ge(dve_done, A("dve", f"gla out {h - 1} 1"))
                        act.activation(oh[:, :, 0:SEQ], ps[:, M_::3, :], ACT.Copy).then_inc(act_done, st.done("act"))
                        act.activation(oh[:, :, SEQ:T], ps[:, T1, 0:96].rearrange("p (a n) -> p a n", a=2), ACT.Copy
                                       ).then_inc(act_done, st.done("act", f"gla oevac {h}"))
                        act.wait_ge(act_done, st.count["act"])
                        if h > 0:
                            act.wait_ge(pe_done, A("pe", f"gla ms {h - 1}"))
                        act.activation(gsq[:, :, :], oh[:, :, :], ACT.Square).then_inc(act_done, st.done("act", f"gla sq {h}"))
                    if s == "v out":
                        act.wait_ge(pe_done, A("pe", f"gla ms {h}"))
                        link(act.activation(rstd[:, :].rearrange("p (a n) -> p a n", a=2), ps[:, S0:S1 + 1, 0:HALF], ACT.Ln,
                                            bias=eps[:, 0:1]))
                        act.activation(rstd[:, :], rstd[:, :], ACT.Exp, scale=-0.5).then_inc(act_done, st.done("act", f"gla rstd {h}"))
                        for which, slot in (("p_state", 5), ("s_state", 7)):
                            act.wait_ge(dve_done, A("dve", f"gla state {h}"))
                            act.dma_start(io[which][bass.ds(l * C_HEADS + h, 1), :, :].rearrange("a p n -> (a p) n"), state[:, slot, :]).then_inc(stored, 16)
                            count["stored"] += 16
                        for i in range(2):
                            k = 2 * h + i
                            round_tile(oc_hi[:, k, :], oc_raw[:, k, :], (dve_done, A("dve", f"gla out {h} {i}")), f"oc hi {k}")

                def prep_a(s):
                    if s == 0:
                        for e, name in (("dve", "gla out 3 1"), ("pe", "gla ms 3"), ("pe", "gla o 3")):
                            act.wait_ge({"dve": dve_done, "pe": pe_done}[e], A(e, name))
                        act.wait_ge(stored, 32 * C_HEADS)
                        for dst, name in ((wuk, "w_uk"), (wuv, "w_uv"), (cct, "a_ckv")):
                            act.dma_start(dst[:, :, :], io[name][bass.ds(l, 1)].rearrange("a (k p) n -> p (a k) n", p=P)).then_inc(a_loaded, 16)
                        act.dma_start(kr_c[:, :], io["a_kr"][bass.ds(l, 1)].rearrange("a p n -> (a p) n")).then_inc(a_loaded, 16)
                    if s == 2:
                        store(io["c_out"][bass.ds(l, 1)].rearrange("a (k p) n -> p (a k) n", p=P), ckv[:, :, :], "dve", "c 1")
                        store(io["kr_out"][bass.ds(l, 1)].rearrange("a p n -> (a p) n"), krot[0:32, :], "dve", "krot")
                    if s == 0:
                        act.wait_ge(dve_done, A("dve", f"evac {UIDX['ckv', 1]} 0 1"))
                        act.wait_ge(act_done, A("act", f"oc hi {KD - 1}"))
                        act.wait_ge(pool_done, A("pool", f"oc lo {KD - 1}"))
                        act.activation(cksq[:, :, :], ckv[:, :, :], ACT.Square).then_inc(act_done, st.done("act", "ckv sq"))
                        act.wait_ge(pe_done, A("pe", "prep a 0"))
                        link(act.activation(rstd[:, :].rearrange("p (a n) -> p a n", a=2), ps[:, 0:2, 0:HALF], ACT.Ln,
                                            bias=eps[:, 0:1]), "prep a 0")
                        act.activation(rstd[:, :], rstd[:, :], ACT.Exp, scale=-0.5).then_inc(act_done, st.done("act", "c rstd"))
                    if prep_evac(s) == "act" and s > 0:
                        act.wait_ge(pe_done, A("pe", f"prep a {s}"))
                        pair = PAIRS[s % 2]
                        if s < 8:
                            act.activation(kn[:, s - 4, :].rearrange("p (a n) -> p a n", a=2), ps[:, pair, 0:HALF], ACT.Copy
                                           ).then_inc(act_done, st.done("act", f"prep a {s}"))
                        elif s < 10:
                            act.activation(kn_c[:, 2 * (s - 8):2 * (s - 8) + 2, :], ps[:, pair, 0:CKEYS], ACT.Copy
                                           ).then_inc(act_done, st.done("act", f"prep a {s}"))
                        else:
                            for i, (_, _, n, dst) in enumerate(VA_TILES[s - 10]):
                                act.activation(dst, ps[0:n, pair.start + i, :], ACT.Copy).then_inc(
                                    act_done, st.done("act", f"prep a {s}" if i == len(VA_TILES[s - 10]) - 1 else None))

                def att(br, j):
                    n = len(JOBS[br])
                    if j < n:
                        _, t, i = JOBS[br][j]
                        pb = prob_view(br, j)
                        nk = key_count(br, i)
                        rows = P if i < 4 else MIXED
                        act.wait_ge(dve_done, A("dve", f"{br} shift {j}"))
                        k = 2 if br == "a" else 4
                        w = nk if br == "a" else nk + 1
                        sc = A_SCALE if br == "a" else B_SCALE
                        for a in range(k):
                            act.activation(pb[0:rows, a, 0:w], pb[0:rows, a, 0:w], ACT.Exp, scale=sc,
                                           accum_out=stat[0:rows, j % 2, 8 + a:9 + a]
                                           ).then_inc(act_done, st.done("act", f"{br} exp {j}" if a == k - 1 else None))
                    if br == "a" and j >= 6 and (j - 6) % 5 == 0:
                        t = (j - 6) // 5
                        if t == 0:
                            act.wait_ge(pe_done, A("pe", "prep a 14"))
                            act.wait_ge(stored, 32 * C_HEADS + 32)
                        round_tile(oa_hi[:, t, :], oa_raw[:, t, :], (dve_done, A("dve", f"a o {5 * t + 4}")), f"oa hi {t}")
                    if br == "b" and j == n + 1:
                        for g in range(4):
                            round_tile(ob_hi[:, g, :], ob_raw[:, g, :], (dve_done, A("dve", f"b o {n - 1}")), f"ob hi {g}")

                for u in range(2):
                    w_hi(u)
                for step in order:
                    if step[0] == "dense":
                        evac(step[1])
                        after_evac(step[1])
                        if step[1] + 2 < NU:
                            w_hi(step[1] + 2)
                    elif step[0] == "norm":
                        norm(step[1])
                    elif step[0] == "gla":
                        gla(step[1], step[2])
                    elif step[0] == "prep_a":
                        prep_a(step[1])
                    elif step[0] == "prep_b":
                        if step[1] == 0:
                            act.wait_ge(pe_done, A("pe", f"a values {len(jobs) - 1}"))
                            for dst, name in ((kb_c, "b_k"), (vb_c, "b_v"), (vb_cm, "b_vm")):
                                act.dma_start(dst[:, :], io[name][bass.ds(l, 1)].rearrange("a p n -> (a p) n")).then_inc(b_loaded, 16)
                            for name, src in (("kw_out", "b_kw"), ("vw_out", "b_vw")):
                                act.dma_start(io[name][bass.ds(l, 1)].rearrange("a p n -> (a p) n")[:, 0:WIN - DEC],
                                               io[src][bass.ds(l, 1)].rearrange("a p n -> (a p) n")[:, DEC:WIN]).then_inc(stored, 16)
                                count["stored"] += 16
                            store(io["kw_out"][bass.ds(l, 1)].rearrange("a p n -> (a p) n")[:, WIN - DEC:WIN], kb[:, SAMP0:T], "dve", f"evac {UIDX['kb', 0]} 0 1")
                            store(io["vw_out"][bass.ds(l, 1)].rearrange("a p n -> (a p) n")[:, WIN - DEC:WIN], vb[:, SAMP0:T], "act", f"evac {UIDX['vb', 0]} 0 1")
                            store(io["kb_out"][bass.ds(l, 1)].rearrange("a p n -> (a p) n"), kb[:, 384:T], "dve", f"evac {UIDX['kb', 0]} 0 1")
                            store(io["vb_out"][bass.ds(l, 1)].rearrange("a p n -> (a p) n"), vb[:, 384:T], "act", f"evac {UIDX['vb', 0]} 0 1")
                        if step[1] == 1:
                            act.wait_ge(pe_done, A("pe", "b vtok"))
                            act.activation(v_own[:, :, :].rearrange("p a n -> p (a n)"), ps[:, T0, :], ACT.Copy).then_inc(act_done, st.done("act", "b vtok"))
                    elif step[0] == "att":
                        att(step[1], step[2])
                    elif step[0] == "split_y":
                        for k in range(KD):
                            act.wait_ge(pe_done, A("pe", f"dense {UIDX['gate_b', 7]}"))
                            round_tile(h_hi[:, k, :], y[:, k, :], (pool_done, A("pool", f"y b {k}")), f"y hi {k}")
                        act.wait_ge(pool_done, A("pool", f"y lo {KD - 1}"))
                        act.wait_ge(spilled, 16)
                        act.dma_start(x[:, :, :], io["x_spill"]).then_inc(x_back, 16)

                act.wait_ge(stored, count["stored"])

            @block.vector
            def _(dve):
                def link(ins, name=None):
                    ins.then_inc(dve_done, st.done("dve", name))
                    dve.wait_ge(dve_done, st.count["dve"])

                def evac(u):
                    kind, n = UNITS[u]
                    if kind == "ff1":
                        t = hid[n // 8 % 2][0][:, n % 8, :]
                        dve.wait_ge(act_done, A("act", f"evac {u} 0 1"))
                        dve.tensor_tensor(t, t, t, ALU.mult).then_inc(dve_done, st.done("dve", f"hid {n}"))
                    if kind.startswith("gate"):
                        dve.wait_ge(act_done, A("act", f"evac {u} 0 1"))
                        s = sig[:, n % 2, :]
                        link(dve.tensor_scalar(s, s, 1.0, None, ALU.add))
                        link(dve.reciprocal(s, s), f"sig {kind} {n}")
                    if evac_engine(kind) != "dve":
                        return
                    for o in range(outs_of(kind)[0]):
                        for hf in range(2):
                            src = dps[bank_of[u, o, hf]][:, 0:HALF]
                            dve.wait_ge(pe_done, A("pe", f"half {u} {o} {hf}"))
                            c = H[hf]
                            if kind == "kralr":
                                ins = dve.tensor_copy(kra[0:112, c], src[0:112, :])
                            elif kind == "cq":
                                if hf == 0 and n >= 2:
                                    dve.wait_ge(dve_done, A("dve", f"gla qe {n - 2}"))
                                ins = dve.tensor_scalar(cproj[n % 2][:, 0, c], src, float(C_DK ** -0.5), None, ALU.mult)
                            elif kind == "cv":
                                h, i = n // 2, n % 2
                                if hf == 0 and h >= 2:
                                    dve.wait_ge(pe_done, A("pe", f"gla vtok {h - 2} 5"))
                                ins = dve.tensor_copy(cproj[h % 2][:, 2 + i, c], src)
                            elif kind in ("ckv", "qr", "qn"):
                                if hf == 0:
                                    dve.wait_ge(pe_done, A("pe", f"gla ms {C_HEADS - 1 if kind == 'qr' else C_HEADS - 2}"))
                                dst = {"ckv": ckv, "qr": qr, "qn": qn}[kind]
                                ins = dve.tensor_copy(dst[:, n, c], src)
                            elif kind == "kb":
                                if hf == 0:
                                    dve.wait_ge(pe_done, A("pe", f"a values {len(jobs) - 1}"))
                                    dve.wait_ge(stored, 32 * C_HEADS + 32)
                                ins = dve.tensor_copy(kb[:, c], src)
                            elif kind == "qb":
                                ins = dve.tensor_copy(qb[:, n, c], src)
                            elif kind == "up_c":
                                if n == 0 and hf == 0:
                                    dve.wait_ge(pe_done, A("pe", f"gla ms {C_HEADS - 1}"))
                                ins = dve.tensor_tensor(y[:, n, c], sig[:, n % 2, c], src, ALU.mult)
                            elif kind in ("up_a", "up_b"):
                                ins = dve.tensor_tensor(sig[:, o, c], sig[:, o, c], src, ALU.mult)
                            elif kind == "ff2":
                                g, m = n // 8, n % 8
                                if g == 0:
                                    if m == 0 and hf == 0:
                                        dve.wait_ge(stored, 32 * C_HEADS + 32 + 96)
                                    ins = dve.tensor_copy(facc[:, m, c], src)
                                else:
                                    if hf == 0:
                                        dve.wait_ge(dve_done, A("dve", f"evac {UIDX['ff2', n - 8]} 0 1"))
                                    ins = dve.tensor_tensor(facc[:, m, c], facc[:, m, c], src, ALU.add)
                            ins.then_inc(dve_done, st.done("dve", f"evac {u} {o} {hf}"))

                def norm(which):
                    src = norm_src[which]
                    for k in range(1, KD, 2):
                        if which == "post_mix":
                            dve.wait_ge(act_done, A("act", f"evac {UIDX['out', k]} 0 1"))
                            dve.wait_ge(pe_done, A("pe", f"dense {UIDX['up_c', KD - 1]}"))
                        elif which == "pre_mlp":
                            dve.wait_ge(dve_done, A("dve", f"x post_mix {k}"))
                        elif which == "post_mlp":
                            dve.wait_ge(dve_done, A("dve", f"evac {UIDX['ff2', 24 + k]} 0 1"))
                            dve.wait_ge(pe_done, A("pe", f"dense {UIDX['ff2', 23]}"))
                        dve.tensor_tensor(sq[:, k, :], src[:, k, :], src[:, k, :], ALU.mult).then_inc(dve_done, st.done("dve", f"sq {which} {k}"))
                    dve.wait_ge(act_done, A("act", f"rstd {which}"))
                    dve.wait_ge(par_loaded, 32)
                    for k in range(KD):
                        g = p_("g_" + which, k)
                        if which in ("pre_mix", "pre_mlp"):
                            if which == "pre_mlp" and k == 0:
                                dve.wait_ge(pe_done, A("pe", f"dense {UIDX['out', KD - 1]}"))
                            dve.scalar_tensor_tensor(h_raw[:, k, :], src[:, k, :], g, rstd[:, :], ALU.mult, ALU.mult
                                                     ).then_inc(dve_done, st.done("dve", f"h raw {which} {k}"))
                        else:
                            t = src[:, k, :]
                            if k == 0:
                                dve.wait_ge(pe_done, A("pe", f"ms {which}"))
                                if which == "post_mix":
                                    dve.wait_ge(x_back, 16)
                            dve.wait_ge(act_done, A("act", f"rstd {which}"))
                            dve.scalar_tensor_tensor(t, t, g, rstd[:, :], ALU.mult, ALU.mult).then_inc(dve_done, st.done("dve", f"nrm {which} {k}"))
                    if which in ("post_mix", "post_mlp"):
                        for k in range(KD):
                            dve.wait_ge(dve_done, A("dve", f"nrm {which} {k}"))
                            dve.tensor_tensor(x[:, k, :], x[:, k, :], src[:, k, :], ALU.add).then_inc(dve_done, st.done("dve", f"x {which} {k}"))

                def sb_view(t, a, n):
                    return t[:, a:a + n]

                def gla(h, s):
                    pr = cproj[h % 2]
                    q, kk = pr[:, 0, :], pr[:, 1, :]
                    q3 = q.rearrange("p (b t) -> p b t", t=BLK)
                    k3 = kk.rearrange("p (b t) -> p b t", t=BLK)
                    if s == "v decay":
                        dve.wait_ge(act_done, A("act", f"gla ln {h}"))
                        if h > 0:
                            dve.wait_ge(act_done, A("act", f"gla eb {h - 1}"))
                            dve.wait_ge(pool_done, A("pool", f"gla kend {h - 1}"))
                        link(dve.scalar_tensor_tensor(lsig[:, :], zlog[:, :], 0.0, ztmp[:, :], ALU.min, ALU.subtract), f"gla lg {h}")
                        for a, n in SUPER:
                            dve.tensor_tensor_scan(bcum[:, a:a + n], c_("ones")[:, 0:n], lsig[:, a:a + n], 0.0, ALU.mult, ALU.add
                                                   ).then_inc(dve_done, st.done("dve", f"gla scan {h}" if a == SAMP0 else None))
                    if s.startswith("v diag"):
                        for j in range(4 * int(s[-1]), 4 * int(s[-1]) + 4):
                            w = BLK - j
                            e = ediag_of(j).rearrange("p (b t) -> p b t", t=w)
                            dve.wait_ge(act_done, A("act", f"gla e {h} {j}"))
                            if j == 0:
                                dve.wait_ge(act_done, A("act", f"evac {UIDX['ck', h]} 0 1"))
                            link(dve.tensor_tensor(e, e, k3[:, :, j:j + 1].to_broadcast([P, NBLK, w]), ALU.mult))
                            dve.tensor_tensor(e, e, q3[:, :, j:], ALU.mult).then_inc(dve_done, st.done("dve", f"gla e {h} {j}"))
                    if s == "v farq":
                        dve.wait_ge(act_done, A("act", f"gla far q {h}"))
                        qf = qfar[:, :].rearrange("p (b i t) -> p b i t", b=4, t=BLK)
                        q4 = q[:, 0:SEQ].rearrange("p (b i t) -> p b i t", b=4, t=BLK)[:, :, 1:, :]
                        dve.tensor_tensor(qf, qf, q4, ALU.mult).then_inc(dve_done, st.done("dve"))
                        dve.tensor_tensor(qfar_s[:, :], qfar_s[:, :], q[:, SAMP0 + BLK:T], ALU.mult).then_inc(dve_done, st.done("dve"))
                        dve.tensor_tensor(kfar_s[:, :], kfar_s[:, :], kk[:, SAMP0:SAMP0 + BLK], ALU.mult).then_inc(dve_done, st.done("dve", f"gla far s {h}"))
                    if s == "v far":
                        for i in range(1, 8):
                            dve.wait_ge(act_done, A("act", f"gla far {h} {i}"))
                            kf = kfar_of(i).rearrange("p (b s) -> p b s", b=4)
                            k4 = kk[:, 0:SEQ].rearrange("p (b s) -> p b s", b=4)[:, :, 0:16 * i]
                            dve.tensor_tensor(kf, kf, k4, ALU.mult).then_inc(dve_done, st.done("dve", f"gla far {h} {i}"))
                    if s == "v kend":
                        dve.wait_ge(act_done, A("act", f"gla kend {h}"))
                        dve.tensor_tensor(kend[:, :], kend[:, :], kk, ALU.mult).then_inc(dve_done, st.done("dve", f"gla kend {h}"))
                        dve.wait_ge(act_done, A("act", f"gla eb {h}"))
                        if h > 0:
                            dve.wait_ge(pe_done, A("pe", f"gla o {h - 1}"))
                        else:
                            dve.wait_ge(spilled, 16)
                        dve.tensor_tensor(qe[:, :], ebl[:, :], q, ALU.mult).then_inc(dve_done, st.done("dve", f"gla qe {h}"))
                    if s == "v amat":
                        if h > 0:
                            dve.wait_ge(pe_done, A("pe", f"gla o {h - 1}"))
                        dve.wait_ge(pe_done, A("pe", f"gla diag {h} 15"))
                        dve.wait_ge(pe_done, A("pe", f"gla far {h} 7"))
                        am = amat[:, 0:SEQ].rearrange("p (b t) -> p b t", b=4)
                        bm = c_("blockmask").rearrange("p (a t) -> p a t", a=1).to_broadcast([P, 4, 128])
                        dve.tensor_tensor(am, ps[:, S0, :].rearrange("p (b t) -> p b t", b=4), bm, ALU.mult).then_inc(dve_done, st.done("dve"))
                        dve.tensor_copy(amat[0:META, META0:SAMP0], ps[0:META, S1, 0:META]).then_inc(dve_done, st.done("dve"))
                        link(dve.tensor_tensor(amat[0:DEC, SAMP0:T], ps[0:DEC, S1, META:48], c_("blockmask", DEC)[:, 0:DEC], ALU.mult))
                        dve.tensor_tensor(amat[:, 0:SEQ], amat[:, 0:SEQ], ps[:, T0, :], ALU.add).then_inc(dve_done, st.done("dve"))
                        dve.tensor_tensor(amat[0:DEC, SAMP0:T], amat[0:DEC, SAMP0:T], ps[0:DEC, T1, 0:DEC], ALU.add
                                          ).then_inc(dve_done, st.done("dve", f"gla amat {h}"))
                    if s == "v silu":
                        dve.wait_ge(act_done, A("act", f"gla gate {h}"))
                        link(dve.tensor_scalar(gsig[:, :, :], gsig[:, :, :], 1.0, None, ALU.add))
                        link(dve.reciprocal(gsig[:, :, :], gsig[:, :, :]))
                        dve.tensor_tensor(gsig[:, :, :], gsig[:, :, :], pr[:, 4:6, :], ALU.mult).then_inc(dve_done, st.done("dve", f"gla silu {h}"))
                    if s == "v state":
                        dve.wait_ge(pe_done, A("pe", f"gla kv {h}"))
                        dve.wait_ge(pool_done, A("pool", "gla zero"))
                        dve.wait_ge(state_loaded, 16 * (h + 1))
                        if h > 0:
                            dve.wait_ge(stored, 32 * h)
                        for sb in range(6):
                            a, n = SUPER[sb]
                            bank = (S0, S1, T0)[sb // 2]
                            kv = ps[:, bank, 256 * (sb % 2):256 * (sb % 2) + 256]
                            link(dve.scalar_tensor_tensor(state[:, STATE_OUT[sb], :], state[:, STATE_IN[sb], :],
                                                          ebl[:, a + n - 1:a + n], kv, ALU.mult, ALU.add),
                                 f"gla state {h}" if sb == 5 else None)
                    if s == "v out":
                        dve.wait_ge(act_done, A("act", f"gla rstd {h}"))
                        for i in range(2):
                            link(dve.scalar_tensor_tensor(oh[:, i, :], oh[:, i, :], p_("g_gla", i), rstd[:, :], ALU.mult, ALU.mult))
                            dve.tensor_tensor(oc_raw[:, 2 * h + i, :], oh[:, i, :], gsig[:, i, :], ALU.mult
                                              ).then_inc(dve_done, st.done("dve", f"gla out {h} {i}"))

                def rotate(dst, raw, pair, rows, name, last):
                    c2 = c_("cos", rows).rearrange("p (a n) -> p a n", a=2)
                    s2 = c_("sin", rows).rearrange("p (a n) -> p a n", a=2)
                    t = rtmp[0:rows, :].rearrange("p (a n) -> p a n", a=2)
                    dve.tensor_tensor(dst.rearrange("p (a n) -> p a n", a=2), raw.rearrange("p (a n) -> p a n", a=2), c2, ALU.mult).then_inc(dve_done, st.done("dve"))
                    dve.tensor_tensor(t, ps[0:rows, pair, 0:HALF], s2, ALU.mult).then_inc(dve_done, st.done("dve", name))
                    dve.wait_ge(dve_done, st.count["dve"])
                    link(dve.tensor_tensor(dst, dst, rtmp[0:rows, :], ALU.add), last)

                def prep_a(s):
                    if s == 1:
                        dve.wait_ge(act_done, A("act", "c rstd"))
                        for k in range(KL):
                            dve.scalar_tensor_tensor(ckv[:, k, :], ckv[:, k, :], p_("g_kv", k), rstd[:, :], ALU.mult, ALU.mult
                                                     ).then_inc(dve_done, st.done("dve", f"c {k}"))
                        dve.wait_ge(pe_done, A("pe", "prep a 1"))
                        rotate(krot[0:96, :], kra[0:96, :], PAIRS[1], 96, "prep a 1", None)
                        dve.tensor_copy(krot[96:128, :], krot[0:32, :]).then_inc(dve_done, st.done("dve", "krot"))
                    if s in (2, 3):
                        dve.wait_ge(pe_done, A("pe", f"prep a {s}"))
                        rotate(qrot[:, s - 2, :], qr[:, s - 2, :], PAIRS[s % 2], P, f"prep a {s}", f"qrot {s - 2}")
                    if s >= 4 and prep_evac(s) == "dve":
                        pair = PAIRS[s % 2]
                        dve.wait_ge(pe_done, A("pe", f"prep a {s}"))
                        if s < 8:
                            dve.tensor_copy(kn[:, s - 4, :].rearrange("p (a n) -> p a n", a=2), ps[:, pair, 0:HALF]
                                            ).then_inc(dve_done, st.done("dve", f"prep a {s}"))
                        elif s < 10:
                            dve.tensor_copy(kn_c[:, 2 * (s - 8):2 * (s - 8) + 2, :], ps[:, pair, 0:CKEYS]
                                            ).then_inc(dve_done, st.done("dve", f"prep a {s}"))
                        else:
                            for i, (_, _, n, dst) in enumerate(VA_TILES[s - 10]):
                                dve.tensor_copy(dst, ps[0:n, pair.start + i, :]).then_inc(dve_done, st.done("dve", f"prep a {s}" if i == len(VA_TILES[s - 10]) - 1 else None))

                def att(br, j):
                    n = len(JOBS[br])
                    if j < n:
                        _, t, i = JOBS[br][j]
                        pb = prob_view(br, j)
                        nk = key_count(br, i)
                        k = 2 if br == "a" else 4
                        rows = P if i < 4 else MIXED
                        sm = stat[0:rows, j % 2, :]
                        dve.wait_ge(pe_done, A("pe", f"{br} scores {j}"))
                        if j >= 2:
                            dve.wait_ge(pe_done, A("pe", f"{br} turn {j - 2}"))
                            dve.wait_ge(pool_done, A("pool", f"{br} prob {j - 2}"))
                        elif br == "b":
                            dve.wait_ge(pe_done, A("pe", f"a turn {len(jobs) - 1}"))
                        elif j == 0:
                            pass
                        if br == "a" and i < 3:
                            link(dve.tensor_reduce(sm[:, 4:6], ps[:, S0:S1 + 1, 0:nk], AX.X, ALU.max))
                            mx = sm[:, 4:6].rearrange("p (a n) -> p a n", n=1)
                            dve.tensor_tensor(pb[:, :, :], ps[:, S0:S1 + 1, 0:nk], mx.to_broadcast([P, 2, nk]), ALU.subtract
                                              ).then_inc(dve_done, st.done("dve", f"a shift {j}"))
                        elif br == "a" and i == 3:
                            nf = nk - META
                            mt = ps[0:rows, M_, 0:32].rearrange("p (a n) -> p a n", a=2)
                            dve.tensor_reduce(sm[:, 0:2], ps[:, S0:S1 + 1, 0:nf], AX.X, ALU.max).then_inc(dve_done, st.done("dve"))
                            link(dve.tensor_reduce(sm[:, 2:4], mt, AX.X, ALU.max))
                            link(dve.tensor_tensor(sm[:, 4:6], sm[:, 0:2], sm[:, 2:4], ALU.max))
                            mx = sm[:, 4:6].rearrange("p (a n) -> p a n", n=1)
                            dve.tensor_tensor(pb[:, :, 0:nf], ps[:, S0:S1 + 1, 0:nf], mx.to_broadcast([P, 2, nf]), ALU.subtract).then_inc(dve_done, st.done("dve"))
                            dve.tensor_tensor(pb[:, :, nf:nk], mt, mx.to_broadcast([P, 2, META]), ALU.subtract
                                              ).then_inc(dve_done, st.done("dve", f"a shift {j}"))
                        elif br == "a":
                            ms = c_("mask_s", MIXED).rearrange("p (a n) -> p a n", a=1).to_broadcast([MIXED, 2, 320])
                            link(dve.tensor_tensor(pb[0:rows, :, :], ps[0:rows, S0:S1 + 1, 0:320], ms, ALU.add))
                            link(dve.tensor_reduce(sm[:, 4:6], pb[0:rows, :, :], AX.X, ALU.max))
                            mx = sm[:, 4:6].rearrange("p (a n) -> p a n", n=1)
                            dve.tensor_tensor(pb[0:rows, :, :], pb[0:rows, :, :], mx.to_broadcast([rows, 2, 320]), ALU.subtract
                                              ).then_inc(dve_done, st.done("dve", f"a shift {j}"))
                        else:
                            for g in range(4):
                                if i < 4:
                                    src = ps[:, S0 + g // 2, 208 * (g % 2) + 208 - nk:208 * (g % 2) + 208]
                                    dist = c_("dist")[:, 208 - nk:208]
                                else:
                                    src = ps[0:rows, S0 + g // 2, 192 * (g % 2):192 * (g % 2) + 192]
                                    dist = c_("dist_s", rows)
                                slope = 2.0 ** -(4 * t + g + 1)
                                dve.scalar_tensor_tensor(pb[0:rows, g, 0:nk], dist, -slope / B_SCALE, src, ALU.mult, ALU.add
                                                         ).then_inc(dve_done, st.done("dve", f"b bias {j}" if g == 3 else None))
                            link(dve.tensor_scalar(pb[0:rows, :, nk], p_("sinks", 4 * t, 4, rows), 1.0 / B_SCALE, None, ALU.mult))
                            link(dve.tensor_reduce(sm[:, 4:8], pb[0:rows, :, :], AX.X, ALU.max))
                            mx = sm[:, 4:8].rearrange("p (a n) -> p a n", n=1)
                            dve.tensor_tensor(pb[0:rows, :, :], pb[0:rows, :, :], mx.to_broadcast([rows, 4, nk + 1]), ALU.subtract
                                              ).then_inc(dve_done, st.done("dve", f"b shift {j}"))
                    if 1 <= j <= n:
                        jj = j - 1
                        _, t, i = JOBS[br][jj]
                        if jj >= 1:
                            dve.wait_ge(pe_done, A("pe", f"{br} values {jj - 1}"))
                        dve.wait_ge(pe_done, A("pe", f"{br} turn {jj}"))
                        if br == "a":
                            if i < 4:
                                nf = 128 * (i + 1)
                                dve.tensor_copy(ptf[:, :, 0:nf], ps[:, T0:T1 + 1, 0:nf]).then_inc(dve_done, st.done("dve"))
                                dve.tensor_copy(ptm[:, 0:256], ps[0:META, O_, 256:512]).then_inc(dve_done, st.done("dve", f"a turned {jj}"))
                            else:
                                dve.tensor_copy(ptf[:, :, 0:96], ps[:, T0:T1 + 1, 0:96]).then_inc(dve_done, st.done("dve"))
                                dve.tensor_copy(ptf[0:DEC, :, 96:144], ps[0:DEC, T0:T1 + 1, 96:144]).then_inc(dve_done, st.done("dve"))
                                dve.tensor_copy(ptf[0:META, :, 144:240], ps[0:META, T0:T1 + 1, 144:240]).then_inc(dve_done, st.done("dve", f"a turned {jj}"))
                        elif i < 4:
                            dve.tensor_copy(ptf[:, 0, :], ps[:, T0, :]).then_inc(dve_done, st.done("dve"))
                            if i > 0:
                                dve.tensor_copy(ptf[0:64, 1, :], ps[0:64, T1, :]).then_inc(dve_done, st.done("dve"))
                            dve.tensor_copy(ptm[:, :], ps[0:META, M_, :]).then_inc(dve_done, st.done("dve", f"b turned {jj}"))
                        else:
                            dve.tensor_copy(ptf[:, 0, 0:192], ps[:, T0, 0:192]).then_inc(dve_done, st.done("dve"))
                            dve.tensor_copy(ptf[0:DEC, 1, 0:192], ps[0:DEC, T1, 0:192]).then_inc(dve_done, st.done("dve"))
                            dve.tensor_copy(ptm[:, 0:384], ps[0:META, M_, 0:384]).then_inc(dve_done, st.done("dve", f"b turned {jj}"))
                    if j >= 2:
                        jj = j - 2
                        _, t, i = JOBS[br][jj]
                        dve.wait_ge(pe_done, A("pe", f"{br} values {jj}"))
                        qc = slice(128 * i, 128 * i + 128) if i < 4 else slice(META0, T)
                        w = 128 if i < 4 else MIXED
                        if br == "a":
                            dve.tensor_copy(oa_raw[:, t, qc], ps[:, O_, 0:w]).then_inc(dve_done, st.done("dve", f"a o {jj}"))
                        else:
                            r = slice(64 * t, 64 * t + 64)
                            dve.tensor_copy(ob_raw[r, :, qc], ps[r, O_, 0:4 * w].rearrange("p (g n) -> p g n", g=4)
                                            ).then_inc(dve_done, st.done("dve", f"b o {jj}"))
                    if j < n:
                        k = 2 if br == "a" else 4
                        sm = stat[0:P if JOBS[br][j][2] < 4 else MIXED, j % 2, :]
                        dve.wait_ge(act_done, A("act", f"{br} exp {j}"))
                        dve.reciprocal(sm[:, 12:12 + k], sm[:, 8:8 + k]).then_inc(dve_done, st.done("dve", f"{br} rsum {j}"))

                for step in order:
                    if step[0] == "dense":
                        evac(step[1])
                    elif step[0] == "norm":
                        norm(step[1])
                    elif step[0] == "gla":
                        gla(step[1], step[2])
                    elif step[0] == "prep_a":
                        prep_a(step[1])
                    elif step[0] == "prep_b":
                        if step[1] == 1:
                            dve.wait_ge(pe_done, A("pe", "b vtok"))
                            dve.tensor_copy(v_prev[:, :, :].rearrange("p a n -> p (a n)"), ps[0:64, T1, 0:384]).then_inc(dve_done, st.done("dve"))
                            dve.tensor_copy(v_pm[:, :], ps[0:META, M_, 0:128]).then_inc(dve_done, st.done("dve"))
                            dve.tensor_copy(v_new[:, :], ps[0:DEC, M_, 128:256]).then_inc(dve_done, st.done("dve", "b vtok"))
                    elif step[0] == "att":
                        att(step[1], step[2])

            @block.gpsimd
            def _(pool):
                def link(ins, name=None):
                    ins.then_inc(pool_done, st.done("pool", name))
                    pool.wait_ge(pool_done, st.count["pool"])

                def w_lo(u):
                    slot = u % WSLOTS
                    pool.wait_ge(act_done, A("act", f"w hi {u}"))
                    pool.tensor_tensor(wlo[slot][:, :], wraw[slot][:, :], whi[slot][:, :].bitcast(F32), ALU.subtract
                                       ).then_inc(pool_done, st.done("pool", f"w lo {u}"))

                def lo_tile(lo, raw, hi, name, hname):
                    pool.wait_ge(act_done, A("act", hname))
                    pool.tensor_tensor(lo, raw, hi.bitcast(F32), ALU.subtract).then_inc(pool_done, st.done("pool", name))

                def evac(u):
                    kind, n = UNITS[u]
                    if kind == "ff1":
                        s = hid[n // 8 % 2]
                        lo_tile(s[1][:, n % 8, :], s[0][:, n % 8, :], s[2][:, n % 8, :], f"hid lo {n}", f"hid hi {n}")
                    if kind in ("up_a", "up_b"):
                        for o in range(2):
                            pool.wait_ge(dve_done, A("dve", f"evac {u} {o} 1"))
                            pool.tensor_tensor(y[:, n + o, :], y[:, n + o, :], sig[:, o, :], ALU.add
                                               ).then_inc(pool_done, st.done("pool", f"y {kind[-1]} {n + o}"))

                def gla(h, s):
                    b3 = bcum[:, :].rearrange("p (b t) -> p b t", t=BLK)
                    if s == "v decay":
                        if h > 0:
                            pool.wait_ge(dve_done, A("dve", f"gla state {h - 1}"))
                            pool.wait_ge(pe_done, A("pe", f"gla o {h - 1}"))
                        if h == 0:
                            link(pool.memset(state[:, 0, :], 0.0), "gla zero")
                    if s.startswith("v diag"):
                        for j in range(4 * int(s[-1]), 4 * int(s[-1]) + 4):
                            w = BLK - j
                            e = ediag_of(j).rearrange("p (b t) -> p b t", t=w)
                            if j == 0:
                                pool.wait_ge(dve_done, A("dve", f"gla scan {h}"))
                            pool.tensor_tensor(e, b3[:, :, j:], b3[:, :, j:j + 1].to_broadcast([P, NBLK, w]), ALU.subtract
                                               ).then_inc(pool_done, st.done("pool", f"gla d {h} {j}"))
                    if s == "v farq":
                        if h > 0:
                            pool.wait_ge(pe_done, A("pe", f"gla far {h - 1} 7"))
                        b4 = bcum[:, 0:SEQ].rearrange("p (b i t) -> p b i t", b=4, t=BLK)
                        qf = qfar[:, :].rearrange("p (b i t) -> p b i t", b=4, t=BLK)
                        for b in range(4):
                            pool.tensor_tensor(qf[:, b], b4[:, b, 1:, :], b4[:, b, 0:7, 15:16].to_broadcast([P, 7, BLK]), ALU.subtract
                                               ).then_inc(pool_done, st.done("pool"))
                        ref = bcum[:, SAMP0 + 15:SAMP0 + 16].to_broadcast([P, BLK])
                        pool.tensor_tensor(qfar_s[:, :], bcum[:, SAMP0 + BLK:T], ref, ALU.subtract).then_inc(pool_done, st.done("pool"))
                        pool.tensor_tensor(kfar_s[:, :], ref, bcum[:, SAMP0:SAMP0 + BLK], ALU.subtract).then_inc(pool_done, st.done("pool", f"gla far q {h}"))
                    if s == "v far":
                        b4 = bcum[:, 0:SEQ].rearrange("p (b s) -> p b s", b=4)
                        for i in range(1, 8):
                            kf = kfar_of(i).rearrange("p (b s) -> p b s", b=4)
                            pool.tensor_tensor(kf, b4[:, :, 16 * i - 1:16 * i].to_broadcast([P, 4, 16 * i]), b4[:, :, 0:16 * i], ALU.subtract
                                               ).then_inc(pool_done, st.done("pool", f"gla far {h} {i}"))
                    if s == "v kend":
                        pool.wait_ge(dve_done, A("dve", f"gla lg {h}"))
                        if h > 0:
                            pool.wait_ge(pe_done, A("pe", f"gla ktok {h - 1} 1"))
                        for i, (a, n) in enumerate(SUPER):
                            pool.tensor_tensor(kend[:, a:a + n], bcum[:, a + n - 1:a + n].to_broadcast([P, n]), bcum[:, a:a + n], ALU.subtract
                                               ).then_inc(pool_done, st.done("pool", f"gla kend {h}" if i == 5 else None))
                    if s == "v out":
                        for i in range(2):
                            k = 2 * h + i
                            lo_tile(oc_lo[:, k, :], oc_raw[:, k, :], oc_hi[:, k, :], f"oc lo {k}", f"oc hi {k}")

                def att(br, j):
                    n = len(JOBS[br])
                    if j < n:
                        _, t, i = JOBS[br][j]
                        pb = prob_view(br, j)
                        k = 2 if br == "a" else 4
                        rows = P if i < 4 else MIXED
                        w = pb.shape[2]
                        pool.wait_ge(dve_done, A("dve", f"{br} rsum {j}"))
                        rs = stat[0:rows, j % 2, 12:12 + k].rearrange("p (a n) -> p a n", n=1).to_broadcast([rows, k, w])
                        pool.tensor_tensor(pb[0:rows, :, :], pb[0:rows, :, :], rs, ALU.mult).then_inc(pool_done, st.done("pool", f"{br} prob {j}"))
                    if br == "a" and j >= 6 and (j - 6) % 5 == 0:
                        t = (j - 6) // 5
                        lo_tile(oa_lo[:, t, :], oa_raw[:, t, :], oa_hi[:, t, :], f"oa lo {t}", f"oa hi {t}")
                    if br == "b" and j == n + 1:
                        for g in range(4):
                            lo_tile(ob_lo[:, g, :], ob_raw[:, g, :], ob_hi[:, g, :], f"ob lo {g}", f"ob hi {g}")

                for u in range(2):
                    w_lo(u)
                for step in order:
                    if step[0] == "dense":
                        evac(step[1])
                        if step[1] + 2 < NU:
                            w_lo(step[1] + 2)
                    elif step[0] == "norm":
                        if step[1] in ("pre_mix", "pre_mlp"):
                            name = "h" if step[1] == "pre_mix" else "h2"
                            for k in range(KD):
                                lo_tile(h_lo[:, k, :], h_raw[:, k, :], h_hi[:, k, :], f"{name} lo {k}", f"{name} hi {k}")
                    elif step[0] == "gla":
                        gla(step[1], step[2])
                    elif step[0] == "att":
                        att(step[1], step[2])
                    elif step[0] == "split_y":
                        for k in range(KD):
                            pool.wait_ge(act_done, A("act", f"y hi {k}"))
                            pool.tensor_tensor(h_lo[:, k, :], y[:, k, :], h_hi[:, k, :].bitcast(F32), ALU.subtract).then_inc(pool_done, st.done("pool", f"y lo {k}"))
        with nc.Fori(0, DEPTH) as l:
            with nc.Block() as block:
                layer(l, block)
            for s_ in block_sems:
                nc.sync.sem_clear(s_)
            nc.all_engine_barrier()

        with nc.Block() as block:
            @block.sync
            def _(sp):
                sp.dma_start(io["y_out"].rearrange("(k p) t -> p k t", p=P), x[:, :, :]).then_inc(last_stored, 16)
                sp.wait_ge(last_stored, 16)
    return st.seen


def shape_constants():
    c = np.zeros((P, NCONST), np.float32)

    def put(name, value, rows=P):
        a, w = CONST[name]
        c[0:rows, a:a + w] = value

    put("ident", np.eye(P))
    put("ones_d", 1.0 / D)
    put("ones_v", 1.0 / C_DV)
    perm = np.zeros((P, P))
    for j in range(P):
        if j % A_ROPE < A_ROPE // 2:
            perm[j + A_ROPE // 2, j] = -1.0
        else:
            perm[j - A_ROPE // 2, j] = 1.0
    put("perm", perm)
    put("selrep", (np.arange(144) % BLK == BLK - 1).astype(np.float32)[None])
    blk = np.arange(P) // BLK
    put("blockmask", (blk[:, None] == blk[None, :]).astype(np.float32))
    half = A_ROPE // 2
    inv = np.float32(10000.0) ** (-np.arange(half, dtype=np.float32) / np.float32(half))
    pos = np.concatenate([np.arange(SEQ), np.zeros(META), PAST + np.arange(DEC)]).astype(np.float32)
    ang = pos[None, :] * inv[np.arange(P) % half][:, None].astype(np.float32)
    put("cos", np.cos(ang.astype(np.float32)))
    put("sin", np.sin(ang.astype(np.float32)))
    far = 1e34
    r = np.arange(P)[:, None]
    prev, own = np.arange(-CHUNK, 0)[None], np.arange(P)[None]
    put("dist", np.concatenate([np.where(r < CHUNK, np.abs(r - prev), far), np.zeros((P, META)),
                                np.where(own // CHUNK <= r // CHUNK, np.abs(r - own), far)], 1))
    d = np.full((MIXED, 192), far)
    q = PAST + np.arange(DEC)[:, None]
    k = PAST - WIN + np.arange(WIN + DEC)[None]
    seen = (k // CHUNK <= q // CHUNK) & (k // CHUNK > q // CHUNK - WIN // CHUNK)
    d[META:, 0:WIN + DEC] = np.where(seen, np.abs(q - k), far)
    d[META:, WIN + DEC:WIN + DEC + META] = 0.0
    d[0:META, WIN + DEC + META:] = 0.0
    put("dist_s", d, MIXED)
    m = np.full((MIXED, 320), NEG)
    m[META:, 0:304] = 0.0
    m[0:META, 304:] = 0.0
    put("mask_s", m, MIXED)
    put("rows", (np.arange(P) < CHUNK).astype(np.float32)[None])
    put("neg", NEG)
    put("ones", 1.0)
    put("eps", EPS)
    return c


def pack_units(i, l):
    w_in = i["w_in"][l]
    sizes = [512, 256, 256, 32, 512, 128, 128, 512, 512, 1024, 16, 1024, 3072]
    edge = np.concatenate([[0], np.cumsum(sizes)])
    part = {n: w_in[:, edge[j]:edge[j + 1]] for j, n in enumerate(
        ("qn", "qr", "ckv", "kr", "qb", "kb", "vb", "cq", "ck", "cv", "alr", "cg", "gate"))}
    qb = part["qb"].reshape(D, B_KV, B_G, B_HD).transpose(0, 2, 1, 3).reshape(D, -1)
    up_b = i["w_up_b"][l].reshape(B_KV, B_G, B_HD, D).transpose(1, 0, 2, 3).reshape(-1, D)
    out = np.empty((NU, P, 1024), np.float32)
    for u, (kind, n) in enumerate(UNITS):
        c = slice(128 * n, 128 * n + 128)
        if kind == "kralr":
            m = np.concatenate([part["kr"]] * 3 + [part["alr"], np.zeros((D, 16), np.float32)], 1)
        elif kind == "qb":
            m = qb[:, c]
        elif kind.startswith("gate"):
            b = "abc".index(kind[-1])
            m = part["gate"][:, D * b + 128 * n:D * b + 128 * n + 128]
        elif kind == "up_c":
            m = i["w_up_c"][l][:, c]
        elif kind in ("up_a", "up_b"):
            m = (i["w_up_a"][l] if kind == "up_a" else up_b)[:, 128 * n:128 * n + 256]
        elif kind == "out":
            m = i["w_out"][l][:, c]
        elif kind == "ff1":
            m = i["w_ff1"][l][:, c]
        elif kind == "ff2":
            g, t = n // 8, n % 8
            m = i["w_ff2"][l][D * g:D * g + D, 128 * t:128 * t + 128]
        else:
            m = part[kind][:, c]
        k = m.shape[0] // P
        out[u] = m.reshape(k, P, m.shape[1]).transpose(1, 0, 2).reshape(P, 1024)
    return out


def pack_params(i, l):
    p = np.zeros((P, NPARAM), np.float32)

    def put(name, v):
        a, w = PARAM[name]
        p[:, a:a + w] = v

    for name in ("g_pre_mix", "g_post_mix", "g_pre_mlp", "g_post_mlp", "g_kv", "g_gla", "b_alpha"):
        put(name, i[name][l].reshape(-1, P).T)
    put("sinks", np.repeat(i["b_sinks"][l][None], P, 0))
    return p


OUTPUTS = {"y_out": (D, T), "c_out": (DEPTH, LORA, T), "kr_out": (DEPTH, A_ROPE, T),
           "kb_out": (DEPTH, P, T - 384), "vb_out": (DEPTH, P, T - 384),
           "kw_out": (DEPTH, P, WIN), "vw_out": (DEPTH, P, WIN),
           "p_state": (DEPTH * C_HEADS, C_DK, C_DV), "s_state": (DEPTH * C_HEADS, C_DK, C_DV)}


def kernel(**inputs):
    import concourse.bacc as bacc
    from concourse.bass_utils import run_bass_kernel_spmd

    i = {k: np.asarray(v) for k, v in inputs.items()}
    two = range(DEPTH)
    t = lambda a: np.ascontiguousarray(np.swapaxes(a, -1, -2))
    a_ckv = np.concatenate([i["cache_A_ckv"][:, 0], i["cache_A_meta_ckv"][:, 0]], 1)
    a_kr = np.concatenate([i["cache_A_krope"][:, 0], i["cache_A_meta_krope"][:, 0]], 1)
    b_k = i["cache_B_k"][:, 0].reshape(DEPTH, WIN, P)
    b_v = i["cache_B_v"][:, 0].reshape(DEPTH, WIN, P)
    b_mk = i["cache_B_meta_k"][:, 0].reshape(DEPTH, META, P)
    arrays = {
        "x": t(np.concatenate([i["x_prompt"][0], i["meta_tokens"], i["x_sample"][0]], 0)),
        "const": shape_constants(),
        "w": np.stack([pack_units(i, l) for l in two]).reshape(DEPTH * NU, P, 1024),
        "par": np.stack([pack_params(i, l) for l in two]),
        "w_alpha": i["w_alpha"], "w_uk": i["w_uk"].reshape(DEPTH, LORA, 512), "w_uv": i["w_uv"].reshape(DEPTH, LORA, 512),
        "a_ckv": t(a_ckv), "a_kr": np.tile(t(a_kr), (1, 4, 1)),
        "b_k": t(np.concatenate([b_k, b_mk], 1)), "b_v": b_v,
        "b_vm": i["cache_B_meta_v"][:, 0].reshape(DEPTH, META, P),
        "b_kw": t(b_k), "b_vw": t(b_v),
        "state": i["state_C"][:, 0].reshape(DEPTH * C_HEADS, C_DK, C_DV),
    }
    arrays = {k: np.ascontiguousarray(v) for k, v in arrays.items()}

    def program(known):
        nc = bacc.Bacc("TRN2", target_bir_lowering=False, num_devices=1)
        io = {k: nc.dram_tensor("in_" + k, v.shape, F32, kind="ExternalInput").ap() for k, v in arrays.items()}
        io.update({k: nc.dram_tensor("out_" + k, v, F32, kind="ExternalOutput").ap() for k, v in OUTPUTS.items()})
        io["x_spill"] = nc.dram_tensor("x_spill", (P, KD, T), F32, kind="Internal").ap()
        return nc, build(nc, io, known)

    _, known = program(None)
    nc, _ = program(known)
    r = run_bass_kernel_spmd(nc, [{"in_" + k: v for k, v in arrays.items()}], core_ids=[0]).results[0]
    o = {k: r["out_" + k] for k in OUTPUTS}

    y = t(o["y_out"])
    c, kr = t(o["c_out"]), t(o["kr_out"])
    kb, vb, kw, vw = t(o["kb_out"]), t(o["vb_out"]), t(o["kw_out"]), t(o["vw_out"])
    f, m, s = slice(0, SEQ), slice(META0, SAMP0), slice(SAMP0, T)
    heads = lambda a: a.reshape(DEPTH, 1, -1, B_KV, B_HD)
    states = lambda a: a.reshape(DEPTH, 1, C_HEADS, C_DK, C_DV)
    return (y[None, f], y[None, s], c[:, None, f], kr[:, None, f], c[:, None, m], kr[:, None, m],
            heads(kb[:, 0:128]), heads(vb[:, 0:128]), heads(kb[:, 128:144]), heads(vb[:, 128:144]),
            states(o["p_state"]), c[:, None, s], kr[:, None, s], heads(kw), heads(vw), states(o["s_state"]))
```

```python
import concourse.bass as bass
from concourse import mybir
from contextlib import ExitStack
import numpy as np

F32 = mybir.dt.float32
F32R = mybir.dt.float32r
ALU = mybir.AluOpType
ACT = mybir.ActivationFunctionType
AX = mybir.AxisListType

P = 128
D = 1024
KD = D // P
SEQ, META, DEC = 512, 16, 32
T = SEQ + META + DEC
HALF = T // 2
DEPTH = 2
CHUNK = 64
PAST = 256
LORA, KL = 256, 2
A_HEADS, A_NOPE, A_ROPE, A_V = 8, 64, 32, 64
B_HEADS, B_KV, B_HD = 8, 2, 64
B_G = B_HEADS // B_KV
WIN = 128
C_HEADS, C_DK, C_DV, C_LR = 4, 128, 256, 16
D_FF = 4 * D
BLK = 16
EPS = 1e-6
A_SCALE = float((A_NOPE + A_ROPE) ** -0.5)
B_SCALE = float(B_HD ** -0.5)
META0, SAMP0 = SEQ, SEQ + META
MIXED = META + DEC
CKEYS = PAST + META
NBLK = T // BLK
SBS = 128 // BLK
NEG = -1e30
WSLOTS = 3

SUPER = [(META0, META)] + [(128 * i, 128) for i in range(SEQ // 128)] + [(SAMP0, DEC)]


def plan_units():
    units = [("kralr", 0)]
    for h in range(C_HEADS):
        units += [("cq", h), ("ck", h), ("cv", 2 * h), ("cv", 2 * h + 1), ("cg", 2 * h), ("cg", 2 * h + 1)]
    units += [("ckv", n) for n in range(2)] + [("qn", n) for n in range(4)] + [("qr", n) for n in range(2)]
    for n in range(KD):
        units += [("gate_c", n), ("up_c", n)]
    units += [("gate_a", 0), ("gate_a", 1)]
    units += [("kb", 0), ("vb", 0)] + [("qb", n) for n in range(4)]
    for b in "ab":
        for n in range(0, KD, 2):
            if (b, n) != ("a", 0):
                units += [("gate_" + b, n), ("gate_" + b, n + 1)]
            units += [("up_" + b, n)]
    units += [("out", n) for n in range(KD)]
    ff1 = [[("ff1", 8 * g + n) for n in range(8)] for g in range(4)]
    ff2 = [[("ff2", 8 * g + n) for n in range(8)] for g in range(4)]
    units += ff1[0] + ff1[1] + ff2[0] + ff1[2] + ff2[1] + ff1[3] + ff2[2] + ff2[3]
    return units


UNITS = plan_units()
NU = len(UNITS)
UIDX = {u: n for n, u in enumerate(UNITS)}


def outs_of(kind):
    return (2, 4) if kind in ("up_a", "up_b") else (1, KD)


CONST = {}
_at = 0
for _name, _w in (("ident", 128), ("ones_d", 128), ("ones_v", 128), ("perm", 128), ("selrep", 144),
                  ("blockmask", 128), ("cos", T), ("sin", T), ("dist", 208), ("mask_s", 320),
                  ("dist_s", 192), ("rows", 128), ("neg", 64), ("ones", 128), ("zeros", 128), ("eps", 1)):
    CONST[_name] = (_at, _w)
    _at += _w
NCONST = _at
PARAM = {}
_at = 0
for _name, _w in (("g_post_mix", 8), ("g_pre_mlp", 8), ("g_post_mlp", 8), ("g_kv", 2),
                  ("g_gla", 2), ("b_alpha", 4), ("sinks", 8)):
    PARAM[_name] = (_at, _w)
    _at += _w
NPARAM = _at


class Steps:

    def __init__(self, known):
        self.count = {e: 0 for e in ("pe", "act", "dve", "pool")}
        self.known = known
        self.seen = {}

    def done(self, engine, name=None):
        self.count[engine] += 1
        if name is not None:
            assert (engine, name) not in self.seen, name
            self.seen[engine, name] = self.count[engine]
        return 1

    def at(self, engine, name):
        if self.known is None:
            return 1
        return self.known[engine, name]


def build(nc, io, known):
    st = Steps(known)
    ctx = ExitStack()
    with ctx:
        def sem(name):
            return ctx.enter_context(nc.semaphore(name))

        base = 16512
        place = {"next": base}

        def at(name, shape, dt, offset):
            size = 4 * int(np.prod(shape[1:]))
            assert offset + size <= 229344, (name, offset + size)
            return nc.alloc_sbuf_tensor_at(name, shape, dt, offset=offset)

        def region(size):
            off = place["next"]
            place["next"] += (size + 31) // 32 * 32
            return off

        row = 4 * T
        r_w = [region(8192) for _ in range(WSLOTS)]
        r_h = region(16 * row)
        r_oc = region(16 * row)
        r_x = region(8 * row)
        r_sig = region(2 * row)
        r_r = region(row)
        r_const = region(4 * NCONST)
        r_par = region(4 * NPARAM)
        r_gpre = region(4 * KD)
        work = place["next"]

        wraw = [at(f"wraw{s}", [P, 1024], F32, r_w[s]) for s in range(WSLOTS)]
        wlo = [at(f"wlo{s}", [P, 1024], F32R, r_w[s]) for s in range(WSLOTS)]
        whi = [at(f"whi{s}", [P, 1024], F32R, r_w[s] + 4096) for s in range(WSLOTS)]

        def split_set(name, n, off):
            return (at(name + "_raw", [P, n, T], F32, off), at(name + "_lo", [P, n, T], F32R, off),
                    at(name + "_hi", [P, n, T], F32R, off + n * row))

        h_raw, h_lo, h_hi = split_set("h", KD, r_h)
        oc_raw, oc_lo, oc_hi = split_set("oc", KD, r_oc)
        hid0 = split_set("hid0", KD, r_oc)
        hid1 = split_set("hid1", KD, work)
        hid = [hid0, hid1]
        mix = at("mix", [P, KD, T], F32, r_oc)
        sq = at("sq", [P, KD, T], F32, r_oc + KD * row)
        sqsum, sqpart = sq[:, 0, :], [sq[:, 1, :], sq[:, 2, :]]
        facc = at("facc", [P, KD, T], F32, work + 16 * row)
        x = at("x", [P, KD, T], F32, r_x)
        y = at("y", [P, KD, T], F32, r_x)
        sig = at("sig", [P, 2, T], F32, r_sig)
        rstd = at("rstd", [P, T], F32, r_r)
        const = at("const", [P, NCONST], F32, r_const)
        par = at("par", [P, NPARAM], F32, r_par)
        g_pre_mix = at("g_pre_mix", [P, KD], F32, r_gpre)

        def c_(name, rows=P):
            a, w = CONST[name]
            return const[0:rows, a:a + w]

        w_alpha = const[:, CONST["mask_s"][0]:CONST["mask_s"][0] + 512]

        def p_(name, n=0, w=1, rows=P, r0=0):
            a = PARAM[name][0] + n
            return par[r0:r0 + rows, a:a + w]

        wk = {"next": work}

        def wt(name, shape, dt=F32, off=None):
            size = 4 * int(np.prod(shape[1:]))
            if off is None:
                off = wk["next"]
                wk["next"] += (size + 31) // 32 * 32
            return at(name, shape, dt, off), off

        kra, _ = wt("kra", [P, T])
        keep = wk["next"]
        cproj = [wt(f"cproj{i}", [P, 6, T])[0] for i in range(2)]
        bcum, _ = wt("bcum", [P, T])
        ediag, ediag_off = wt("ediag", [P, NBLK * BLK * (BLK + 1) // 2])
        kfar, _ = wt("kfar", [P, 64 * 28])
        zlog = at("zlog", [P, T], F32, ediag_off)
        ztmp = at("ztmp", [P, T], F32, ediag_off + row)
        lsig = at("lsig", [P, T], F32, ediag_off + 2 * row)
        kfar_s, _ = wt("kfar_s", [P, BLK])
        qfar, _ = wt("qfar", [P, 4 * 112])
        qfar_s, _ = wt("qfar_s", [P, BLK])
        kend, _ = wt("kend", [P, T])
        ebl, _ = wt("ebl", [P, T])
        amat, _ = wt("amat", [P, T])
        ktok, _ = wt("ktok", [P, 6, 128])
        state, _ = wt("state", [P, 8, C_DV])
        assert wk["next"] <= 229344, wk["next"]
        gsq = at("gsq", [P, 2, T], F32, r_x)
        oh = at("oh", [P, 2, T], F32, r_x + 2 * row)
        vtok = at("vtok", [P, 6, 256], F32, r_x + 4 * row)
        qe = at("qe", [P, T], F32, r_x + 4 * row + 6144)
        gsig = sig
        cksq = at("cksq", [P, 2, T], F32, r_sig)
        wk["next"] = keep
        oa_raw, oa_lo, oa_hi = split_set("oa", 4, keep)
        qn = at("qn", [P, 4, T], F32, keep)
        wk["next"] = keep + 8 * row
        a_tmp = keep + 4 * row
        ckv = at("ckv", [P, KL, T], F32, a_tmp)
        cct = at("cct", [P, KL, CKEYS], F32, a_tmp + 2 * row)
        qr, _ = wt("qr", [P, 2, T])
        qrot, _ = wt("qrot", [P, 2, T])
        kn, _ = wt("kn", [P, 4, T])
        krot, _ = wt("krot", [P, T])
        va, _ = wt("va", [P, 4, 512])
        va_pm, _ = wt("va_pm", [META, 512])
        va_new, _ = wt("va_new", [DEC, 512])
        kn_c, _ = wt("kn_c", [P, 4, CKEYS])
        va_c, _ = wt("va_c", [P, 2, 512])
        va_cm, _ = wt("va_cm", [META, 512])
        kr_c, _ = wt("kr_c", [P, CKEYS])
        p_off = wk["next"]
        prob = [wt(f"prob{i}", [P, 1056])[0] for i in range(2)]
        wuk = at("wuk", [P, KL, 512], F32, p_off)
        wuv = at("wuv", [P, KL, 512], F32, p_off + 4096)
        ptf_off = wk["next"]
        ptf, _ = wt("ptf", [P, 2, 512])
        ptm, _ = wt("ptm", [META, 512])
        stat, _ = wt("stat", [P, 2, 24])
        a_end = wk["next"]
        assert a_end <= 229344, a_end
        wk["next"] = keep + 8 * row
        ob_raw, ob_lo, ob_hi = split_set("ob", 4, wk["next"])
        wk["next"] += 8 * row
        qb = at("qb", [P, 4, T], F32, wk["next"])
        wk["next"] += 4 * row
        kb, _ = wt("kb", [P, T])
        vb, _ = wt("vb", [P, T])
        v_own, _ = wt("v_own", [P, 4, 128])
        v_prev, _ = wt("v_prev", [64, 3, 128])
        v_pm, _ = wt("v_pm", [META, 128])
        v_new, _ = wt("v_new", [DEC, 128])
        kb_c, _ = wt("kb_c", [P, WIN + META])
        vb_c, _ = wt("vb_c", [P, 128])
        vb_cm, _ = wt("vb_cm", [META, 128])
        assert wk["next"] <= p_off, (wk["next"], p_off)

        dps = [ctx.enter_context(nc.psum_tensor(f"dense{i}", [P, 512], F32)) for i in range(2)]
        ps = ctx.enter_context(nc.psum_tensor("att", [P, 6, 512], F32))
        S0, S1, M_, T0, T1, O_ = range(6)
        PAIRS = [slice(0, 2), slice(3, 5)]

        pe_done, act_done, dve_done, pool_done = (sem(n) for n in ("pe_done", "act_done", "dve_done", "pool_done"))
        w_loaded = [sem(f"w_loaded{s}") for s in range(WSLOTS)]
        w_ahead = [sem(f"w_ahead{s}") for s in range(WSLOTS)]
        par_loaded = sem("par_loaded")
        spilled = sem("x_spilled")
        x_back = sem("x_back")
        a_loaded = sem("a_cache_loaded")
        b_loaded = sem("b_cache_loaded")
        state_loaded = sem("state_loaded")
        stored = sem("outputs_stored")
        block_sems = [pe_done, act_done, dve_done, pool_done, *w_loaded, *w_ahead, par_loaded, spilled, x_back, a_loaded,
                      b_loaded, state_loaded, stored]
        ahead_loaded = sem("ahead_loaded")
        block_sems.append(ahead_loaded)
        ones_loaded, rest_loaded, w_first = sem("ones_loaded"), sem("rest_loaded"), sem("first_weights_loaded")
        x_loaded = [sem(f"x_loaded{i}") for i in range(4)]
        first_sq, first_ms, first_rstd, first_hi, first_lo = (sem("first_" + n) for n in ("sq", "ms", "rstd", "hi", "lo"))
        last_stored = sem("last_stored")

        rtmp = at("rtmp", [P, T], F32, ptf_off)
        eps = c_("eps")
        zero_l = c_("zeros")
        STATE_IN = [0, 1, 2, 3, 4, 6]
        STATE_OUT = [1, 2, 3, 4, 5, 7]
        VTOK_PAIRS = [(1, 2), (3, 4), (0, 5)]
        VTOK_BANKS = [M_, O_, T1]
        VA_TILES = [
            [(ckv, 0, 128, va[:, 0, :]), (ckv, 128, 128, va[:, 1, :])],
            [(ckv, 256, 128, va[:, 2, :]), (ckv, 384, 128, va[:, 3, :])],
            [(cct, 0, 128, va_c[:, 0, :]), (cct, 128, 128, va_c[:, 1, :])],
            [(cct, PAST, META, va_cm[:, :]), (ckv, META0, META, va_pm[:, :])],
            [(ckv, SAMP0, DEC, va_new[:, :])],
        ]
        PREP_A_OVER = [("act", "prep a 14"), ("dve", "prep a 13"), ("dve", "krot"), ("dve", "qrot 1")]

        def ediag_of(j):
            a = NBLK * (BLK * j - j * (j - 1) // 2)
            return ediag[:, a:a + NBLK * (BLK - j)]

        def kfar_of(i):
            a = 32 * i * (i - 1)
            return kfar[:, a:a + 64 * i]

        def prep_evac(s):
            if s == 0:
                return "act"
            if s < 4:
                return "dve"
            return "act" if s % 2 == 0 else "dve"

        with nc.Block() as block:
            @block.sync
            def _(sp):
                sp.dma_start(const[:, 0:256], io["const"][:, 0:256]).then_inc(ones_loaded, 16)
                for i in range(4):
                    sp.dma_start(x[:, 2 * i:2 * i + 2, :], io["x"][256 * i:256 * i + 256, :].rearrange("(k p) t -> p k t", p=P)
                                 ).then_inc(x_loaded[i], 16)
                for u in range(WSLOTS):
                    sp.dma_start(wraw[u][:, :], io["w"][u]).then_inc(w_first, 16)
                sp.dma_start(g_pre_mix[:, :], io["g_pre_mix"][0]).then_inc(rest_loaded, 16)
                sp.dma_start(const[:, 256:], io["const"][:, 256:]).then_inc(rest_loaded, 16)
                sp.wait_ge(w_first, 16 * WSLOTS)
                sp.wait_ge(rest_loaded, 32)

            @block.tensor
            def _(pe):
                pe.wait_ge(ones_loaded, 16)
                for k in range(KD):
                    pe.wait_ge(first_sq, k + 1)
                    for hf in range(2):
                        mm = pe.matmul(ps[:, T0 + hf, 0:HALF], c_("ones_d"), sq[:, k, HALF * hf:HALF * hf + HALF],
                                       start=(k == 0), stop=(k == KD - 1))
                mm.then_inc(first_ms, 1)

            @block.scalar
            def _(act):
                act.preload_act_table_set("natural_log_exp_and_others")
                for k in range(KD):
                    act.wait_ge(x_loaded[k // 2], 16)
                    act.activation(sq[:, k, :], x[:, k, :], ACT.Square).then_inc(first_sq, 1)
                act.wait_ge(w_first, 16 * WSLOTS)
                for u in range(2):
                    act.activation(whi[u][:, :], wraw[u][:, :], ACT.Copy).then_inc(first_hi, 1)
                act.wait_ge(first_ms, 1)
                act.wait_ge(rest_loaded, 32)
                act.activation(rstd[:, :].rearrange("p (a n) -> p a n", a=2), ps[:, PAIRS[1], 0:HALF], ACT.Ln,
                               bias=eps[:, 0:1]).then_inc(first_rstd, 1)
                act.wait_ge(first_rstd, 1)
                act.activation(rstd[:, :], rstd[:, :], ACT.Exp, scale=-0.5).then_inc(first_rstd, 1)
                act.wait_ge(first_rstd, 2)

            @block.gpsimd
            def _(pool):
                for u in range(2):
                    pool.wait_ge(first_hi, u + 1)
                    pool.tensor_tensor(wlo[u][:, :], wraw[u][:, :], whi[u][:, :].bitcast(F32), ALU.subtract).then_inc(first_lo, 1)
                pool.wait_ge(first_lo, 2)

        def layer(l, block):
            H = (slice(0, HALF), slice(HALF, T))
            def A(e, n):
                return st.at(e, n)

            moving = {"h": (h_hi, h_lo), "oc": (oc_hi, oc_lo), "oa": (oa_hi, oa_lo), "ob": (ob_hi, ob_lo),
                      "y": (h_hi, h_lo), "h2": (h_hi, h_lo), "hid0": (hid0[2], hid0[1]), "hid1": (hid1[2], hid1[1])}

            def source(kind, n):
                if kind == "up_c":
                    return "oc"
                if kind == "up_a":
                    return "oa"
                if kind == "up_b":
                    return "ob"
                if kind == "out":
                    return "y"
                if kind == "ff1":
                    return "h2"
                if kind == "ff2":
                    return "hid%d" % (n // 8 % 2)
                return "h"

            def ready_names(kind, n, k):
                s = source(kind, n)
                if s.startswith("hid"):
                    g = n // 8
                    return ("act", f"hid hi {8 * g + k}"), ("pool", f"hid lo {8 * g + k}")
                lo = lo_engine(k) if s in ("h", "h2", "y") else "pool"
                return ("act", f"{s} hi {k}"), (lo, f"{s} lo {k}")

            halves_done = []
            for u, (kind, n) in enumerate(UNITS):
                for o in range(outs_of(kind)[0]):
                    for hf in range(2):
                        halves_done.append((u, o, hf))
            bank_of = {key: i % 2 for i, key in enumerate(halves_done)}
            before = {key: halves_done[i - 2] for i, key in enumerate(halves_done) if i >= 2}

            def evac_engine(kind):
                return "act" if kind in ("ck", "cg", "out", "ff1", "vb") else "dve"

            order = []
            dn = iter(range(NU))

            def dense(k=1):
                for _ in range(k):
                    order.append(("dense", next(dn)))

            order.append(("tokens", "pre_mix"))
            dense(1)
            dense(6)
            def gla_steps(*steps):
                for h, what in steps:
                    order.append(("gla", h, what))

            for h in range(C_HEADS):
                gla_steps((h, "p z"), (h, "v decay"))
                dense()
                if h > 0:
                    gla_steps((h - 1, "p ms"), (h - 1, "v out"))
                gla_steps((h, "v diag 0"), (h, "v diag 1"))
                dense()
                gla_steps((h, "p vtok"), (h, "v vtok"), (h, "p diag 0"), (h, "p diag 1"), (h, "v diag 2"), (h, "v diag 3"), (h, "v farq"))
                dense()
                gla_steps((h, "v far"), (h, "v kend"), (h, "p diag 2"), (h, "p diag 3"))
                dense()
                gla_steps((h, "p ktok"), (h, "p far"), (h, "v ktok"), (h, "v amat"))
                dense()
                gla_steps((h, "p kv"), (h, "v state"), (h, "v silu"))
                dense()
                gla_steps((h, "p o"), (h, "v o"))
            gla_steps((C_HEADS - 1, "p ms"), (C_HEADS - 1, "v out"))
            dense(2)
            for s in range(len(VA_TILES) + 10):
                order.append(("prep_a", s))
            jobs = [("a", t, i) for t in range(4) for i in range(5)]
            for j in range(len(jobs) + 2):
                order.append(("att", "a", j))
                if j not in (5, 10, 15, 21):
                    dense()
            dense(2)
            order.append(("prep_b", 0))
            dense(5)
            order.append(("prep_b", 1))
            jobs_b = [("b", kv, i) for kv in range(2) for i in range(5)]
            for j in range(len(jobs_b) + 2):
                order.append(("att", "b", j))
                dense()
            while True:
                try:
                    u = next(dn)
                except StopIteration:
                    break
                if UNITS[u] == ("up_b", 6):
                    order.append(("split_y", 0))
                if UNITS[u] == ("out", 0):
                    order.append(("split_y", 1))
                if UNITS[u] == ("ff1", 0):
                    order += [("norm", "post_mix"), ("mean", "pre_mlp"), ("tokens", "pre_mlp")]
                order.append(("dense", u))
            order += [("norm", "post_mlp"), ("mean", "next")]
            JOBS = {"a": jobs, "b": jobs_b}
            AHEAD = [u % WSLOTS for u in range(NU - WSLOTS, NU)]
            Y_SPLIT = [range(6), range(6, KD)]

            def y_engine(b, n):
                return "dve" if b == "b" and n >= 6 else "pool"

            def x_engine(k):
                return "pool" if k % 2 else "dve"

            def lo_engine(k):
                return "dve" if k % 2 else "pool"

            by_name = {"pe": pe_done, "act": act_done, "dve": dve_done, "pool": pool_done}
            norm_src = {"post_mix": mix, "post_mlp": facc}

            def summed(u):
                kind, n = UNITS[u]
                if kind == "out":
                    return "post_mix", n
                if kind == "ff2" and n >= 24:
                    return "post_mlp", n - 24
                return None

            def sig_free(b, n):
                if b == "c":
                    return (dve_done, A("dve", f"evac {UIDX['up_c', n - 2]} 0 1")) if n >= 2 else (pe_done, A("pe", "prep a 0"))
                if b == "a" and n < 2:
                    return dve_done, A("dve", f"evac {UIDX['up_c', n + 6]} 0 1")
                return pool_done, A("pool", f"y a {n + 6}" if n < 2 else f"y {b} {n - 2}")

            def key_count(br, i):
                if br == "a":
                    return 128 * (i + 1) + META if i < 4 else 320
                return (144 if i == 0 else 208) if i < 4 else 192

            def prob_view(br, j):
                _, t, i = JOBS[br][j]
                nk = key_count(br, i)
                if br == "a":
                    return prob[j % 2][:, 0:2 * nk].rearrange("p (a n) -> p a n", a=2)
                return prob[j % 2][:, 0:4 * (nk + 1)].rearrange("p (a n) -> p a n", a=4)

            @block.sync
            def _(sp):
                sp.dma_start(par[:, :], io["par"][bass.ds(l, 1), :, :].rearrange("a p n -> (a p) n")).then_inc(par_loaded, 16)
                sp.dma_start(w_alpha[96:112, :], io["w_alpha"][bass.ds(l, 1), :, :].rearrange("a p n -> (a p) n")).then_inc(par_loaded, 16)

                def load(slot, u):
                    sp.dma_start(wraw[slot][:, :], io["w"][bass.ds(l * NU + u, 1), :, :].rearrange("a p n -> (a p) n")
                                 ).then_inc(w_loaded[slot], 16)

                for u in range(WSLOTS, NU):
                    sp.wait_ge(pe_done, A("pe", f"dense {u - WSLOTS}"))
                    load(u % WSLOTS, u)
                sp.wait_ge(dve_done, A("dve", "h raw pre_mix 7"))
                sp.dma_start(g_pre_mix[:, :], io["g_pre_mix"][bass.ds(l + 1, 1), :, :].rearrange("a p n -> (a p) n")
                             ).then_inc(ahead_loaded, 16)
                for n, slot in enumerate(AHEAD):
                    sp.wait_ge(pe_done, A("pe", f"dense {NU - WSLOTS + n}"))
                    sp.dma_start(wraw[slot][:, :], io["w"][bass.ds(l * NU + NU + slot, 1), :, :].rearrange("a p n -> (a p) n")
                                 ).then_inc(w_ahead[slot], 16)
                sp.wait_ge(ahead_loaded, 16)
                for slot in AHEAD:
                    sp.wait_ge(w_ahead[slot], 16)

            @block.tensor
            def _(pe):
                first_use = set()

                def dense_unit(u):
                    kind, n = UNITS[u]
                    nout, kt = outs_of(kind)
                    slot = u % WSLOTS
                    hi_w = whi[slot][:, :].rearrange("p (k m) -> p k m", k=kt)
                    lo_w = wlo[slot][:, :].rearrange("p (k m) -> p k m", k=kt)
                    src = source(kind, n)
                    hi_x, lo_x = moving[src]
                    key = (src, n // 8) if kind == "ff2" else src
                    fresh = key not in first_use
                    first_use.add(key)
                    if u >= 2:
                        pe.wait_ge(act_done, A("act", f"w hi {u}"))
                        pe.wait_ge(pool_done, A("pool", f"w lo {u}"))
                    m = 112 if kind == "kralr" else 128
                    by_tile = fresh and src in ("h", "h2", "y")
                    if by_tile:
                        for hf in range(2):
                            if (u, 0, hf) in before:
                                pu, po, ph = before[u, 0, hf]
                                e = evac_engine(UNITS[pu][0])
                                pe.wait_ge(by_name[e], A(e, f"evac {pu} {po} {ph}"))
                        for k in range(kt):
                            for e, name in ready_names(kind, n, k):
                                pe.wait_ge(by_name[e], A(e, name))
                            for hf in range(2):
                                for i, (a, b) in enumerate(((hi_w, hi_x), (lo_w, hi_x), (hi_w, lo_x))):
                                    mm = pe.matmul(dps[bank_of[u, 0, hf]][0:m, 0:HALF], a[:, k, 0:m], b[:, k, H[hf]],
                                                   start=(k == 0 and i == 0), stop=(k == kt - 1 and i == 2))
                                if k == kt - 1:
                                    mm.then_inc(pe_done, st.done("pe", f"half {u} 0 {hf}"))
                        st.seen["pe", f"dense {u}"] = st.count["pe"]
                        return
                    for o in range(nout):
                        for hf in range(2):
                            bank = dps[bank_of[u, o, hf]]
                            if (u, o, hf) in before:
                                pu, po, ph = before[u, o, hf]
                                pe.wait_ge(act_done if evac_engine(UNITS[pu][0]) == "act" else dve_done,
                                           A(evac_engine(UNITS[pu][0]), f"evac {pu} {po} {ph}"))
                            for k in range(kt):
                                if fresh and o == 0 and hf == 0:
                                    for e, name in ready_names(kind, n, k):
                                        pe.wait_ge({"act": act_done, "pool": pool_done}[e], A(e, name))
                                for i, (a, b) in enumerate(((hi_w, hi_x), (lo_w, hi_x), (hi_w, lo_x))):
                                    mm = pe.matmul(bank[0:m, 0:HALF], a[:, k, o * 128:o * 128 + m], b[:, k, H[hf]],
                                                   start=(k == 0 and i == 0), stop=(k == kt - 1 and i == 2))
                            last = o == nout - 1 and hf == 1
                            mm.then_inc(pe_done, st.done("pe", f"half {u} {o} {hf}"))
                    st.seen["pe", f"dense {u}"] = st.count["pe"]

                def norm(which):
                    for hf in range(2):
                        pe.wait_ge(dve_done, A("dve", f"sum {which} 7 {hf}"))
                        mm = pe.matmul(ps[:, S0 + hf, 0:HALF], c_("ones_d"), sqsum[:, H[hf]], start=True, stop=True)
                    mm.then_inc(pe_done, st.done("pe", f"ms {which}"))

                def mean(which):
                    for k in range(KD):
                        pe.wait_ge(act_done, A("act", f"sq {which} {k}"))
                        for hf in range(2):
                            mm = pe.matmul(ps[:, T0 + hf, 0:HALF], c_("ones_d"), sq[:, k, H[hf]],
                                           start=(k == 0), stop=(k == KD - 1))
                    mm.then_inc(pe_done, st.done("pe", f"ms {which}"))

                def gla(h, s):
                    pr = cproj[h % 2]
                    q, kk = pr[:, 0, :], pr[:, 1, :]
                    if s == "p z":
                        if h == 0:
                            pe.wait_ge(dve_done, A("dve", f"evac {UIDX['kralr', 0]} 0 1"))
                            pe.wait_ge(par_loaded, 32)
                        else:
                            pe.wait_ge(dve_done, A("dve", f"gla state {h - 1}"))
                        for hf in range(2):
                            mm = pe.matmul(ps[:, S0 + hf, 0:HALF], w_alpha[96:112, 128 * h:128 * h + 128],
                                           kra[96:112, H[hf]], start=True, stop=True)
                        mm.then_inc(pe_done, st.done("pe", f"gla z {h}"))
                    if s.startswith("p diag"):
                        if s == "p diag 0":
                            pe.wait_ge(act_done, A("act", f"gla z {h}"))
                            if h > 0:
                                pe.wait_ge(act_done, A("act", f"gla rstd {h - 1}"))
                        for j in range(4 * int(s[-1]), 4 * int(s[-1]) + 4):
                            w = BLK - j
                            pe.wait_ge(dve_done, A("dve", f"gla e {h} {j}"))
                            a0 = CONST["selrep"][0] + 15 - j
                            e = ediag_of(j).rearrange("p (b t) -> p b t", t=w)
                            out0 = ps[:, S0, :].rearrange("p (b t) -> p b t", t=BLK)
                            out1 = ps[:, S1, 0:48].rearrange("p (b t) -> p b t", t=BLK)
                            pe.matmul(out0[:, :, j:], const[:, a0:a0 + 128], e[:, 0:32, :],
                                      start=(j == 0), stop=(j == 15))
                            mm = pe.matmul(out1[:, :, j:], const[:, a0:a0 + 128], e[:, 32:35, :],
                                           start=(j == 0), stop=(j == 15))
                            mm.then_inc(pe_done, st.done("pe", f"gla diag {h} {j}"))
                    if s == "p vtok":
                        pe.wait_ge(dve_done, A("dve", f"evac {UIDX['cv', 2 * h + 1]} 0 1"))
                        if h > 0:
                            pe.wait_ge(act_done, A("act", f"gla oevac {h - 1}"))
                        for g, pair in enumerate(VTOK_PAIRS):
                            for c, sb in enumerate(pair):
                                a, n = SUPER[sb]
                                for i in range(2):
                                    mm = pe.transpose(ps[0:n, VTOK_BANKS[g], 256 * c + 128 * i:256 * c + 128 * i + 128],
                                                      pr[:, 2 + i, a:a + n], c_("ident"))
                            mm.then_inc(pe_done, st.done("pe", f"gla vtok {h} {g}"))
                    if s == "p far":
                        for bank, n in ((T0, 512), (T1, 32)):
                            pe.matmul(ps[:, bank, 0:n], zero_l, c_("cos")[:, 0:n], start=True, stop=False,
                                      skip_group_check=True)
                        pe.wait_ge(dve_done, A("dve", f"gla far s {h}"))
                        pe.matmul(ps[0:16, T1, 16:32], kfar_s[:, :], qfar_s[:, :], start=False, stop=True,
                                  skip_group_check=True)
                        for i in range(1, 8):
                            pe.wait_ge(dve_done, A("dve", f"gla far {h} {i}"))
                            kf = kfar_of(i).rearrange("p (b s) -> p b s", b=4)
                            qf = qfar[:, :].rearrange("p (b i t) -> p b i t", b=4, t=BLK)
                            for sb in range(4):
                                mm = pe.matmul(ps[0:16 * i, T0, 128 * sb + 16 * i:128 * sb + 16 * i + 16],
                                               kf[:, sb, :], qf[:, sb, i - 1, :], start=False, stop=True,
                                               skip_group_check=True)
                            mm.then_inc(pe_done, st.done("pe", f"gla far {h} {i}"))
                    if s == "p ktok":
                        pe.wait_ge(dve_done, A("dve", f"gla kend {h}"))
                        pe.wait_ge(act_done, A("act", f"gla vtok {h}"))
                        for g, bank in ((0, M_), (1, O_)):
                            for i in range(3):
                                a, n = SUPER[3 * g + i]
                                mm = pe.transpose(ps[0:n, bank, 128 * i:128 * i + 128], kend[:, a:a + n], c_("ident"))
                            mm.then_inc(pe_done, st.done("pe", f"gla ktok {h} {g}"))
                    if s == "p kv":
                        pe.wait_ge(dve_done, A("dve", f"gla amat {h}"))
                        pe.wait_ge(act_done, A("act", f"gla ktok {h} 1"))
                        for sb in range(6):
                            a, n = SUPER[sb]
                            bank = (S0, S1, T0)[sb // 2]
                            mm = pe.matmul(ps[:, bank, 256 * (sb % 2):256 * (sb % 2) + 256], ktok[0:n, sb, :],
                                           vtok[0:n, sb, :], start=(sb % 2 == 0), stop=True, skip_group_check=True)
                        mm.then_inc(pe_done, st.done("pe", f"gla kv {h}"))
                    if s == "p o":
                        pe.wait_ge(dve_done, A("dve", f"gla state {h}"))
                        for vt in range(2):
                            for sb in range(6):
                                a, n = SUPER[sb]
                                if n == 128:
                                    dst = ps[:, (M_, O_)[vt], a:a + n]
                                else:
                                    dst = ps[:, T1, 48 * vt + a - SEQ:48 * vt + a - SEQ + n]
                                first = (sb == 1) or (vt == 0 and sb == 0)
                                pe.matmul(dst, vtok[0:n, sb, 128 * vt:128 * vt + 128], amat[0:n, a:a + n],
                                          start=first, stop=False, skip_group_check=True)
                                mm = pe.matmul(dst, state[:, STATE_IN[sb], 128 * vt:128 * vt + 128],
                                               qe[:, a:a + n], start=False, stop=True, skip_group_check=True)
                        mm.then_inc(pe_done, st.done("pe", f"gla o {h}"))
                    if s == "p ms":
                        pe.wait_ge(act_done, A("act", f"gla sq {h}"))
                        if h + 1 < C_HEADS:
                            pe.wait_ge(act_done, A("act", f"gla z {h + 1}"))
                        for i in range(2):
                            for hf in range(2):
                                mm = pe.matmul(ps[:, S0 + hf, 0:HALF], c_("ones_v"), gsq[:, i, H[hf]],
                                               start=(i == 0), stop=(i == 1))
                        mm.then_inc(pe_done, st.done("pe", f"gla ms {h}"))

                def prep_a(s):
                    pair = PAIRS[s % 2].start
                    if s >= 2:
                        e = prep_evac(s - 2)
                        pe.wait_ge(act_done if e == "act" else dve_done, A(e, f"prep a {s - 2}"))
                    elif s == 0:
                        pe.wait_ge(act_done, A("act", f"gla rstd {C_HEADS - 1}"))
                        pe.wait_ge(dve_done, A("dve", f"gla state {C_HEADS - 1}"))
                    if s == 0:
                        pe.wait_ge(act_done, A("act", "ckv sq"))
                        for k in range(KL):
                            for hf in range(2):
                                mm = pe.matmul(ps[:, pair + hf, 0:HALF], c_("ones_v"), cksq[:, k, H[hf]],
                                               start=(k == 0), stop=(k == KL - 1))
                    elif s == 1:
                        for hf in range(2):
                            mm = pe.matmul(ps[0:96, pair + hf, 0:HALF], const[0:96, CONST["perm"][0]:CONST["perm"][0] + 96],
                                           kra[0:96, H[hf]], start=True, stop=True)
                    elif s in (2, 3):
                        u = UIDX["qr", s - 2]
                        pe.wait_ge(dve_done, A("dve", f"evac {u} 0 1"))
                        for hf in range(2):
                            mm = pe.matmul(ps[:, pair + hf, 0:HALF], c_("perm"), qr[:, s - 2, H[hf]],
                                           start=True, stop=True)
                    elif s in (4, 5, 6, 7):
                        if s == 4:
                            pe.wait_ge(dve_done, A("dve", "c 1"))
                            pe.wait_ge(a_loaded, 64)
                        for hf in range(2):
                            for k in range(KL):
                                mm = pe.matmul(ps[:, pair + hf, 0:HALF], wuk[:, k, 128 * (s - 4):128 * (s - 4) + 128],
                                               ckv[:, k, H[hf]], start=(k == 0), stop=(k == KL - 1))
                    elif s in (8, 9):
                        for i in range(2):
                            n = 2 * (s - 8) + i
                            for k in range(KL):
                                mm = pe.matmul(ps[:, pair + i, 0:CKEYS], wuk[:, k, 128 * n:128 * n + 128],
                                               cct[:, k, :], start=(k == 0), stop=(k == KL - 1))
                    else:
                        for i, (src, a, n, _) in enumerate(VA_TILES[s - 10]):
                            for k in range(KL):
                                mm = pe.matmul(ps[0:n, pair + i, 0:512], src[:, k, a:a + n], wuv[:, k, :],
                                               start=(k == 0), stop=(k == KL - 1))
                    mm.then_inc(pe_done, st.done("pe", f"prep a {s}"))

                def scores(br, j):
                    _, t, i = JOBS[br][j]
                    if br == "a":
                        if j >= 1:
                            pe.wait_ge(dve_done, A("dve", f"a shift {j - 1}"))
                        if j == 0:
                            for e, name in PREP_A_OVER:
                                pe.wait_ge({"act": act_done, "dve": dve_done, "pool": pool_done}[e], A(e, name))
                        for a in range(2):
                            h = 2 * t + a
                            r64, r32 = slice(64 * a, 64 * a + 64), slice(32 * (h % 4), 32 * (h % 4) + 32)
                            if i < 4:
                                qc, nk = slice(128 * i, 128 * i + 128), 128 * (i + 1)
                                pe.matmul(ps[:, S0 + a, 0:nk], qn[r64, t, qc], kn[r64, t, 0:nk], start=True, stop=False,
                                          skip_group_check=True)
                                pe.matmul(ps[:, S0 + a, 0:nk], qrot[r32, h // 4, qc], krot[r32, 0:nk], start=False, stop=True,
                                          skip_group_check=True)
                                r1 = slice(r32.start, r32.start + 1)
                                pe.matmul(ps[:, S0 + a, nk - 64:nk], c_("rows")[r1], c_("neg")[r1], start=False, stop=True,
                                          skip_group_check=True)
                                mdst = ps[:, S0 + a, nk:nk + META] if i < 3 else ps[:, M_, 16 * a:16 * a + 16]
                                pe.matmul(mdst, qn[r64, t, qc], kn[r64, t, META0:META0 + META],
                                          start=(i == 3 and a == 0), stop=False, skip_group_check=True)
                                mm = pe.matmul(mdst, qr[r32, h // 4, qc],
                                               krot[r32, META0:META0 + META], start=False, stop=True, skip_group_check=True)
                                if i == 3 and a == 0:
                                    mm.then_inc(pe_done, st.done("pe"))
                                    pe.wait_ge(pe_done, st.count["pe"])
                            else:
                                qc = slice(META0, T)
                                first = True
                                for c0, n, kk_, kr_, rope in ((0, PAST, kn_c[r64, t, 0:PAST], kr_c[r32, 0:PAST], qrot),
                                                              (256, DEC, kn[r64, t, SAMP0:T], krot[r32, SAMP0:T], qrot),
                                                              (288, META, kn_c[r64, t, PAST:CKEYS], kr_c[r32, PAST:CKEYS], qr),
                                                              (304, META, kn[r64, t, META0:SAMP0], krot[r32, META0:SAMP0], qr)):
                                    dst = ps[0:MIXED, S0 + a, c0:c0 + n]
                                    pe.matmul(dst, qn[r64, t, qc], kk_, start=first, stop=False, skip_group_check=True)
                                    mm = pe.matmul(dst, rope[r32, h // 4, qc], kr_, start=False, stop=True,
                                                   skip_group_check=True)
                                    first = False
                    else:
                        if j >= 1:
                            pe.wait_ge(dve_done, A("dve", f"b bias {j - 1}"))
                        else:
                            pe.wait_ge(act_done, A("act", "b vtok"))
                            pe.wait_ge(dve_done, A("dve", "b vtok"))
                            pe.wait_ge(dve_done, A("dve", f"evac {UIDX['qb', 3]} 0 1"))
                            pe.wait_ge(b_loaded, 48)
                        r64 = slice(64 * t, 64 * t + 64)
                        for g in range(B_G):
                            if i < 4:
                                c0 = 208 * (g % 2)
                                qc = slice(128 * i, 128 * i + 128)
                                parts = [(64, META, kb[r64, META0:SAMP0]), (80, 128, kb[r64, qc])]
                                if i > 0:
                                    parts.append((0, 64, kb[r64, 128 * i - 64:128 * i]))
                                rows = P
                            else:
                                c0 = 192 * (g % 2)
                                qc = slice(META0, T)
                                parts = [(0, WIN, kb_c[r64, 0:WIN]), (128, DEC, kb[r64, SAMP0:T]),
                                         (160, META, kb_c[r64, WIN:WIN + META]), (176, META, kb[r64, META0:SAMP0])]
                                rows = MIXED
                            for n_, (o, w, key) in enumerate(parts):
                                mm = pe.matmul(ps[0:rows, S0 + g // 2, c0 + o:c0 + o + w], qb[r64, g, qc], key,
                                               start=(g % 2 == 0 and n_ == 0), stop=True, skip_group_check=True)
                    mm.then_inc(pe_done, st.done("pe", f"{br} scores {j}"))

                def turn(br, j):
                    _, t, i = JOBS[br][j]
                    pe.wait_ge(pool_done, A("pool", f"{br} prob {j}"))
                    if j >= 1:
                        pe.wait_ge(dve_done, A("dve", f"{br} turned {j - 1}"))
                    if j >= 2:
                        pe.wait_ge(dve_done, A("dve", f"{br} o {j - 2}"))
                    nk = key_count(br, i)
                    pb = prob_view(br, j)
                    if br == "a":
                        for a in range(2):
                            if i < 4:
                                for kt in range(i + 1):
                                    pe.transpose(ps[:, T0 + a, 128 * kt:128 * kt + 128], pb[:, a, 128 * kt:128 * kt + 128],
                                                 c_("ident"))
                                mm = pe.transpose(ps[0:META, O_, 256 + 128 * a:384 + 128 * a],
                                                  pb[:, a, nk - META:nk], c_("ident"))
                            else:
                                idn = const[0:MIXED, 0:MIXED]
                                for n_, (c0, w) in enumerate(((0, 128), (128, 128), (256, DEC), (288, META), (304, META))):
                                    mm = pe.transpose(ps[0:w, T0 + a, 48 * n_:48 * n_ + 48], pb[0:MIXED, a, c0:c0 + w], idn)
                    else:
                        for g in range(B_G):
                            if i < 4:
                                o = 0 if i > 0 else -64
                                c = slice(128 * g, 128 * g + 128)
                                if i > 0:
                                    pe.transpose(ps[0:64, T1, c], pb[:, g, 0:64], c_("ident"))
                                pe.transpose(ps[:, T0, c], pb[:, g, 80 + o:208 + o], c_("ident"))
                                mm = pe.transpose(ps[0:META, M_, c], pb[:, g, 64 + o:80 + o], c_("ident"))
                            else:
                                idn = const[0:MIXED, 0:MIXED]
                                c = slice(48 * g, 48 * g + 48)
                                pe.transpose(ps[:, T0, c], pb[0:MIXED, g, 0:WIN], idn)
                                pe.transpose(ps[0:DEC, T1, c], pb[0:MIXED, g, WIN:WIN + DEC], idn)
                                pe.transpose(ps[0:META, M_, c], pb[0:MIXED, g, 160:176], idn)
                                mm = pe.transpose(ps[0:META, M_, 192 + 48 * g:240 + 48 * g], pb[0:MIXED, g, 176:192], idn)
                    mm.then_inc(pe_done, st.done("pe", f"{br} turn {j}"))

                def values(br, j):
                    _, t, i = JOBS[br][j]
                    pe.wait_ge(dve_done, A("dve", f"{br} turned {j}"))
                    if j >= 1:
                        pe.wait_ge(dve_done, A("dve", f"{br} o {j - 1}"))
                    if br == "a":
                        for a in range(2):
                            hc = slice(64 * (2 * t + a), 64 * (2 * t + a) + 64)
                            if i < 4:
                                dst = ps[64 * a:64 * a + 64, O_, 0:128]
                                for kt in range(i + 1):
                                    pe.matmul(dst, va[:, kt, hc], ptf[:, a, 128 * kt:128 * kt + 128],
                                              start=(kt == 0), stop=False)
                                mm = pe.matmul(dst, va_pm[:, hc], ptm[:, 128 * a:128 * a + 128], start=False, stop=True)
                            else:
                                dst = ps[64 * a:64 * a + 64, O_, 0:MIXED]
                                pe.matmul(dst, va_c[:, 0, hc], ptf[:, a, 0:48], start=True, stop=False)
                                pe.matmul(dst, va_c[:, 1, hc], ptf[:, a, 48:96], start=False, stop=False)
                                pe.matmul(dst, va_new[:, hc], ptf[0:DEC, a, 96:144], start=False, stop=False)
                                pe.matmul(dst, va_cm[:, hc], ptf[0:META, a, 144:192], start=False, stop=False)
                                mm = pe.matmul(dst, va_pm[:, hc], ptf[0:META, a, 192:240], start=False, stop=True)
                    else:
                        hc = slice(64 * t, 64 * t + 64)
                        if i < 4:
                            dst = ps[64 * t:64 * t + 64, O_, 0:512]
                            pe.matmul(dst, v_own[:, i, hc], ptf[:, 0, :], start=True, stop=False)
                            if i > 0:
                                pe.matmul(dst, v_prev[:, i - 1, hc], ptf[0:64, 1, :], start=False, stop=False)
                            mm = pe.matmul(dst, v_pm[:, hc], ptm[:, :], start=False, stop=True)
                        else:
                            dst = ps[64 * t:64 * t + 64, O_, 0:192]
                            pe.matmul(dst, vb_c[:, hc], ptf[:, 0, 0:192], start=True, stop=False)
                            pe.matmul(dst, v_new[:, hc], ptf[0:DEC, 1, 0:192], start=False, stop=False)
                            pe.matmul(dst, vb_cm[:, hc], ptm[:, 0:192], start=False, stop=False)
                            mm = pe.matmul(dst, v_pm[:, hc], ptm[:, 192:384], start=False, stop=True)
                    mm.then_inc(pe_done, st.done("pe", f"{br} values {j}"))

                def prep_b(s):
                    if s == 0:
                        pe.wait_ge(act_done, A("act", f"evac {UIDX['vb', 0]} 0 1"))
                        pe.wait_ge(dve_done, A("dve", f"a o {len(jobs) - 1}"))
                        for i in range(4):
                            pe.transpose(ps[:, T0, 128 * i:128 * i + 128], vb[:, 128 * i:128 * i + 128], c_("ident"))
                        for i in range(1, 4):
                            pe.transpose(ps[0:64, T1, 128 * i - 128:128 * i], vb[:, 128 * i - 64:128 * i], c_("ident"))
                        pe.transpose(ps[0:META, M_, 0:128], vb[:, META0:SAMP0], c_("ident"))
                        mm = pe.transpose(ps[0:DEC, M_, 128:256], vb[:, SAMP0:T], c_("ident"))
                        mm.then_inc(pe_done, st.done("pe", "b vtok"))

                for step in order:
                    if step[0] == "dense":
                        dense_unit(step[1])
                    elif step[0] == "norm":
                        norm(step[1])
                    elif step[0] == "mean":
                        mean(step[1])
                    elif step[0] == "gla":
                        gla(step[1], step[2])
                    elif step[0] == "prep_a":
                        prep_a(step[1])
                    elif step[0] == "prep_b":
                        prep_b(step[1])
                    elif step[0] == "att":
                        br, j = step[1], step[2]
                        n = len(JOBS[br])
                        if 1 <= j <= n:
                            turn(br, j - 1)
                        if j >= 2:
                            values(br, j - 2)
                        if j < n:
                            scores(br, j)

            @block.scalar
            def _(act):
                def store(dst, src, e, name):
                    act.wait_ge({"act": act_done, "dve": dve_done}[e], A(e, name))
                    act.dma_start(dst, src).then_inc(stored, 16)
                    count["stored"] += 16

                count = {"stored": 0}

                def w_hi(u):
                    slot = u % WSLOTS
                    if u >= WSLOTS:
                        act.wait_ge(w_loaded[slot], 16 * (u // WSLOTS))
                    act.activation(whi[slot][:, :], wraw[slot][:, :], ACT.Copy).then_inc(act_done, st.done("act", f"w hi {u}"))

                def round_tile(dst, src, wait, name):
                    act.wait_ge(*wait)
                    act.activation(dst, src, ACT.Copy).then_inc(act_done, st.done("act", name))

                def link(ins, name=None):
                    ins.then_inc(act_done, st.done("act", name))
                    act.wait_ge(act_done, st.count["act"])

                def evac(u):
                    kind, n = UNITS[u]
                    if kind.startswith("gate"):
                        act.wait_ge(*sig_free(kind[-1], n))
                        for hf in range(2):
                            s = sig[:, n % 2, H[hf]]
                            act.wait_ge(pe_done, A("pe", f"half {u} 0 {hf}"))
                            link(act.activation(s, dps[bank_of[u, 0, hf]][:, 0:HALF], ACT.Abs))
                            link(act.activation(s, s, ACT.Exp, scale=-1.0))
                            act.activation(s, s, ACT.Ln, bias=1.0).then_inc(act_done, st.done("act", f"gate ln {u} {hf}"))
                            act.wait_ge(dve_done, A("dve", f"evac {u} 0 {hf}"))
                            act.activation(s, s, ACT.Exp).then_inc(act_done, st.done("act", f"sig {u} {hf}"))
                        return
                    if kind == "ff2" and summed(u):
                        for hf in range(2):
                            if n == 24 and hf == 0:
                                act.wait_ge(pe_done, A("pe", f"dense {UIDX['ff2', 23]}"))
                            act.wait_ge(dve_done, A("dve", f"evac {u} 0 {hf}"))
                            square(u, hf, facc[:, n - 24, H[hf]])
                    if evac_engine(kind) != "act":
                        return
                    for hf in range(2):
                        src = dps[bank_of[u, 0, hf]][:, 0:HALF]
                        act.wait_ge(pe_done, A("pe", f"half {u} 0 {hf}"))
                        if kind == "ck":
                            if hf == 0 and n >= 2:
                                act.wait_ge(dve_done, A("dve", f"gla kend {n - 2}"))
                            ins = act.activation(cproj[n % 2][:, 1, H[hf]], src, ACT.Copy)
                        elif kind == "cg":
                            h, i = n // 2, n % 2
                            if hf == 0 and h >= 2:
                                act.wait_ge(dve_done, A("dve", f"gla silu {h - 2}"))
                            ins = act.activation(cproj[h % 2][:, 4 + i, H[hf]], src, ACT.Copy)
                        elif kind == "vb":
                            if hf == 0:
                                act.wait_ge(dve_done, A("dve", f"a o {len(jobs) - 1}"))
                                act.wait_ge(pe_done, A("pe", f"a values {len(jobs) - 1}"))
                            ins = act.activation(vb[:, H[hf]], src, ACT.Copy)
                        elif kind == "out":
                            if hf == 0 and n == 0:
                                act.wait_ge(pe_done, A("pe", f"dense {UIDX['up_c', KD - 1]}"))
                            square(u, hf, src)
                            ins = act.activation(mix[:, n, H[hf]], src, ACT.Copy)
                        elif kind == "ff1":
                            g = n // 8
                            if hf == 0:
                                if g >= 2 and n % 8 == 0:
                                    act.wait_ge(pe_done, A("pe", f"dense {UIDX['ff2', 8 * (g - 2) + 7]}"))
                                if g == 0 and n == 0:
                                    act.wait_ge(dve_done, A("dve", "h raw pre_mlp 7"))
                                    act.wait_ge(pe_done, A("pe", "ms pre_mlp"))
                                if g == 1 and n == 8:
                                    act.wait_ge(pe_done, A("pe", f"dense {UIDX['up_b', 6]}"))
                            ins = act.activation(hid[g % 2][0][:, n % 8, H[hf]], src, ACT.Relu)
                        ins.then_inc(act_done, st.done("act", f"evac {u} 0 {hf}"))

                def after_evac(u):
                    kind, n = UNITS[u]
                    if kind == "ff1":
                        g = n // 8
                        round_tile(hid[g % 2][2][:, n % 8, :], hid[g % 2][0][:, n % 8, :],
                                   (dve_done, A("dve", f"hid {n}")), f"hid hi {n}")

                def square(u, hf, src):
                    which, n = summed(u)
                    if n >= 3:
                        act.wait_ge(dve_done, A("dve", f"sum {which} {n - 2} {hf}"))
                    dst = sqsum if n == 0 else sqpart[n % 2]
                    act.activation(dst[:, H[hf]], src, ACT.Square).then_inc(act_done, st.done("act", f"sq {which} {n} {hf}"))

                def to_rstd(which, pair):
                    act.wait_ge(pe_done, A("pe", f"ms {which}"))
                    link(act.activation(rstd[:, :].rearrange("p (a n) -> p a n", a=2), ps[:, pair, 0:HALF], ACT.Ln,
                                        bias=eps[:, 0:1]))
                    act.activation(rstd[:, :], rstd[:, :], ACT.Exp, scale=-0.5).then_inc(act_done, st.done("act", f"rstd {which}"))

                def norm(which):
                    to_rstd(which, PAIRS[0])

                def ahead_hi(slot):
                    act.wait_ge(w_ahead[slot], 16)
                    act.activation(whi[slot][:, :], wraw[slot][:, :], ACT.Copy).then_inc(act_done, st.done("act", f"ahead hi {slot}"))

                def mean(which):
                    after = "post_mix" if which == "pre_mlp" else "post_mlp"
                    for k in range(KD):
                        e = x_engine(k)
                        act.wait_ge(by_name[e], A(e, f"x {after} {k}"))
                        act.activation(sq[:, k, :], x[:, k, :], ACT.Square).then_inc(act_done, st.done("act", f"sq {which} {k}"))
                        if which == "next" and k in (1, 4):
                            ahead_hi(1 if k == 1 else 0)
                    to_rstd(which, PAIRS[1])
                    if which == "next":
                        act.wait_ge(act_done, st.count["act"])

                def tokens(which):
                    name = "h" if which == "pre_mix" else "h2"
                    if which == "pre_mix":
                        act.dma_start(io["x_spill"], x[:, :, :]).then_inc(spilled, 16)
                    for k in range(KD):
                        round_tile(h_hi[:, k, :], h_raw[:, k, :], (dve_done, A("dve", f"h raw {which} {k}")), f"{name} hi {k}")

                def gla(h, s):
                    pr = cproj[h % 2]
                    if s == "v decay":
                        if h > 0:
                            act.wait_ge(dve_done, A("dve", f"gla state {h - 1}"))
                            act.wait_ge(pe_done, A("pe", f"gla o {h - 1}"))
                            act.wait_ge(pe_done, A("pe", f"gla diag {h - 1} 15"))
                        act.dma_start(state[:, 6, :], io["state"][bass.ds(l * C_HEADS + h, 1), :, :].rearrange("a p n -> (a p) n")).then_inc(state_loaded, 16)
                        act.wait_ge(pe_done, A("pe", f"gla z {h}"))
                        zz = zlog[:, :]
                        link(act.activation(zz.rearrange("p (a n) -> p a n", a=2), ps[:, S0:S1 + 1, 0:HALF], ACT.Identity,
                                            bias=p_("b_alpha", h)), f"gla z {h}")
                        link(act.activation(ztmp[:, :], zz, ACT.Abs))
                        link(act.activation(ztmp[:, :], ztmp[:, :], ACT.Exp, scale=-1.0))
                        act.activation(ztmp[:, :], ztmp[:, :], ACT.Ln, bias=1.0).then_inc(act_done, st.done("act", f"gla ln {h}"))
                    if s.startswith("v diag"):
                        for j in range(4 * int(s[-1]), 4 * int(s[-1]) + 4):
                            e = ediag_of(j)
                            act.wait_ge(pool_done, A("pool", f"gla d {h} {j}"))
                            act.activation(e, e, ACT.Exp, scale=1.0 / 16).then_inc(act_done, st.done("act", f"gla e {h} {j}"))
                    if s == "v vtok":
                        act.wait_ge(spilled, 16)
                        if h > 0:
                            act.wait_ge(pe_done, A("pe", f"gla o {h - 1}"))
                        for g, pair in enumerate(VTOK_PAIRS):
                            act.wait_ge(pe_done, A("pe", f"gla vtok {h} {g}"))
                            if g < 2:
                                act.activation(vtok[:, pair[0]:pair[0] + 2, :], ps[:, VTOK_BANKS[g], :].rearrange("p (c n) -> p c n", c=2),
                                               ACT.Copy).then_inc(act_done, st.done("act"))
                            else:
                                for c, sb in enumerate(pair):
                                    n = SUPER[sb][1]
                                    act.activation(vtok[0:n, sb, :], ps[0:n, T1, 256 * c:256 * c + 256], ACT.Copy
                                                   ).then_inc(act_done, st.done("act", f"gla vtok {h}" if c == 1 else None))
                    if s == "v farq":
                        act.wait_ge(pool_done, A("pool", f"gla far q {h}"))
                        act.activation(qfar[:, :], qfar[:, :], ACT.Exp, scale=1.0 / 16).then_inc(act_done, st.done("act"))
                        act.activation(qfar_s[:, :], qfar_s[:, :], ACT.Exp, scale=1.0 / 16).then_inc(act_done, st.done("act"))
                        act.activation(kfar_s[:, :], kfar_s[:, :], ACT.Exp, scale=1.0 / 16).then_inc(act_done, st.done("act", f"gla far q {h}"))
                    if s == "v far":
                        for i in range(1, 8):
                            act.wait_ge(pool_done, A("pool", f"gla far {h} {i}"))
                            kf = kfar_of(i)
                            act.activation(kf, kf, ACT.Exp, scale=1.0 / 16).then_inc(act_done, st.done("act", f"gla far {h} {i}"))
                    if s == "v kend":
                        act.wait_ge(dve_done, A("dve", f"gla scan {h}"))
                        if h > 0:
                            act.wait_ge(dve_done, A("dve", f"gla state {h - 1}"))
                        act.activation(ebl[:, :], bcum[:, :], ACT.Exp, scale=1.0 / 16).then_inc(act_done, st.done("act", f"gla eb {h}"))
                        act.wait_ge(pool_done, A("pool", f"gla kend {h}"))
                        act.activation(kend[:, :], kend[:, :], ACT.Exp, scale=1.0 / 16).then_inc(act_done, st.done("act", f"gla kend {h}"))
                    if s == "v ktok":
                        for g in range(2):
                            bank = (M_, O_)[g]
                            act.wait_ge(pe_done, A("pe", f"gla ktok {h} {g}"))
                            for i in range(3):
                                n = SUPER[3 * g + i][1]
                                ins = act.activation(ktok[0:n, 3 * g + i, :], ps[0:n, bank, 128 * i:128 * i + 128], ACT.Copy)
                                ins.then_inc(act_done, st.done("act", f"gla ktok {h} {g}" if i == 2 else None))
                    if s == "v silu":
                        act.wait_ge(act_done, A("act", f"evac {UIDX['cg', 2 * h + 1]} 0 1"))
                        if h >= 1:
                            act.wait_ge(dve_done, A("dve", f"gla out {h - 1} 1"))
                        act.activation(gsig[:, :, :], pr[:, 4:6, :], ACT.Exp, scale=-1.0).then_inc(act_done, st.done("act", f"gla gate {h}"))
                    if s == "v o":
                        act.wait_ge(pe_done, A("pe", f"gla o {h}"))
                        act.wait_ge(spilled, 16)
                        if h > 0:
                            act.wait_ge(dve_done, A("dve", f"gla out {h - 1} 1"))
                        act.activation(oh[:, :, 0:SEQ], ps[:, M_::3, :], ACT.Copy).then_inc(act_done, st.done("act"))
                        act.activation(oh[:, :, SEQ:T], ps[:, T1, 0:96].rearrange("p (a n) -> p a n", a=2), ACT.Copy
                                       ).then_inc(act_done, st.done("act", f"gla oevac {h}"))
                        act.wait_ge(act_done, st.count["act"])
                        if h > 0:
                            act.wait_ge(pe_done, A("pe", f"gla ms {h - 1}"))
                        act.activation(gsq[:, :, :], oh[:, :, :], ACT.Square).then_inc(act_done, st.done("act", f"gla sq {h}"))
                    if s == "v out":
                        act.wait_ge(pe_done, A("pe", f"gla ms {h}"))
                        link(act.activation(rstd[:, :].rearrange("p (a n) -> p a n", a=2), ps[:, S0:S1 + 1, 0:HALF], ACT.Ln,
                                            bias=eps[:, 0:1]))
                        act.activation(rstd[:, :], rstd[:, :], ACT.Exp, scale=-0.5).then_inc(act_done, st.done("act", f"gla rstd {h}"))
                        for which, slot in (("p_state", 5), ("s_state", 7)):
                            act.wait_ge(dve_done, A("dve", f"gla state {h}"))
                            act.dma_start(io[which][bass.ds(l * C_HEADS + h, 1), :, :].rearrange("a p n -> (a p) n"), state[:, slot, :]).then_inc(stored, 16)
                            count["stored"] += 16
                        for i in range(2):
                            k = 2 * h + i
                            round_tile(oc_hi[:, k, :], oc_raw[:, k, :], (dve_done, A("dve", f"gla out {h} {i}")), f"oc hi {k}")

                def prep_a(s):
                    if s == 0:
                        for e, name in (("dve", "gla out 3 1"), ("pe", "gla ms 3"), ("pe", "gla o 3")):
                            act.wait_ge({"dve": dve_done, "pe": pe_done}[e], A(e, name))
                        act.wait_ge(stored, 32 * C_HEADS)
                        for dst, name in ((wuk, "w_uk"), (wuv, "w_uv"), (cct, "a_ckv")):
                            act.dma_start(dst[:, :, :], io[name][bass.ds(l, 1)].rearrange("a (k p) n -> p (a k) n", p=P)).then_inc(a_loaded, 16)
                        act.dma_start(kr_c[:, :], io["a_kr"][bass.ds(l, 1)].rearrange("a p n -> (a p) n")).then_inc(a_loaded, 16)
                    if s == 2:
                        store(io["c_out"][bass.ds(l, 1)].rearrange("a (k p) n -> p (a k) n", p=P), ckv[:, :, :], "dve", "c 1")
                        store(io["kr_out"][bass.ds(l, 1)].rearrange("a p n -> (a p) n"), krot[0:32, :], "dve", "krot")
                    if s == 0:
                        act.wait_ge(dve_done, A("dve", f"evac {UIDX['ckv', 1]} 0 1"))
                        act.wait_ge(act_done, A("act", f"oc hi {KD - 1}"))
                        act.wait_ge(pool_done, A("pool", f"oc lo {KD - 1}"))
                        act.activation(cksq[:, :, :], ckv[:, :, :], ACT.Square).then_inc(act_done, st.done("act", "ckv sq"))
                        act.wait_ge(pe_done, A("pe", "prep a 0"))
                        link(act.activation(rstd[:, :].rearrange("p (a n) -> p a n", a=2), ps[:, 0:2, 0:HALF], ACT.Ln,
                                            bias=eps[:, 0:1]), "prep a 0")
                        act.activation(rstd[:, :], rstd[:, :], ACT.Exp, scale=-0.5).then_inc(act_done, st.done("act", "c rstd"))
                    if prep_evac(s) == "act" and s > 0:
                        act.wait_ge(pe_done, A("pe", f"prep a {s}"))
                        pair = PAIRS[s % 2]
                        if s < 8:
                            act.activation(kn[:, s - 4, :].rearrange("p (a n) -> p a n", a=2), ps[:, pair, 0:HALF], ACT.Copy
                                           ).then_inc(act_done, st.done("act", f"prep a {s}"))
                        elif s < 10:
                            act.activation(kn_c[:, 2 * (s - 8):2 * (s - 8) + 2, :], ps[:, pair, 0:CKEYS], ACT.Copy
                                           ).then_inc(act_done, st.done("act", f"prep a {s}"))
                        else:
                            for i, (_, _, n, dst) in enumerate(VA_TILES[s - 10]):
                                act.activation(dst, ps[0:n, pair.start + i, :], ACT.Copy).then_inc(
                                    act_done, st.done("act", f"prep a {s}" if i == len(VA_TILES[s - 10]) - 1 else None))

                def att(br, j):
                    n = len(JOBS[br])
                    if j < n:
                        _, t, i = JOBS[br][j]
                        pb = prob_view(br, j)
                        nk = key_count(br, i)
                        rows = P if i < 4 else MIXED
                        act.wait_ge(dve_done, A("dve", f"{br} shift {j}"))
                        k = 2 if br == "a" else 4
                        w = nk if br == "a" else nk + 1
                        sc = A_SCALE if br == "a" else B_SCALE
                        for a in range(k):
                            act.activation(pb[0:rows, a, 0:w], pb[0:rows, a, 0:w], ACT.Exp, scale=sc,
                                           accum_out=stat[0:rows, j % 2, 8 + a:9 + a]
                                           ).then_inc(act_done, st.done("act", f"{br} exp {j}" if a == k - 1 else None))
                    if br == "a" and j >= 6 and (j - 6) % 5 == 0:
                        t = (j - 6) // 5
                        if t == 0:
                            act.wait_ge(pe_done, A("pe", "prep a 14"))
                            act.wait_ge(stored, 32 * C_HEADS + 32)
                        round_tile(oa_hi[:, t, :], oa_raw[:, t, :], (dve_done, A("dve", f"a o {5 * t + 4}")), f"oa hi {t}")
                    if br == "b" and j == n + 1:
                        for g in range(4):
                            round_tile(ob_hi[:, g, :], ob_raw[:, g, :], (dve_done, A("dve", f"b o {n - 1}")), f"ob hi {g}")

                for step in order:
                    if step[0] == "dense":
                        evac(step[1])
                        after_evac(step[1])
                        if step[1] + 2 < NU:
                            w_hi(step[1] + 2)
                    elif step[0] == "norm":
                        norm(step[1])
                    elif step[0] == "mean":
                        mean(step[1])
                    elif step[0] == "tokens":
                        tokens(step[1])
                    elif step[0] == "gla":
                        gla(step[1], step[2])
                    elif step[0] == "prep_a":
                        prep_a(step[1])
                    elif step[0] == "prep_b":
                        if step[1] == 0:
                            act.wait_ge(pe_done, A("pe", f"a values {len(jobs) - 1}"))
                            for dst, name in ((kb_c, "b_k"), (vb_c, "b_v"), (vb_cm, "b_vm")):
                                act.dma_start(dst[:, :], io[name][bass.ds(l, 1)].rearrange("a p n -> (a p) n")).then_inc(b_loaded, 16)
                            for name, src in (("kw_out", "b_kw"), ("vw_out", "b_vw")):
                                act.dma_start(io[name][bass.ds(l, 1)].rearrange("a p n -> (a p) n")[:, 0:WIN - DEC],
                                               io[src][bass.ds(l, 1)].rearrange("a p n -> (a p) n")[:, DEC:WIN]).then_inc(stored, 16)
                                count["stored"] += 16
                            store(io["kw_out"][bass.ds(l, 1)].rearrange("a p n -> (a p) n")[:, WIN - DEC:WIN], kb[:, SAMP0:T], "dve", f"evac {UIDX['kb', 0]} 0 1")
                            store(io["vw_out"][bass.ds(l, 1)].rearrange("a p n -> (a p) n")[:, WIN - DEC:WIN], vb[:, SAMP0:T], "act", f"evac {UIDX['vb', 0]} 0 1")
                            store(io["kb_out"][bass.ds(l, 1)].rearrange("a p n -> (a p) n"), kb[:, 384:T], "dve", f"evac {UIDX['kb', 0]} 0 1")
                            store(io["vb_out"][bass.ds(l, 1)].rearrange("a p n -> (a p) n"), vb[:, 384:T], "act", f"evac {UIDX['vb', 0]} 0 1")
                        if step[1] == 1:
                            act.wait_ge(pe_done, A("pe", "b vtok"))
                            act.activation(v_own[:, :, :].rearrange("p a n -> p (a n)"), ps[:, T0, :], ACT.Copy).then_inc(act_done, st.done("act", "b vtok"))
                    elif step[0] == "att":
                        att(step[1], step[2])
                    elif step[0] == "split_y":
                        act.wait_ge(pe_done, A("pe", f"dense {UIDX['gate_b', 7]}"))
                        for k in Y_SPLIT[step[1]]:
                            e = y_engine("b", k)
                            round_tile(h_hi[:, k, :], y[:, k, :], (by_name[e], A(e, f"y b {k}")), f"y hi {k}")
                        if step[1] == 1:
                            act.wait_ge(pool_done, A("pool", f"y lo {KD - 2}"))
                            act.wait_ge(dve_done, A("dve", f"y lo {KD - 1}"))
                            act.wait_ge(spilled, 16)
                            act.dma_start(x[:, :, :], io["x_spill"]).then_inc(x_back, 16)

                act.wait_ge(stored, count["stored"])

            @block.vector
            def _(dve):
                def link(ins, name=None):
                    ins.then_inc(dve_done, st.done("dve", name))
                    dve.wait_ge(dve_done, st.count["dve"])

                def add_square(u, hf):
                    which, n = summed(u)
                    dve.wait_ge(act_done, A("act", f"sq {which} {n} {hf}"))
                    if n >= 2:
                        dve.wait_ge(dve_done, A("dve", f"sum {which} {n - 1} {hf}"))
                    if n >= 1:
                        dve.tensor_tensor(sqsum[:, H[hf]], sqsum[:, H[hf]], sqpart[n % 2][:, H[hf]], ALU.add
                                          ).then_inc(dve_done, st.done("dve", f"sum {which} {n} {hf}"))

                def evac(u):
                    kind, n = UNITS[u]
                    if kind == "out":
                        for hf in range(2):
                            add_square(u, hf)
                    if kind == "ff1":
                        t = hid[n // 8 % 2][0][:, n % 8, :]
                        dve.wait_ge(act_done, A("act", f"evac {u} 0 1"))
                        dve.tensor_tensor(t, t, t, ALU.mult).then_inc(dve_done, st.done("dve", f"hid {n}"))
                    if evac_engine(kind) != "dve":
                        return
                    for o in range(outs_of(kind)[0]):
                        for hf in range(2):
                            src = dps[bank_of[u, o, hf]][:, 0:HALF]
                            dve.wait_ge(pe_done, A("pe", f"half {u} {o} {hf}"))
                            c = H[hf]
                            if kind.startswith("gate"):
                                dve.wait_ge(act_done, A("act", f"gate ln {u} {hf}"))
                                s = sig[:, n % 2, c]
                                ins = dve.scalar_tensor_tensor(s, src, 0.0, s, ALU.min, ALU.subtract)
                            elif kind == "kralr":
                                ins = dve.tensor_copy(kra[0:112, c], src[0:112, :])
                            elif kind == "cq":
                                if hf == 0 and n >= 2:
                                    dve.wait_ge(dve_done, A("dve", f"gla qe {n - 2}"))
                                ins = dve.tensor_scalar(cproj[n % 2][:, 0, c], src, float(C_DK ** -0.5), None, ALU.mult)
                            elif kind == "cv":
                                h, i = n // 2, n % 2
                                if hf == 0 and h >= 2:
                                    dve.wait_ge(pe_done, A("pe", f"gla vtok {h - 2} 2"))
                                ins = dve.tensor_copy(cproj[h % 2][:, 2 + i, c], src)
                            elif kind in ("ckv", "qr", "qn"):
                                if hf == 0:
                                    dve.wait_ge(pe_done, A("pe", f"gla ms {C_HEADS - 1 if kind == 'qr' else C_HEADS - 2}"))
                                dst = {"ckv": ckv, "qr": qr, "qn": qn}[kind]
                                ins = dve.tensor_copy(dst[:, n, c], src)
                            elif kind == "kb":
                                if hf == 0:
                                    dve.wait_ge(pe_done, A("pe", f"a values {len(jobs) - 1}"))
                                    dve.wait_ge(stored, 32 * C_HEADS + 32)
                                ins = dve.tensor_copy(kb[:, c], src)
                            elif kind == "qb":
                                ins = dve.tensor_copy(qb[:, n, c], src)
                            elif kind == "up_c":
                                if n == 0 and hf == 0:
                                    dve.wait_ge(pe_done, A("pe", f"gla ms {C_HEADS - 1}"))
                                dve.wait_ge(act_done, A("act", f"sig {u - 1} {hf}"))
                                ins = dve.tensor_tensor(y[:, n, c], sig[:, n % 2, c], src, ALU.mult)
                            elif kind in ("up_a", "up_b"):
                                dve.wait_ge(act_done, A("act", f"sig {UIDX['gate_' + kind[-1], n + o]} {hf}"))
                                ins = dve.tensor_tensor(sig[:, o, c], sig[:, o, c], src, ALU.mult)
                            elif kind == "ff2":
                                g, m = n // 8, n % 8
                                if g == 0:
                                    if m == 0 and hf == 0:
                                        dve.wait_ge(stored, 32 * C_HEADS + 32 + 96)
                                    ins = dve.tensor_copy(facc[:, m, c], src)
                                else:
                                    if hf == 0:
                                        dve.wait_ge(dve_done, A("dve", f"evac {UIDX['ff2', n - 8]} 0 1"))
                                    ins = dve.tensor_tensor(facc[:, m, c], facc[:, m, c], src, ALU.add)
                            ins.then_inc(dve_done, st.done("dve", f"evac {u} {o} {hf}"))
                            if summed(u):
                                add_square(u, hf)
                        if kind in ("up_a", "up_b") and y_engine(kind[-1], n + o) == "dve":
                            dve.wait_ge(dve_done, A("dve", f"evac {u} {o} 1"))
                            dve.wait_ge(pool_done, A("pool", f"y a {n + o}"))
                            dve.tensor_tensor(y[:, n + o, :], y[:, n + o, :], sig[:, o, :], ALU.add
                                              ).then_inc(dve_done, st.done("dve", f"y b {n + o}"))

                def norm(which):
                    src = norm_src[which]
                    dve.wait_ge(act_done, A("act", f"rstd {which}"))
                    if which == "post_mix":
                        dve.wait_ge(x_back, 16)
                        for hf in range(2):
                            dve.wait_ge(act_done, A("act", f"evac {UIDX['out', 7]} 0 {hf}"))
                    for k in range(KD):
                        t = src[:, k, :]
                        dve.scalar_tensor_tensor(t, t, p_("g_" + which, k), rstd[:, :], ALU.mult, ALU.mult
                                                 ).then_inc(dve_done, st.done("dve", f"nrm {which} {k}"))
                        if x_engine(k) == "dve":
                            dve.wait_ge(dve_done, A("dve", f"nrm {which} {k}"))
                            dve.tensor_tensor(x[:, k, :], x[:, k, :], t, ALU.add).then_inc(dve_done, st.done("dve", f"x {which} {k}"))

                def mean(which):
                    pass

                def tokens(which):
                    name = "h" if which == "pre_mix" else "h2"
                    if which == "pre_mlp":
                        dve.wait_ge(act_done, A("act", f"rstd {which}"))
                        dve.wait_ge(pe_done, A("pe", f"dense {UIDX['out', KD - 1]}"))
                    def lo(k):
                        dve.wait_ge(act_done, A("act", f"{name} hi {k}"))
                        dve.tensor_tensor(h_lo[:, k, :], h_raw[:, k, :], h_hi[:, k, :].bitcast(F32), ALU.subtract
                                          ).then_inc(dve_done, st.done("dve", f"{name} lo {k}"))
                    for k in range(KD):
                        g = g_pre_mix[:, k:k + 1] if which == "pre_mix" else p_("g_" + which, k)
                        if which == "pre_mlp":
                            e = x_engine(k)
                            dve.wait_ge(by_name[e], A(e, f"x post_mix {k}"))
                        dve.scalar_tensor_tensor(h_raw[:, k, :], x[:, k, :], g, rstd[:, :], ALU.mult, ALU.mult
                                                 ).then_inc(dve_done, st.done("dve", f"h raw {which} {k}"))
                        if lo_engine(k - 1) == "dve" and k > 0:
                            lo(k - 1)
                    lo(KD - 1)

                def sb_view(t, a, n):
                    return t[:, a:a + n]

                def gla(h, s):
                    pr = cproj[h % 2]
                    q, kk = pr[:, 0, :], pr[:, 1, :]
                    q3 = q.rearrange("p (b t) -> p b t", t=BLK)
                    k3 = kk.rearrange("p (b t) -> p b t", t=BLK)
                    if s == "v decay":
                        dve.wait_ge(act_done, A("act", f"gla ln {h}"))
                        if h > 0:
                            dve.wait_ge(act_done, A("act", f"gla eb {h - 1}"))
                            dve.wait_ge(pool_done, A("pool", f"gla kend {h - 1}"))
                        link(dve.scalar_tensor_tensor(lsig[:, :], zlog[:, :], 0.0, ztmp[:, :], ALU.min, ALU.subtract), f"gla lg {h}")
                        for a, n in SUPER:
                            dve.tensor_tensor_scan(bcum[:, a:a + n], c_("ones")[:, 0:n], lsig[:, a:a + n], 0.0, ALU.mult, ALU.add
                                                   ).then_inc(dve_done, st.done("dve", f"gla scan {h}" if a == SAMP0 else None))
                    if s.startswith("v diag"):
                        for j in range(4 * int(s[-1]), 4 * int(s[-1]) + 4):
                            w = BLK - j
                            e = ediag_of(j).rearrange("p (b t) -> p b t", t=w)
                            dve.wait_ge(act_done, A("act", f"gla e {h} {j}"))
                            if j == 0:
                                dve.wait_ge(act_done, A("act", f"evac {UIDX['ck', h]} 0 1"))
                            link(dve.tensor_tensor(e, e, k3[:, :, j:j + 1].to_broadcast([P, NBLK, w]), ALU.mult))
                            dve.tensor_tensor(e, e, q3[:, :, j:], ALU.mult).then_inc(dve_done, st.done("dve", f"gla e {h} {j}"))
                    if s == "v farq":
                        dve.wait_ge(act_done, A("act", f"gla far q {h}"))
                        qf = qfar[:, :].rearrange("p (b i t) -> p b i t", b=4, t=BLK)
                        q4 = q[:, 0:SEQ].rearrange("p (b i t) -> p b i t", b=4, t=BLK)[:, :, 1:, :]
                        dve.tensor_tensor(qf, qf, q4, ALU.mult).then_inc(dve_done, st.done("dve"))
                        dve.tensor_tensor(qfar_s[:, :], qfar_s[:, :], q[:, SAMP0 + BLK:T], ALU.mult).then_inc(dve_done, st.done("dve"))
                        dve.tensor_tensor(kfar_s[:, :], kfar_s[:, :], kk[:, SAMP0:SAMP0 + BLK], ALU.mult).then_inc(dve_done, st.done("dve", f"gla far s {h}"))
                    if s == "v far":
                        for i in range(1, 8):
                            dve.wait_ge(act_done, A("act", f"gla far {h} {i}"))
                            kf = kfar_of(i).rearrange("p (b s) -> p b s", b=4)
                            k4 = kk[:, 0:SEQ].rearrange("p (b s) -> p b s", b=4)[:, :, 0:16 * i]
                            dve.tensor_tensor(kf, kf, k4, ALU.mult).then_inc(dve_done, st.done("dve", f"gla far {h} {i}"))
                    if s == "v kend":
                        dve.wait_ge(act_done, A("act", f"gla kend {h}"))
                        dve.tensor_tensor(kend[:, :], kend[:, :], kk, ALU.mult).then_inc(dve_done, st.done("dve", f"gla kend {h}"))
                        dve.wait_ge(act_done, A("act", f"gla eb {h}"))
                        if h > 0:
                            dve.wait_ge(pe_done, A("pe", f"gla o {h - 1}"))
                        else:
                            dve.wait_ge(spilled, 16)
                        dve.tensor_tensor(qe[:, :], ebl[:, :], q, ALU.mult).then_inc(dve_done, st.done("dve", f"gla qe {h}"))
                    if s == "v amat":
                        if h > 0:
                            dve.wait_ge(pe_done, A("pe", f"gla o {h - 1}"))
                        dve.wait_ge(pe_done, A("pe", f"gla diag {h} 15"))
                        dve.wait_ge(pe_done, A("pe", f"gla far {h} 7"))
                        am = amat[:, 0:SEQ].rearrange("p (b t) -> p b t", b=4)
                        bm = c_("blockmask").rearrange("p (a t) -> p a t", a=1).to_broadcast([P, 4, 128])
                        dve.tensor_tensor(am, ps[:, S0, :].rearrange("p (b t) -> p b t", b=4), bm, ALU.mult).then_inc(dve_done, st.done("dve"))
                        dve.tensor_copy(amat[0:META, META0:SAMP0], ps[0:META, S1, 0:META]).then_inc(dve_done, st.done("dve"))
                        link(dve.tensor_tensor(amat[0:DEC, SAMP0:T], ps[0:DEC, S1, META:48], c_("blockmask", DEC)[:, 0:DEC], ALU.mult))
                        dve.tensor_tensor(amat[:, 0:SEQ], amat[:, 0:SEQ], ps[:, T0, :], ALU.add).then_inc(dve_done, st.done("dve"))
                        dve.tensor_tensor(amat[0:DEC, SAMP0:T], amat[0:DEC, SAMP0:T], ps[0:DEC, T1, 0:DEC], ALU.add
                                          ).then_inc(dve_done, st.done("dve", f"gla amat {h}"))
                    if s == "v silu":
                        dve.wait_ge(act_done, A("act", f"gla gate {h}"))
                        link(dve.tensor_scalar(gsig[:, :, :], gsig[:, :, :], 1.0, None, ALU.add))
                        link(dve.reciprocal(gsig[:, :, :], gsig[:, :, :]))
                        dve.tensor_tensor(gsig[:, :, :], gsig[:, :, :], pr[:, 4:6, :], ALU.mult).then_inc(dve_done, st.done("dve", f"gla silu {h}"))
                    if s == "v state":
                        dve.wait_ge(pe_done, A("pe", f"gla kv {h}"))
                        dve.wait_ge(pool_done, A("pool", "gla zero"))
                        dve.wait_ge(state_loaded, 16 * (h + 1))
                        if h > 0:
                            dve.wait_ge(stored, 32 * h)
                        for sb in range(6):
                            a, n = SUPER[sb]
                            bank = (S0, S1, T0)[sb // 2]
                            kv = ps[:, bank, 256 * (sb % 2):256 * (sb % 2) + 256]
                            link(dve.scalar_tensor_tensor(state[:, STATE_OUT[sb], :], state[:, STATE_IN[sb], :],
                                                          ebl[:, a + n - 1:a + n], kv, ALU.mult, ALU.add),
                                 f"gla state {h}" if sb == 5 else None)
                    if s == "v out":
                        dve.wait_ge(act_done, A("act", f"gla rstd {h}"))
                        for i in range(2):
                            link(dve.scalar_tensor_tensor(oh[:, i, :], oh[:, i, :], p_("g_gla", i), rstd[:, :], ALU.mult, ALU.mult))
                            dve.tensor_tensor(oc_raw[:, 2 * h + i, :], oh[:, i, :], gsig[:, i, :], ALU.mult
                                              ).then_inc(dve_done, st.done("dve", f"gla out {h} {i}"))

                def rotate(dst, raw, pair, rows, name, last):
                    c2 = c_("cos", rows).rearrange("p (a n) -> p a n", a=2)
                    s2 = c_("sin", rows).rearrange("p (a n) -> p a n", a=2)
                    t = rtmp[0:rows, :].rearrange("p (a n) -> p a n", a=2)
                    dve.tensor_tensor(dst.rearrange("p (a n) -> p a n", a=2), raw.rearrange("p (a n) -> p a n", a=2), c2, ALU.mult).then_inc(dve_done, st.done("dve"))
                    dve.tensor_tensor(t, ps[0:rows, pair, 0:HALF], s2, ALU.mult).then_inc(dve_done, st.done("dve", name))
                    dve.wait_ge(dve_done, st.count["dve"])
                    link(dve.tensor_tensor(dst, dst, rtmp[0:rows, :], ALU.add), last)

                def prep_a(s):
                    if s == 1:
                        dve.wait_ge(act_done, A("act", "c rstd"))
                        for k in range(KL):
                            dve.scalar_tensor_tensor(ckv[:, k, :], ckv[:, k, :], p_("g_kv", k), rstd[:, :], ALU.mult, ALU.mult
                                                     ).then_inc(dve_done, st.done("dve", f"c {k}"))
                        dve.wait_ge(pe_done, A("pe", "prep a 1"))
                        rotate(krot[0:96, :], kra[0:96, :], PAIRS[1], 96, "prep a 1", None)
                        dve.tensor_copy(krot[96:128, :], krot[0:32, :]).then_inc(dve_done, st.done("dve", "krot"))
                    if s in (2, 3):
                        dve.wait_ge(pe_done, A("pe", f"prep a {s}"))
                        rotate(qrot[:, s - 2, :], qr[:, s - 2, :], PAIRS[s % 2], P, f"prep a {s}", f"qrot {s - 2}")
                    if s >= 4 and prep_evac(s) == "dve":
                        pair = PAIRS[s % 2]
                        dve.wait_ge(pe_done, A("pe", f"prep a {s}"))
                        if s < 8:
                            dve.tensor_copy(kn[:, s - 4, :].rearrange("p (a n) -> p a n", a=2), ps[:, pair, 0:HALF]
                                            ).then_inc(dve_done, st.done("dve", f"prep a {s}"))
                        elif s < 10:
                            dve.tensor_copy(kn_c[:, 2 * (s - 8):2 * (s - 8) + 2, :], ps[:, pair, 0:CKEYS]
                                            ).then_inc(dve_done, st.done("dve", f"prep a {s}"))
                        else:
                            for i, (_, _, n, dst) in enumerate(VA_TILES[s - 10]):
                                dve.tensor_copy(dst, ps[0:n, pair.start + i, :]).then_inc(dve_done, st.done("dve", f"prep a {s}" if i == len(VA_TILES[s - 10]) - 1 else None))

                def att(br, j):
                    n = len(JOBS[br])
                    if j < n:
                        _, t, i = JOBS[br][j]
                        pb = prob_view(br, j)
                        nk = key_count(br, i)
                        k = 2 if br == "a" else 4
                        rows = P if i < 4 else MIXED
                        sm = stat[0:rows, j % 2, :]
                        dve.wait_ge(pe_done, A("pe", f"{br} scores {j}"))
                        if j >= 2:
                            dve.wait_ge(pe_done, A("pe", f"{br} turn {j - 2}"))
                            dve.wait_ge(pool_done, A("pool", f"{br} prob {j - 2}"))
                        elif br == "b":
                            dve.wait_ge(pe_done, A("pe", f"a turn {len(jobs) - 1}"))
                        elif j == 0:
                            pass
                        if br == "a" and i < 3:
                            link(dve.tensor_reduce(sm[:, 4:6], ps[:, S0:S1 + 1, 0:nk], AX.X, ALU.max))
                            mx = sm[:, 4:6].rearrange("p (a n) -> p a n", n=1)
                            dve.tensor_tensor(pb[:, :, :], ps[:, S0:S1 + 1, 0:nk], mx.to_broadcast([P, 2, nk]), ALU.subtract
                                              ).then_inc(dve_done, st.done("dve", f"a shift {j}"))
                        elif br == "a" and i == 3:
                            nf = nk - META
                            mt = ps[0:rows, M_, 0:32].rearrange("p (a n) -> p a n", a=2)
                            dve.tensor_reduce(sm[:, 0:2], ps[:, S0:S1 + 1, 0:nf], AX.X, ALU.max).then_inc(dve_done, st.done("dve"))
                            link(dve.tensor_reduce(sm[:, 2:4], mt, AX.X, ALU.max))
                            link(dve.tensor_tensor(sm[:, 4:6], sm[:, 0:2], sm[:, 2:4], ALU.max))
                            mx = sm[:, 4:6].rearrange("p (a n) -> p a n", n=1)
                            dve.tensor_tensor(pb[:, :, 0:nf], ps[:, S0:S1 + 1, 0:nf], mx.to_broadcast([P, 2, nf]), ALU.subtract).then_inc(dve_done, st.done("dve"))
                            dve.tensor_tensor(pb[:, :, nf:nk], mt, mx.to_broadcast([P, 2, META]), ALU.subtract
                                              ).then_inc(dve_done, st.done("dve", f"a shift {j}"))
                        elif br == "a":
                            ms = c_("mask_s", MIXED).rearrange("p (a n) -> p a n", a=1).to_broadcast([MIXED, 2, 320])
                            link(dve.tensor_tensor(pb[0:rows, :, :], ps[0:rows, S0:S1 + 1, 0:320], ms, ALU.add))
                            link(dve.tensor_reduce(sm[:, 4:6], pb[0:rows, :, :], AX.X, ALU.max))
                            mx = sm[:, 4:6].rearrange("p (a n) -> p a n", n=1)
                            dve.tensor_tensor(pb[0:rows, :, :], pb[0:rows, :, :], mx.to_broadcast([rows, 2, 320]), ALU.subtract
                                              ).then_inc(dve_done, st.done("dve", f"a shift {j}"))
                        else:
                            for g in range(4):
                                if i < 4:
                                    src = ps[:, S0 + g // 2, 208 * (g % 2) + 208 - nk:208 * (g % 2) + 208]
                                    dist = c_("dist")[:, 208 - nk:208]
                                else:
                                    src = ps[0:rows, S0 + g // 2, 192 * (g % 2):192 * (g % 2) + 192]
                                    dist = c_("dist_s", rows)
                                slope = 2.0 ** -(4 * t + g + 1)
                                dve.scalar_tensor_tensor(pb[0:rows, g, 0:nk], dist, -slope / B_SCALE, src, ALU.mult, ALU.add
                                                         ).then_inc(dve_done, st.done("dve", f"b bias {j}" if g == 3 else None))
                            link(dve.tensor_scalar(pb[0:rows, :, nk], p_("sinks", 4 * t, 4, rows), 1.0 / B_SCALE, None, ALU.mult))
                            link(dve.tensor_reduce(sm[:, 4:8], pb[0:rows, :, :], AX.X, ALU.max))
                            mx = sm[:, 4:8].rearrange("p (a n) -> p a n", n=1)
                            dve.tensor_tensor(pb[0:rows, :, :], pb[0:rows, :, :], mx.to_broadcast([rows, 4, nk + 1]), ALU.subtract
                                              ).then_inc(dve_done, st.done("dve", f"b shift {j}"))
                    if 1 <= j <= n:
                        jj = j - 1
                        _, t, i = JOBS[br][jj]
                        if jj >= 1:
                            dve.wait_ge(pe_done, A("pe", f"{br} values {jj - 1}"))
                        dve.wait_ge(pe_done, A("pe", f"{br} turn {jj}"))
                        if br == "a":
                            if i < 4:
                                nf = 128 * (i + 1)
                                dve.tensor_copy(ptf[:, :, 0:nf], ps[:, T0:T1 + 1, 0:nf]).then_inc(dve_done, st.done("dve"))
                                dve.tensor_copy(ptm[:, 0:256], ps[0:META, O_, 256:512]).then_inc(dve_done, st.done("dve", f"a turned {jj}"))
                            else:
                                dve.tensor_copy(ptf[:, :, 0:96], ps[:, T0:T1 + 1, 0:96]).then_inc(dve_done, st.done("dve"))
                                dve.tensor_copy(ptf[0:DEC, :, 96:144], ps[0:DEC, T0:T1 + 1, 96:144]).then_inc(dve_done, st.done("dve"))
                                dve.tensor_copy(ptf[0:META, :, 144:240], ps[0:META, T0:T1 + 1, 144:240]).then_inc(dve_done, st.done("dve", f"a turned {jj}"))
                        elif i < 4:
                            dve.tensor_copy(ptf[:, 0, :], ps[:, T0, :]).then_inc(dve_done, st.done("dve"))
                            if i > 0:
                                dve.tensor_copy(ptf[0:64, 1, :], ps[0:64, T1, :]).then_inc(dve_done, st.done("dve"))
                            dve.tensor_copy(ptm[:, :], ps[0:META, M_, :]).then_inc(dve_done, st.done("dve", f"b turned {jj}"))
                        else:
                            dve.tensor_copy(ptf[:, 0, 0:192], ps[:, T0, 0:192]).then_inc(dve_done, st.done("dve"))
                            dve.tensor_copy(ptf[0:DEC, 1, 0:192], ps[0:DEC, T1, 0:192]).then_inc(dve_done, st.done("dve"))
                            dve.tensor_copy(ptm[:, 0:384], ps[0:META, M_, 0:384]).then_inc(dve_done, st.done("dve", f"b turned {jj}"))
                    if j >= 2:
                        jj = j - 2
                        _, t, i = JOBS[br][jj]
                        dve.wait_ge(pe_done, A("pe", f"{br} values {jj}"))
                        qc = slice(128 * i, 128 * i + 128) if i < 4 else slice(META0, T)
                        w = 128 if i < 4 else MIXED
                        if br == "a":
                            dve.tensor_copy(oa_raw[:, t, qc], ps[:, O_, 0:w]).then_inc(dve_done, st.done("dve", f"a o {jj}"))
                        else:
                            r = slice(64 * t, 64 * t + 64)
                            dve.tensor_copy(ob_raw[r, :, qc], ps[r, O_, 0:4 * w].rearrange("p (g n) -> p g n", g=4)
                                            ).then_inc(dve_done, st.done("dve", f"b o {jj}"))
                    if j < n:
                        k = 2 if br == "a" else 4
                        sm = stat[0:P if JOBS[br][j][2] < 4 else MIXED, j % 2, :]
                        dve.wait_ge(act_done, A("act", f"{br} exp {j}"))
                        dve.reciprocal(sm[:, 12:12 + k], sm[:, 8:8 + k]).then_inc(dve_done, st.done("dve", f"{br} rsum {j}"))

                for step in order:
                    if step[0] == "dense":
                        evac(step[1])
                    elif step[0] == "norm":
                        norm(step[1])
                    elif step[0] == "mean":
                        mean(step[1])
                    elif step[0] == "tokens":
                        tokens(step[1])
                    elif step[0] == "gla":
                        gla(step[1], step[2])
                    elif step[0] == "prep_a":
                        prep_a(step[1])
                    elif step[0] == "prep_b":
                        if step[1] == 1:
                            dve.wait_ge(pe_done, A("pe", "b vtok"))
                            dve.tensor_copy(v_prev[:, :, :].rearrange("p a n -> p (a n)"), ps[0:64, T1, 0:384]).then_inc(dve_done, st.done("dve"))
                            dve.tensor_copy(v_pm[:, :], ps[0:META, M_, 0:128]).then_inc(dve_done, st.done("dve"))
                            dve.tensor_copy(v_new[:, :], ps[0:DEC, M_, 128:256]).then_inc(dve_done, st.done("dve", "b vtok"))
                    elif step[0] == "att":
                        att(step[1], step[2])
                    elif step[0] == "split_y":
                        for k in Y_SPLIT[step[1]]:
                            if lo_engine(k) == "dve":
                                dve.wait_ge(act_done, A("act", f"y hi {k}"))
                                dve.tensor_tensor(h_lo[:, k, :], y[:, k, :], h_hi[:, k, :].bitcast(F32), ALU.subtract
                                                  ).then_inc(dve_done, st.done("dve", f"y lo {k}"))

            @block.gpsimd
            def _(pool):
                def link(ins, name=None):
                    ins.then_inc(pool_done, st.done("pool", name))
                    pool.wait_ge(pool_done, st.count["pool"])

                def w_lo(u):
                    slot = u % WSLOTS
                    pool.wait_ge(act_done, A("act", f"w hi {u}"))
                    pool.tensor_tensor(wlo[slot][:, :], wraw[slot][:, :], whi[slot][:, :].bitcast(F32), ALU.subtract
                                       ).then_inc(pool_done, st.done("pool", f"w lo {u}"))

                def lo_tile(lo, raw, hi, name, hname):
                    pool.wait_ge(act_done, A("act", hname))
                    pool.tensor_tensor(lo, raw, hi.bitcast(F32), ALU.subtract).then_inc(pool_done, st.done("pool", name))

                def evac(u):
                    kind, n = UNITS[u]
                    if kind == "ff1":
                        s = hid[n // 8 % 2]
                        lo_tile(s[1][:, n % 8, :], s[0][:, n % 8, :], s[2][:, n % 8, :], f"hid lo {n}", f"hid hi {n}")
                    if kind in ("up_a", "up_b"):
                        for o in range(2):
                            if y_engine(kind[-1], n + o) != "pool":
                                continue
                            pool.wait_ge(dve_done, A("dve", f"evac {u} {o} 1"))
                            pool.tensor_tensor(y[:, n + o, :], y[:, n + o, :], sig[:, o, :], ALU.add
                                               ).then_inc(pool_done, st.done("pool", f"y {kind[-1]} {n + o}"))

                def norm(which):
                    for k in range(KD):
                        if x_engine(k) == "pool":
                            pool.wait_ge(dve_done, A("dve", f"nrm {which} {k}"))
                            if k == 1 and which == "post_mix":
                                pool.wait_ge(x_back, 16)
                            pool.tensor_tensor(x[:, k, :], x[:, k, :], norm_src[which][:, k, :], ALU.add
                                               ).then_inc(pool_done, st.done("pool", f"x {which} {k}"))

                def mean(which):
                    if which == "next":
                        for slot in (1, 0):
                            lo_tile(wlo[slot][:, :], wraw[slot][:, :], whi[slot][:, :], f"ahead lo {slot}", f"ahead hi {slot}")
                        pool.wait_ge(pool_done, st.count["pool"])

                def gla(h, s):
                    b3 = bcum[:, :].rearrange("p (b t) -> p b t", t=BLK)
                    if s == "v decay":
                        if h > 0:
                            pool.wait_ge(dve_done, A("dve", f"gla state {h - 1}"))
                            pool.wait_ge(pe_done, A("pe", f"gla o {h - 1}"))
                        if h == 0:
                            link(pool.memset(state[:, 0, :], 0.0), "gla zero")
                    if s.startswith("v diag"):
                        for j in range(4 * int(s[-1]), 4 * int(s[-1]) + 4):
                            w = BLK - j
                            e = ediag_of(j).rearrange("p (b t) -> p b t", t=w)
                            if j == 0:
                                pool.wait_ge(dve_done, A("dve", f"gla scan {h}"))
                            pool.tensor_tensor(e, b3[:, :, j:], b3[:, :, j:j + 1].to_broadcast([P, NBLK, w]), ALU.subtract
                                               ).then_inc(pool_done, st.done("pool", f"gla d {h} {j}"))
                    if s == "v farq":
                        if h > 0:
                            pool.wait_ge(pe_done, A("pe", f"gla far {h - 1} 7"))
                        b4 = bcum[:, 0:SEQ].rearrange("p (b i t) -> p b i t", b=4, t=BLK)
                        qf = qfar[:, :].rearrange("p (b i t) -> p b i t", b=4, t=BLK)
                        for b in range(4):
                            pool.tensor_tensor(qf[:, b], b4[:, b, 1:, :], b4[:, b, 0:7, 15:16].to_broadcast([P, 7, BLK]), ALU.subtract
                                               ).then_inc(pool_done, st.done("pool"))
                        ref = bcum[:, SAMP0 + 15:SAMP0 + 16].to_broadcast([P, BLK])
                        pool.tensor_tensor(qfar_s[:, :], bcum[:, SAMP0 + BLK:T], ref, ALU.subtract).then_inc(pool_done, st.done("pool"))
                        pool.tensor_tensor(kfar_s[:, :], ref, bcum[:, SAMP0:SAMP0 + BLK], ALU.subtract).then_inc(pool_done, st.done("pool", f"gla far q {h}"))
                    if s == "v far":
                        b4 = bcum[:, 0:SEQ].rearrange("p (b s) -> p b s", b=4)
                        for i in range(1, 8):
                            kf = kfar_of(i).rearrange("p (b s) -> p b s", b=4)
                            pool.tensor_tensor(kf, b4[:, :, 16 * i - 1:16 * i].to_broadcast([P, 4, 16 * i]), b4[:, :, 0:16 * i], ALU.subtract
                                               ).then_inc(pool_done, st.done("pool", f"gla far {h} {i}"))
                    if s == "v kend":
                        pool.wait_ge(dve_done, A("dve", f"gla lg {h}"))
                        if h > 0:
                            pool.wait_ge(pe_done, A("pe", f"gla ktok {h - 1} 1"))
                        for i, (a, n) in enumerate(SUPER):
                            pool.tensor_tensor(kend[:, a:a + n], bcum[:, a + n - 1:a + n].to_broadcast([P, n]), bcum[:, a:a + n], ALU.subtract
                                               ).then_inc(pool_done, st.done("pool", f"gla kend {h}" if i == 5 else None))
                    if s == "v out":
                        for i in range(2):
                            k = 2 * h + i
                            lo_tile(oc_lo[:, k, :], oc_raw[:, k, :], oc_hi[:, k, :], f"oc lo {k}", f"oc hi {k}")

                def att(br, j):
                    n = len(JOBS[br])
                    if j < n:
                        _, t, i = JOBS[br][j]
                        pb = prob_view(br, j)
                        k = 2 if br == "a" else 4
                        rows = P if i < 4 else MIXED
                        w = pb.shape[2]
                        pool.wait_ge(dve_done, A("dve", f"{br} rsum {j}"))
                        rs = stat[0:rows, j % 2, 12:12 + k].rearrange("p (a n) -> p a n", n=1).to_broadcast([rows, k, w])
                        pool.tensor_tensor(pb[0:rows, :, :], pb[0:rows, :, :], rs, ALU.mult).then_inc(pool_done, st.done("pool", f"{br} prob {j}"))
                    if br == "a" and j >= 6 and (j - 6) % 5 == 0:
                        t = (j - 6) // 5
                        lo_tile(oa_lo[:, t, :], oa_raw[:, t, :], oa_hi[:, t, :], f"oa lo {t}", f"oa hi {t}")
                    if br == "b" and j == n + 1:
                        for g in range(4):
                            lo_tile(ob_lo[:, g, :], ob_raw[:, g, :], ob_hi[:, g, :], f"ob lo {g}", f"ob hi {g}")

                for step in order:
                    if step[0] == "dense":
                        evac(step[1])
                        if step[1] + 2 < NU:
                            w_lo(step[1] + 2)
                    elif step[0] == "norm":
                        norm(step[1])
                    elif step[0] == "mean":
                        mean(step[1])
                    elif step[0] == "tokens":
                        name = "h" if step[1] == "pre_mix" else "h2"
                        for k in range(KD):
                            if lo_engine(k) == "pool":
                                lo_tile(h_lo[:, k, :], h_raw[:, k, :], h_hi[:, k, :], f"{name} lo {k}", f"{name} hi {k}")
                    elif step[0] == "gla":
                        gla(step[1], step[2])
                    elif step[0] == "att":
                        att(step[1], step[2])
                    elif step[0] == "split_y":
                        for k in Y_SPLIT[step[1]]:
                            if lo_engine(k) == "pool":
                                lo_tile(h_lo[:, k, :], y[:, k, :], h_hi[:, k, :], f"y lo {k}", f"y hi {k}")
        with nc.Fori(0, DEPTH) as l:
            with nc.Block() as block:
                layer(l, block)
            for s_ in block_sems:
                nc.sync.sem_clear(s_)
            nc.all_engine_barrier()

        with nc.Block() as block:
            @block.sync
            def _(sp):
                sp.dma_start(io["y_out"].rearrange("(k p) t -> p k t", p=P), x[:, :, :]).then_inc(last_stored, 16)
                sp.wait_ge(last_stored, 16)
    return st.seen


def shape_constants():
    c = np.zeros((P, NCONST), np.float32)

    def put(name, value, rows=P):
        a, w = CONST[name]
        c[0:rows, a:a + w] = value

    put("ident", np.eye(P))
    put("ones_d", 1.0 / D)
    put("ones_v", 1.0 / C_DV)
    perm = np.zeros((P, P))
    for j in range(P):
        if j % A_ROPE < A_ROPE // 2:
            perm[j + A_ROPE // 2, j] = -1.0
        else:
            perm[j - A_ROPE // 2, j] = 1.0
    put("perm", perm)
    put("selrep", (np.arange(144) % BLK == BLK - 1).astype(np.float32)[None])
    blk = np.arange(P) // BLK
    put("blockmask", (blk[:, None] == blk[None, :]).astype(np.float32))
    half = A_ROPE // 2
    inv = np.float32(10000.0) ** (-np.arange(half, dtype=np.float32) / np.float32(half))
    pos = np.concatenate([np.arange(SEQ), np.zeros(META), PAST + np.arange(DEC)]).astype(np.float32)
    ang = pos[None, :] * inv[np.arange(P) % half][:, None].astype(np.float32)
    put("cos", np.cos(ang.astype(np.float32)))
    put("sin", np.sin(ang.astype(np.float32)))
    far = 1e34
    r = np.arange(P)[:, None]
    prev, own = np.arange(-CHUNK, 0)[None], np.arange(P)[None]
    put("dist", np.concatenate([np.where(r < CHUNK, np.abs(r - prev), far), np.zeros((P, META)),
                                np.where(own // CHUNK <= r // CHUNK, np.abs(r - own), far)], 1))
    d = np.full((MIXED, 192), far)
    q = PAST + np.arange(DEC)[:, None]
    k = PAST - WIN + np.arange(WIN + DEC)[None]
    seen = (k // CHUNK <= q // CHUNK) & (k // CHUNK > q // CHUNK - WIN // CHUNK)
    d[META:, 0:WIN + DEC] = np.where(seen, np.abs(q - k), far)
    d[META:, WIN + DEC:WIN + DEC + META] = 0.0
    d[0:META, WIN + DEC + META:] = 0.0
    put("dist_s", d, MIXED)
    m = np.full((MIXED, 320), NEG)
    m[META:, 0:304] = 0.0
    m[0:META, 304:] = 0.0
    put("mask_s", m, MIXED)
    put("rows", (np.arange(P) < CHUNK).astype(np.float32)[None])
    put("neg", NEG)
    put("ones", 1.0)
    put("eps", EPS)
    return c


def pack_units(i, l):
    w_in = i["w_in"][l]
    sizes = [512, 256, 256, 32, 512, 128, 128, 512, 512, 1024, 16, 1024, 3072]
    edge = np.concatenate([[0], np.cumsum(sizes)])
    part = {n: w_in[:, edge[j]:edge[j + 1]] for j, n in enumerate(
        ("qn", "qr", "ckv", "kr", "qb", "kb", "vb", "cq", "ck", "cv", "alr", "cg", "gate"))}
    qb = part["qb"].reshape(D, B_KV, B_G, B_HD).transpose(0, 2, 1, 3).reshape(D, -1)
    up_b = i["w_up_b"][l].reshape(B_KV, B_G, B_HD, D).transpose(1, 0, 2, 3).reshape(-1, D)
    out = np.empty((NU, P, 1024), np.float32)
    for u, (kind, n) in enumerate(UNITS):
        c = slice(128 * n, 128 * n + 128)
        if kind == "kralr":
            m = np.concatenate([part["kr"]] * 3 + [part["alr"], np.zeros((D, 16), np.float32)], 1)
        elif kind == "qb":
            m = qb[:, c]
        elif kind.startswith("gate"):
            b = "abc".index(kind[-1])
            m = part["gate"][:, D * b + 128 * n:D * b + 128 * n + 128]
        elif kind == "up_c":
            m = i["w_up_c"][l][:, c]
        elif kind in ("up_a", "up_b"):
            m = (i["w_up_a"][l] if kind == "up_a" else up_b)[:, 128 * n:128 * n + 256]
        elif kind == "out":
            m = i["w_out"][l][:, c]
        elif kind == "ff1":
            m = i["w_ff1"][l][:, c]
        elif kind == "ff2":
            g, t = n // 8, n % 8
            m = i["w_ff2"][l][D * g:D * g + D, 128 * t:128 * t + 128]
        else:
            m = part[kind][:, c]
        k = m.shape[0] // P
        out[u] = m.reshape(k, P, m.shape[1]).transpose(1, 0, 2).reshape(P, 1024)
    return out


def pack_params(i, l):
    p = np.zeros((P, NPARAM), np.float32)

    def put(name, v):
        a, w = PARAM[name]
        p[:, a:a + w] = v

    for name in ("g_post_mix", "g_pre_mlp", "g_post_mlp", "g_kv", "g_gla", "b_alpha"):
        put(name, i[name][l].reshape(-1, P).T)
    put("sinks", np.repeat(i["b_sinks"][l][None], P, 0))
    return p


OUTPUTS = {"y_out": (D, T), "c_out": (DEPTH, LORA, T), "kr_out": (DEPTH, A_ROPE, T),
           "kb_out": (DEPTH, P, T - 384), "vb_out": (DEPTH, P, T - 384),
           "kw_out": (DEPTH, P, WIN), "vw_out": (DEPTH, P, WIN),
           "p_state": (DEPTH * C_HEADS, C_DK, C_DV), "s_state": (DEPTH * C_HEADS, C_DK, C_DV)}


def kernel(**inputs):
    import concourse.bacc as bacc
    from concourse.bass_utils import run_bass_kernel_spmd

    i = {k: np.asarray(v) for k, v in inputs.items()}
    two = range(DEPTH)
    t = lambda a: np.ascontiguousarray(np.swapaxes(a, -1, -2))
    a_ckv = np.concatenate([i["cache_A_ckv"][:, 0], i["cache_A_meta_ckv"][:, 0]], 1)
    a_kr = np.concatenate([i["cache_A_krope"][:, 0], i["cache_A_meta_krope"][:, 0]], 1)
    b_k = i["cache_B_k"][:, 0].reshape(DEPTH, WIN, P)
    b_v = i["cache_B_v"][:, 0].reshape(DEPTH, WIN, P)
    b_mk = i["cache_B_meta_k"][:, 0].reshape(DEPTH, META, P)
    arrays = {
        "x": t(np.concatenate([i["x_prompt"][0], i["meta_tokens"], i["x_sample"][0]], 0)),
        "const": shape_constants(),
        "w": np.concatenate([pack_units(i, l) for l in two] + [np.zeros((WSLOTS, P, 1024), np.float32)]),
        "g_pre_mix": np.concatenate([i["g_pre_mix"].reshape(DEPTH, KD, P).transpose(0, 2, 1), np.zeros((1, P, KD), np.float32)]),
        "par": np.stack([pack_params(i, l) for l in two]),
        "w_alpha": i["w_alpha"], "w_uk": i["w_uk"].reshape(DEPTH, LORA, 512), "w_uv": i["w_uv"].reshape(DEPTH, LORA, 512),
        "a_ckv": t(a_ckv), "a_kr": np.tile(t(a_kr), (1, 4, 1)),
        "b_k": t(np.concatenate([b_k, b_mk], 1)), "b_v": b_v,
        "b_vm": i["cache_B_meta_v"][:, 0].reshape(DEPTH, META, P),
        "b_kw": t(b_k), "b_vw": t(b_v),
        "state": i["state_C"][:, 0].reshape(DEPTH * C_HEADS, C_DK, C_DV),
    }
    arrays = {k: np.ascontiguousarray(v) for k, v in arrays.items()}

    def program(known):
        nc = bacc.Bacc("TRN2", target_bir_lowering=False, num_devices=1)
        io = {k: nc.dram_tensor("in_" + k, v.shape, F32, kind="ExternalInput").ap() for k, v in arrays.items()}
        io.update({k: nc.dram_tensor("out_" + k, v, F32, kind="ExternalOutput").ap() for k, v in OUTPUTS.items()})
        io["x_spill"] = nc.dram_tensor("x_spill", (P, KD, T), F32, kind="Internal").ap()
        return nc, build(nc, io, known)

    _, known = program(None)
    nc, _ = program(known)
    r = run_bass_kernel_spmd(nc, [{"in_" + k: v for k, v in arrays.items()}], core_ids=[0]).results[0]
    o = {k: r["out_" + k] for k in OUTPUTS}

    y = t(o["y_out"])
    c, kr = t(o["c_out"]), t(o["kr_out"])
    kb, vb, kw, vw = t(o["kb_out"]), t(o["vb_out"]), t(o["kw_out"]), t(o["vw_out"])
    f, m, s = slice(0, SEQ), slice(META0, SAMP0), slice(SAMP0, T)
    heads = lambda a: a.reshape(DEPTH, 1, -1, B_KV, B_HD)
    states = lambda a: a.reshape(DEPTH, 1, C_HEADS, C_DK, C_DV)
    return (y[None, f], y[None, s], c[:, None, f], kr[:, None, f], c[:, None, m], kr[:, None, m],
            heads(kb[:, 0:128]), heads(vb[:, 0:128]), heads(kb[:, 128:144]), heads(vb[:, 128:144]),
            states(o["p_state"]), c[:, None, s], kr[:, None, s], heads(kw), heads(vw), states(o["s_state"]))
```

```python
import concourse.bass as bass
from concourse import mybir
from contextlib import ExitStack
import numpy as np

F32 = mybir.dt.float32
F32R = mybir.dt.float32r
ALU = mybir.AluOpType
ACT = mybir.ActivationFunctionType
AX = mybir.AxisListType

P = 128
D = 1024
KD = D // P
SEQ, META, DEC = 512, 16, 32
T = SEQ + META + DEC
HALF = T // 2
DEPTH = 2
CHUNK = 64
PAST = 256
LORA, KL = 256, 2
A_HEADS, A_NOPE, A_ROPE, A_V = 8, 64, 32, 64
B_HEADS, B_KV, B_HD = 8, 2, 64
B_G = B_HEADS // B_KV
WIN = 128
C_HEADS, C_DK, C_DV, C_LR = 4, 128, 256, 16
D_FF = 4 * D
BLK = 16
EPS = 1e-6
A_SCALE = float((A_NOPE + A_ROPE) ** -0.5)
B_SCALE = float(B_HD ** -0.5)
META0, SAMP0 = SEQ, SEQ + META
MIXED = META + DEC
CKEYS = PAST + META
NBLK = T // BLK
NEG = -1e30
WSLOTS = 3

SUPER = [(META0, META)] + [(128 * i, 128) for i in range(SEQ // 128)] + [(SAMP0, DEC)]


def plan_units():
    units = [("kralr", 0)]
    for h in range(C_HEADS):
        units += [("cq", h), ("ck", h), ("cv", 2 * h), ("cv", 2 * h + 1), ("cg", 2 * h), ("cg", 2 * h + 1)]
    units += [("ckv", n) for n in range(2)] + [("qn", n) for n in range(4)] + [("qr", n) for n in range(2)]
    for n in range(KD):
        units += [("gate_c", n), ("up_c", n)]
    units += [("gate_a", 0), ("gate_a", 1)]
    units += [("kb", 0), ("vb", 0)] + [("qb", n) for n in range(4)]
    for b in "ab":
        for n in range(0, KD, 2):
            if (b, n) != ("a", 0):
                units += [("gate_" + b, n), ("gate_" + b, n + 1)]
            units += [("up_" + b, n)]
    units += [("out", n) for n in range(KD)]
    ff1 = [[("ff1", 8 * g + n) for n in range(8)] for g in range(4)]
    ff2 = [[("ff2", 8 * g + n) for n in range(8)] for g in range(4)]
    units += ff1[0] + ff1[1] + ff2[0] + ff1[2] + ff2[1] + ff1[3] + ff2[2] + ff2[3]
    return units


UNITS = plan_units()
NU = len(UNITS)
UIDX = {u: n for n, u in enumerate(UNITS)}


def outs_of(kind):
    return (2, 4) if kind in ("up_a", "up_b") else (1, KD)


CONST = {}
_at = 0
for _name, _w in (("ident", 128), ("ones_d", 128), ("eps", 1), ("ones_v", 128), ("perm", 128), ("selrep", 144),
                  ("blockmask", 128), ("cos", T), ("sin", T), ("dist", 208), ("mask_s", 320),
                  ("dist_s", 192), ("ones", 128)):
    CONST[_name] = (_at, _w)
    _at += _w
NCONST = _at
CONST_FIRST = CONST["ones_v"][0]
PARAM = {}
_at = 0
for _name, _w in (("g_post_mix", 8), ("g_pre_mlp", 8), ("g_post_mlp", 8), ("g_kv", 2),
                  ("g_gla", 2), ("b_alpha", 4), ("sinks", 8)):
    PARAM[_name] = (_at, _w)
    _at += _w
NPARAM = _at


class Steps:

    def __init__(self, known):
        self.count = {e: 0 for e in ("pe", "act", "dve", "pool")}
        self.known = known
        self.seen = {}

    def done(self, engine, name=None):
        self.count[engine] += 1
        if name is not None:
            assert (engine, name) not in self.seen, name
            self.seen[engine, name] = self.count[engine]
        return 1

    def at(self, engine, name):
        if self.known is None:
            return 1
        return self.known[engine, name]


def build(nc, io, known):
    st = Steps(known)
    ctx = ExitStack()
    with ctx:
        def sem(name):
            return ctx.enter_context(nc.semaphore(name))

        base = 16512
        place = {"next": base}

        def at(name, shape, dt, offset):
            size = 4 * int(np.prod(shape[1:]))
            assert offset + size <= 229344, (name, offset + size)
            return nc.alloc_sbuf_tensor_at(name, shape, dt, offset=offset)

        def region(size):
            off = place["next"]
            place["next"] += (size + 31) // 32 * 32
            return off

        row = 4 * T
        r_w = [region(8192) for _ in range(WSLOTS)]
        r_h = region(16 * row)
        r_oc = region(16 * row)
        r_x = region(8 * row)
        r_sig = region(2 * row)
        r_r = region(row)
        r_const = region(4 * NCONST)
        r_par = region(4 * NPARAM)
        r_gpre = region(4 * KD)
        work = place["next"]

        wraw = [at(f"wraw{s}", [P, 1024], F32, r_w[s]) for s in range(WSLOTS)]
        wlo = [at(f"wlo{s}", [P, 1024], F32R, r_w[s]) for s in range(WSLOTS)]
        whi = [at(f"whi{s}", [P, 1024], F32R, r_w[s] + 4096) for s in range(WSLOTS)]

        def split_set(name, n, off):
            return (at(name + "_raw", [P, n, T], F32, off), at(name + "_lo", [P, n, T], F32R, off),
                    at(name + "_hi", [P, n, T], F32R, off + n * row))

        h_raw, h_lo, h_hi = split_set("h", KD, r_h)
        oc_raw, oc_lo, oc_hi = split_set("oc", KD, r_oc)
        hid0 = split_set("hid0", KD, r_oc)
        hid1 = split_set("hid1", KD, work)
        hid = [hid0, hid1]
        mix = at("mix", [P, KD, T], F32, r_oc)
        sq = at("sq", [P, KD, T], F32, r_oc + KD * row)
        sqsum, sqpart = sq[:, 0, :], [sq[:, 1, :], sq[:, 2, :]]
        facc = at("facc", [P, KD, T], F32, work + 16 * row)
        x = at("x", [P, KD, T], F32, r_x)
        y = at("y", [P, KD, T], F32, r_x)
        sig = at("sig", [P, 2, T], F32, r_sig)
        rstd = at("rstd", [P, T], F32, r_r)
        const = at("const", [P, NCONST], F32, r_const)
        par = at("par", [P, NPARAM], F32, r_par)
        g_pre_mix = at("g_pre_mix", [P, KD], F32, r_gpre)

        def c_(name, rows=P):
            a, w = CONST[name]
            return const[0:rows, a:a + w]

        w_alpha = const[:, CONST["mask_s"][0]:CONST["mask_s"][0] + 512]

        def p_(name, n=0, w=1, rows=P, r0=0):
            a = PARAM[name][0] + n
            return par[r0:r0 + rows, a:a + w]

        wk = {"next": work}

        def wt(name, shape, dt=F32, off=None):
            size = 4 * int(np.prod(shape[1:]))
            if off is None:
                off = wk["next"]
                wk["next"] += (size + 31) // 32 * 32
            return at(name, shape, dt, off), off

        kra, _ = wt("kra", [P, T])
        keep = wk["next"]
        cproj = [wt(f"cproj{i}", [P, 6, T])[0] for i in range(2)]
        bcum, _ = wt("bcum", [P, T])
        ediag, ediag_off = wt("ediag", [P, NBLK * BLK * (BLK + 1) // 2])
        kfar, _ = wt("kfar", [P, 64 * 28])
        zlog = at("zlog", [P, T], F32, ediag_off)
        ztmp = at("ztmp", [P, T], F32, ediag_off + row)
        lsig = at("lsig", [P, T], F32, ediag_off + 2 * row)
        kfar_s, _ = wt("kfar_s", [P, BLK])
        qfar, _ = wt("qfar", [P, 4 * 112])
        qfar_s, _ = wt("qfar_s", [P, BLK])
        kend, _ = wt("kend", [P, T])
        ebl, _ = wt("ebl", [P, T])
        amat, _ = wt("amat", [P, T])
        ktok, _ = wt("ktok", [P, 6, 128])
        state, _ = wt("state", [P, 8, C_DV])
        assert wk["next"] <= 229344, wk["next"]
        gsq = at("gsq", [P, 2, T], F32, r_x)
        oh = at("oh", [P, 2, T], F32, r_x + 2 * row)
        vtok = at("vtok", [P, 6, 256], F32, r_x + 4 * row)
        qe = at("qe", [P, T], F32, r_x + 4 * row + 6144)
        gsig = sig
        cksq = at("cksq", [P, 2, T], F32, r_x)
        wk["next"] = keep
        oa_raw, oa_lo, oa_hi = split_set("oa", 4, keep)
        qn = at("qn", [P, 4, T], F32, keep)
        wk["next"] = keep + 8 * row
        a_tmp = keep + 4 * row
        ckv = at("ckv", [P, KL, T], F32, a_tmp)
        cct = at("cct", [P, KL, CKEYS], F32, a_tmp + 2 * row)
        qr, _ = wt("qr", [P, 2, T])
        qrot, _ = wt("qrot", [P, 2, T])
        kn, _ = wt("kn", [P, 4, T])
        krot, _ = wt("krot", [P, T])
        va, _ = wt("va", [P, 4, 512])
        va_mix, _ = wt("va_mix", [MIXED, 512])
        kn_c, _ = wt("kn_c", [P, 4, CKEYS])
        va_c, _ = wt("va_c", [P, 2, 512])
        va_cm, _ = wt("va_cm", [META, 512])
        kr_c, _ = wt("kr_c", [P, CKEYS])
        p_off = wk["next"]
        prob = [wt(f"prob{i}", [P, 1056])[0] for i in range(2)]
        wuk = at("wuk", [P, KL, 512], F32, p_off)
        wuv = at("wuv", [P, KL, 512], F32, p_off + 4096)
        ptf_off = wk["next"]
        ptf, _ = wt("ptf", [P, 2, 512])
        ptm, _ = wt("ptm", [META, 512])
        stat, _ = wt("stat", [P, 2, 24])
        a_end = wk["next"]
        assert a_end <= 229344, a_end
        wk["next"] = keep + 8 * row
        ob_raw, ob_lo, ob_hi = split_set("ob", 4, wk["next"])
        wk["next"] += 8 * row
        qb = at("qb", [P, 4, T], F32, wk["next"])
        wk["next"] += 4 * row
        kb, _ = wt("kb", [P, T])
        vb, _ = wt("vb", [P, T])
        v_own, _ = wt("v_own", [P, 4, 128])
        v_prev, _ = wt("v_prev", [80, 3, 128])
        v_mix, _ = wt("v_mix", [MIXED, 128])
        kb_c, _ = wt("kb_c", [P, WIN + META])
        vb_c, _ = wt("vb_c", [P, 128])
        vb_cm, _ = wt("vb_cm", [META, 128])
        assert wk["next"] <= p_off, (wk["next"], p_off)

        dps = [ctx.enter_context(nc.psum_tensor(f"dense{i}", [P, 512], F32)) for i in range(2)]
        ps = ctx.enter_context(nc.psum_tensor("att", [P, 6, 512], F32))
        S0, S1, M_, T0, T1, O_ = range(6)
        PAIRS = [slice(0, 2), slice(3, 5)]

        pe_done, act_done, dve_done, pool_done = (sem(n) for n in ("pe_done", "act_done", "dve_done", "pool_done"))
        w_loaded = [sem(f"w_loaded{s}") for s in range(WSLOTS)]
        w_ahead = [sem(f"w_ahead{s}") for s in range(WSLOTS)]
        par_loaded = sem("par_loaded")
        spilled = sem("x_spilled")
        x_back = sem("x_back")
        a_loaded = {n: sem(f"a_{n}_loaded") for n in ("w_uk", "a_ckv", "w_uv", "a_kr")}
        b_loaded = sem("b_cache_loaded")
        state_loaded = sem("state_loaded")
        stored = sem("outputs_stored")
        block_sems = [pe_done, act_done, dve_done, pool_done, *w_loaded, *w_ahead, par_loaded, spilled, x_back, *a_loaded.values(),
                      b_loaded, state_loaded, stored]
        ahead_loaded = sem("ahead_loaded")
        block_sems.append(ahead_loaded)
        ones_loaded, rest_loaded = sem("ones_loaded"), sem("rest_loaded")
        w_first, w2_first = sem("first_weights_loaded"), sem("third_weights_loaded")
        x_loaded = [sem(f"x_loaded{i}") for i in range(4)]
        first_sq, first_ms, first_rstd, first_hi, first_lo = (sem("first_" + n) for n in ("sq", "ms", "rstd", "hi", "lo"))
        last_stored = sem("last_stored")

        rtmp = at("rtmp", [P, T], F32, ptf_off)
        eps = c_("eps")
        DIAG_SPLIT = 16
        STATE_IN = [0, 1, 2, 3, 4, 6]
        STATE_OUT = [1, 2, 3, 4, 5, 7]
        VTOK_PAIRS = [(1, 2), (3, 4), (0, 5)]
        VTOK_BANKS = [M_, O_, T1]
        VA_TILES = [
            [(ckv, 0, 128, va[:, 0, :]), (ckv, 128, 128, va[:, 1, :])],
            [(ckv, 256, 128, va[:, 2, :]), (ckv, 384, 128, va[:, 3, :])],
            [(cct, 0, 128, va_c[:, 0, :]), (cct, 128, 128, va_c[:, 1, :])],
            [(cct, PAST, META, va_cm[:, :]), (ckv, META0, MIXED, va_mix[:, :])],
        ]
        PREP_A = [0, 1, 2, 4, 3] + list(range(5, len(VA_TILES) + 10))
        PREP_A_OVER = [("act", "prep a 12"), ("dve", "prep a 13"), ("dve", "krot"), ("dve", "qrot 1")]

        def ediag_of(j):
            a = NBLK * (BLK * j - j * (j - 1) // 2)
            return ediag[:, a:a + NBLK * (BLK - j)]

        def kfar_of(i):
            a = 32 * i * (i - 1)
            return kfar[:, a:a + 64 * i]

        def prep_pair(s):
            return PAIRS[PREP_A.index(s) % 2]

        def prep_evac(s):
            if s == 0:
                return "act"
            if s < 4:
                return "dve"
            return "act" if s % 2 == 0 else "dve"

        with nc.Block() as block:
            @block.sync
            def _(sp):
                sp.dma_start(const[:, 0:CONST_FIRST], io["const"][:, 0:CONST_FIRST]).then_inc(ones_loaded, 16)
                for i in range(4):
                    sp.dma_start(x[:, 2 * i:2 * i + 2, :], io["x"][256 * i:256 * i + 256, :].rearrange("(k p) t -> p k t", p=P)
                                 ).then_inc(x_loaded[i], 16)
                for u in range(2):
                    sp.dma_start(wraw[u][:, :], io["w"][u]).then_inc(w_first, 16)
                sp.dma_start(g_pre_mix[:, :], io["g_pre_mix"][0]).then_inc(w_first, 16)
                sp.dma_start(wraw[2][:, :], io["w"][2]).then_inc(w2_first, 16)
                sp.dma_start(const[:, CONST_FIRST:], io["const"][:, CONST_FIRST:]).then_inc(rest_loaded, 16)
                sp.wait_ge(w_first, 48)

            @block.tensor
            def _(pe):
                pe.wait_ge(ones_loaded, 16)
                for k in range(KD):
                    pe.wait_ge(first_sq, k + 1)
                    for hf in range(2):
                        mm = pe.matmul(ps[:, T0 + hf, 0:HALF], c_("ones_d"), sq[:, k, HALF * hf:HALF * hf + HALF],
                                       start=(k == 0), stop=(k == KD - 1))
                mm.then_inc(first_ms, 1)

            @block.scalar
            def _(act):
                act.preload_act_table_set("natural_log_exp_and_others")
                for k in range(KD):
                    act.wait_ge(x_loaded[k // 2], 16)
                    act.activation(sq[:, k, :], x[:, k, :], ACT.Square).then_inc(first_sq, 1)
                act.wait_ge(w_first, 48)
                for u in range(2):
                    act.activation(whi[u][:, :], wraw[u][:, :], ACT.Copy).then_inc(first_hi, 1)
                act.wait_ge(first_ms, 1)
                act.wait_ge(ones_loaded, 16)
                act.activation(rstd[:, :].rearrange("p (a n) -> p a n", a=2), ps[:, PAIRS[1], 0:HALF], ACT.Ln,
                               bias=eps[:, 0:1]).then_inc(first_rstd, 1)
                act.wait_ge(first_rstd, 1)
                act.activation(rstd[:, :], rstd[:, :], ACT.Exp, scale=-0.5).then_inc(first_rstd, 1)
                act.wait_ge(first_rstd, 2)

            @block.gpsimd
            def _(pool):
                for u in range(2):
                    pool.wait_ge(first_hi, u + 1)
                    pool.tensor_tensor(wlo[u][:, :], wraw[u][:, :], whi[u][:, :].bitcast(F32), ALU.subtract).then_inc(first_lo, 1)
                pool.wait_ge(first_lo, 2)

        def layer(l, block):
            H = (slice(0, HALF), slice(HALF, T))
            def A(e, n):
                return st.at(e, n)

            moving = {"h": (h_hi, h_lo), "oc": (oc_hi, oc_lo), "oa": (oa_hi, oa_lo), "ob": (ob_hi, ob_lo),
                      "y": (h_hi, h_lo), "h2": (h_hi, h_lo), "hid0": (hid0[2], hid0[1]), "hid1": (hid1[2], hid1[1])}

            def source(kind, n):
                if kind == "up_c":
                    return "oc"
                if kind == "up_a":
                    return "oa"
                if kind == "up_b":
                    return "ob"
                if kind == "out":
                    return "y"
                if kind == "ff1":
                    return "h2"
                if kind == "ff2":
                    return "hid%d" % (n // 8 % 2)
                return "h"

            def ready_names(kind, n, k):
                s = source(kind, n)
                if s == "ob":
                    return ("act", "ob hi 4"), ("pool", "ob lo 4")
                if s.startswith("hid"):
                    g = n // 8
                    return ("act", f"hid hi {8 * g + k}"), ("pool", f"hid lo {8 * g + k}")
                lo = lo_engine(s, k) if s in ("h", "h2", "y") else "dve" if s == "oc" else "pool"
                return ("act", f"{s} hi {k}"), (lo, f"{s} lo {k}")

            halves_done = []
            for u, (kind, n) in enumerate(UNITS):
                for o in range(outs_of(kind)[0]):
                    for hf in range(2):
                        halves_done.append((u, o, hf))
            bank_of = {key: i % 2 for i, key in enumerate(halves_done)}
            before = {key: halves_done[i - 2] for i, key in enumerate(halves_done) if i >= 2}

            def evac_engine(kind):
                return "act" if kind in ("ck", "cg", "out", "ff1", "vb") else "dve"

            order = []
            dn = iter(range(NU))

            def dense(k=1):
                for _ in range(k):
                    order.append(("dense", next(dn)))

            order.append(("tokens", "pre_mix"))
            dense(1)
            dense(6)
            def gla_steps(*steps):
                for h, what in steps:
                    order.append(("gla", h, what))

            for h in range(C_HEADS):
                gla_steps((h, "p z"), (h, "v decay"))
                dense()
                if h > 0:
                    gla_steps((h - 1, "p ms"))
                gla_steps((h, "v diag 0"))
                dense()
                if h > 0:
                    gla_steps((h - 1, "v out"))
                gla_steps((h, "p vtok"), (h, "v vtok"), (h, "v diag 1"), (h, "v diag 2"))
                dense()
                gla_steps((h, "v diag 3"), (h, "v farq"), (h, "v kend"), (h, "v far"), (h, "p diag 0"), (h, "p diag 1"), (h, "p diag 2"))
                dense()
                gla_steps((h, "p diag 3"), (h, "p ktok"), (h, "p far"), (h, "v ktok"), (h, "v amat"))
                dense()
                gla_steps((h, "p kv"), (h, "v state"), (h, "v silu"))
                if h == C_HEADS - 1:
                    order.append(("prep_a", "square"))
                dense()
                if h == C_HEADS - 1:
                    order.append(("prep_a", 0))
                gla_steps((h, "p o"), (h, "v o"))
            dense(1)
            gla_steps((C_HEADS - 1, "p ms"), (C_HEADS - 1, "v out"))
            order += [("prep_a", "load"), ("prep_a", 1)]
            dense(1)
            for s in PREP_A[2:]:
                order.append(("prep_a", s))
            jobs = [("a", t, i) for t in range(4) for i in range(5)]
            for j in range(len(jobs) + 2):
                order.append(("att", "a", j))
                if j not in (5, 10, 15, 21):
                    dense()
            dense(2)
            order.append(("prep_b", 0))
            dense(2)
            order.append(("prep_b", 1))
            dense(2)
            jobs_b = [("b", kv, i) for kv in range(2) for i in range(5)]
            for j in range(len(jobs_b) + 2):
                order.append(("att", "b", j))
                dense()
            while True:
                try:
                    u = next(dn)
                except StopIteration:
                    break
                if UNITS[u] == ("up_b", 6):
                    order.append(("split_y", 0))
                if UNITS[u] == ("out", 0):
                    order.append(("split_y", 1))
                if UNITS[u] == ("ff1", 0):
                    order += [("norm", "post_mix"), ("mean", "pre_mlp"), ("tokens", "pre_mlp")]
                order.append(("dense", u))
            order += [("norm", "post_mlp"), ("mean", "next")]
            JOBS = {"a": jobs, "b": jobs_b}
            BLOCKS = [slice(128 * i, 128 * i + 128) for i in range(4)] + [slice(META0, T)]
            AHEAD = [u % WSLOTS for u in range(NU - WSLOTS, NU)]
            Y_SPLIT = [range(6), range(6, KD)]

            def y_engine(b, n):
                return "dve" if b == "b" and n >= 6 else "pool"

            def x_engine(k):
                return "pool" if k % 2 else "dve"

            def lo_engine(s, k):
                return "dve" if (k >= 6 if s == "y" else k % 2) else "pool"

            by_name = {"pe": pe_done, "act": act_done, "dve": dve_done, "pool": pool_done}
            norm_src = {"post_mix": mix, "post_mlp": facc}

            def summed(u):
                kind, n = UNITS[u]
                if kind == "out":
                    return "post_mix", n
                if kind == "ff2" and n >= 24:
                    return "post_mlp", n - 24
                return None

            def sig_free(b, n):
                if b == "c":
                    return (dve_done, A("dve", f"evac {UIDX['up_c', n - 2]} 0 1")) if n >= 2 else (dve_done, A("dve", f"gla out {C_HEADS - 1} 1"))
                if b == "a" and n < 2:
                    return dve_done, A("dve", f"evac {UIDX['up_c', n + 6]} 0 1")
                return pool_done, A("pool", f"y a {n + 6}" if n < 2 else f"y {b} {n - 2}")

            def key_count(br, i):
                if br == "a":
                    return 128 * (i + 1) + META if i < 4 else 320
                return (144 if i == 0 else 208) if i < 4 else 192

            def prob_view(br, j):
                _, t, i = JOBS[br][j]
                nk = key_count(br, i)
                if br == "a":
                    return prob[j % 2][:, 0:2 * nk].rearrange("p (a n) -> p a n", a=2)
                return prob[j % 2][:, 0:4 * (nk + 1)].rearrange("p (a n) -> p a n", a=4)

            @block.sync
            def _(sp):
                sp.dma_start(par[:, :], io["par"][bass.ds(l, 1), :, :].rearrange("a p n -> (a p) n")).then_inc(par_loaded, 16)
                sp.wait_ge(rest_loaded, 16)
                sp.dma_start(w_alpha[96:112, :], io["w_alpha"][bass.ds(l, 1), :, :].rearrange("a p n -> (a p) n")).then_inc(par_loaded, 16)

                def load(slot, u):
                    sp.dma_start(wraw[slot][:, :], io["w"][bass.ds(l * NU + u, 1), :, :].rearrange("a p n -> (a p) n")
                                 ).then_inc(w_loaded[slot], 16)

                for u in range(WSLOTS, NU):
                    sp.wait_ge(pe_done, A("pe", f"dense {u - WSLOTS}"))
                    load(u % WSLOTS, u)
                sp.wait_ge(dve_done, A("dve", "h raw pre_mix 7"))
                sp.dma_start(g_pre_mix[:, :], io["g_pre_mix"][bass.ds(l + 1, 1), :, :].rearrange("a p n -> (a p) n")
                             ).then_inc(ahead_loaded, 16)
                for n, slot in enumerate(AHEAD):
                    sp.wait_ge(pe_done, A("pe", f"dense {NU - WSLOTS + n}"))
                    sp.dma_start(wraw[slot][:, :], io["w"][bass.ds(l * NU + NU + slot, 1), :, :].rearrange("a p n -> (a p) n")
                                 ).then_inc(w_ahead[slot], 16)
                sp.wait_ge(ahead_loaded, 16)
                for slot in AHEAD:
                    sp.wait_ge(w_ahead[slot], 16)

            @block.tensor
            def _(pe):
                first_use = set()

                def dense_unit(u):
                    kind, n = UNITS[u]
                    nout, kt = outs_of(kind)
                    slot = u % WSLOTS
                    hi_w = whi[slot][:, :].rearrange("p (k m) -> p k m", k=kt)
                    lo_w = wlo[slot][:, :].rearrange("p (k m) -> p k m", k=kt)
                    src = source(kind, n)
                    hi_x, lo_x = moving[src]
                    key = (src, n // 8) if kind == "ff2" else src
                    fresh = key not in first_use
                    first_use.add(key)
                    if u >= 2:
                        pe.wait_ge(act_done, A("act", f"w hi {u}"))
                        pe.wait_ge(pool_done, A("pool", f"w lo {u}"))
                    m = 112 if kind == "kralr" else 128
                    by_tile = fresh and src in ("h", "h2", "y")
                    if by_tile:
                        for hf in range(2):
                            if (u, 0, hf) in before:
                                pu, po, ph = before[u, 0, hf]
                                e = evac_engine(UNITS[pu][0])
                                pe.wait_ge(by_name[e], A(e, f"evac {pu} {po} {ph}"))
                        for k in range(kt):
                            for e, name in ready_names(kind, n, k):
                                pe.wait_ge(by_name[e], A(e, name))
                            for hf in range(2):
                                for i, (a, b) in enumerate(((hi_w, hi_x), (lo_w, hi_x), (hi_w, lo_x))):
                                    mm = pe.matmul(dps[bank_of[u, 0, hf]][0:m, 0:HALF], a[:, k, 0:m], b[:, k, H[hf]],
                                                   start=(k == 0 and i == 0), stop=(k == kt - 1 and i == 2))
                                if k == kt - 1:
                                    mm.then_inc(pe_done, st.done("pe", f"half {u} 0 {hf}"))
                        st.seen["pe", f"dense {u}"] = st.count["pe"]
                        return
                    for o in range(nout):
                        for hf in range(2):
                            bank = dps[bank_of[u, o, hf]]
                            if (u, o, hf) in before:
                                pu, po, ph = before[u, o, hf]
                                pe.wait_ge(act_done if evac_engine(UNITS[pu][0]) == "act" else dve_done,
                                           A(evac_engine(UNITS[pu][0]), f"evac {pu} {po} {ph}"))
                            for k in range(kt):
                                if fresh and o == 0 and hf == 0:
                                    for e, name in ready_names(kind, n, k):
                                        pe.wait_ge(by_name[e], A(e, name))
                                for i, (a, b) in enumerate(((hi_w, hi_x), (lo_w, hi_x), (hi_w, lo_x))):
                                    mm = pe.matmul(bank[0:m, 0:HALF], a[:, k, o * 128:o * 128 + m], b[:, k, H[hf]],
                                                   start=(k == 0 and i == 0), stop=(k == kt - 1 and i == 2))
                            mm.then_inc(pe_done, st.done("pe", f"half {u} {o} {hf}"))
                    st.seen["pe", f"dense {u}"] = st.count["pe"]

                def norm(which):
                    for hf in range(2):
                        pe.wait_ge(dve_done, A("dve", f"sum {which} 7 {hf}"))
                        mm = pe.matmul(ps[:, S0 + hf, 0:HALF], c_("ones_d"), sqsum[:, H[hf]], start=True, stop=True)
                    mm.then_inc(pe_done, st.done("pe", f"ms {which}"))

                def mean(which):
                    for k in range(KD):
                        pe.wait_ge(act_done, A("act", f"sq {which} {k}"))
                        for hf in range(2):
                            mm = pe.matmul(ps[:, T0 + hf, 0:HALF], c_("ones_d"), sq[:, k, H[hf]],
                                           start=(k == 0), stop=(k == KD - 1))
                    mm.then_inc(pe_done, st.done("pe", f"ms {which}"))

                def gla(h, s):
                    pr = cproj[h % 2]
                    q, kk = pr[:, 0, :], pr[:, 1, :]
                    if s == "p z":
                        if h == 0:
                            pe.wait_ge(dve_done, A("dve", f"evac {UIDX['kralr', 0]} 0 1"))
                            pe.wait_ge(par_loaded, 32)
                        else:
                            pe.wait_ge(dve_done, A("dve", f"gla state {h - 1}"))
                        for hf in range(2):
                            mm = pe.matmul(ps[:, S0 + hf, 0:HALF], w_alpha[96:112, 128 * h:128 * h + 128],
                                           kra[96:112, H[hf]], start=True, stop=True)
                        mm.then_inc(pe_done, st.done("pe", f"gla z {h}"))
                    if s.startswith("p diag"):
                        if s == "p diag 0":
                            pe.wait_ge(act_done, A("act", f"gla z {h}"))
                            if h > 0:
                                pe.wait_ge(act_done, A("act", f"gla rstd {h - 1}"))
                        for j in range(4 * int(s[-1]), 4 * int(s[-1]) + 4):
                            w = BLK - j
                            pe.wait_ge(dve_done, A("dve", f"gla e {h} {j}"))
                            a0 = CONST["selrep"][0] + 15 - j
                            e = ediag_of(j).rearrange("p (b t) -> p b t", t=w)
                            for bank, b0, b1 in ((S0, 0, DIAG_SPLIT), (S1, DIAG_SPLIT, NBLK)):
                                out = ps[:, bank, 0:BLK * (b1 - b0)].rearrange("p (b t) -> p b t", t=BLK)
                                mm = pe.matmul(out[:, :, j:], const[:, a0:a0 + 128], e[:, b0:b1, :],
                                               start=(j == 0), stop=(j == 15))
                            mm.then_inc(pe_done, st.done("pe", f"gla diag {h} {j}"))
                    if s == "p vtok":
                        pe.wait_ge(dve_done, A("dve", f"evac {UIDX['cv', 2 * h + 1]} 0 1"))
                        if h > 0:
                            pe.wait_ge(act_done, A("act", f"gla oevac {h - 1}"))
                        for g, pair in enumerate(VTOK_PAIRS):
                            for c, sb in enumerate(pair):
                                a, n = SUPER[sb]
                                for i in range(2):
                                    mm = pe.transpose(ps[0:n, VTOK_BANKS[g], 256 * c + 128 * i:256 * c + 128 * i + 128],
                                                      pr[:, 2 + i, a:a + n], c_("ident"))
                            mm.then_inc(pe_done, st.done("pe", f"gla vtok {h} {g}"))
                    if s == "p far":
                        pe.wait_ge(dve_done, A("dve", f"gla far s {h}"))
                        pe.matmul(ps[0:BLK, T1, 0:BLK], kfar_s[:, :], qfar_s[:, :], start=True, stop=True,
                                  skip_group_check=True)
                        for i in range(7, 0, -1):
                            pe.wait_ge(dve_done, A("dve", f"gla far {h} {i}"))
                            kf = kfar_of(i).rearrange("p (b s) -> p b s", b=4)
                            qf = qfar[:, :].rearrange("p (b i t) -> p b i t", b=4, t=BLK)
                            for sb in range(4):
                                mm = pe.matmul(ps[0:16 * i, T0, 128 * sb + 16 * i:128 * sb + 16 * i + 16],
                                               kf[:, sb, :], qf[:, sb, i - 1, :], start=(i == 7 and sb == 0), stop=True,
                                               skip_group_check=True)
                            mm.then_inc(pe_done, st.done("pe", f"gla far {h} {i}"))
                    if s == "p ktok":
                        pe.wait_ge(dve_done, A("dve", f"gla kend {h}"))
                        pe.wait_ge(act_done, A("act", f"gla vtok {h}"))
                        for g, bank in ((0, M_), (1, O_)):
                            for i in range(3):
                                a, n = SUPER[3 * g + i]
                                mm = pe.transpose(ps[0:n, bank, 128 * i:128 * i + 128], kend[:, a:a + n], c_("ident"))
                            mm.then_inc(pe_done, st.done("pe", f"gla ktok {h} {g}"))
                    if s == "p kv":
                        pe.wait_ge(dve_done, A("dve", f"gla amat {h}"))
                        pe.wait_ge(act_done, A("act", f"gla ktok {h} 1"))
                        for sb in range(6):
                            a, n = SUPER[sb]
                            bank = (S0, S1, T0)[sb // 2]
                            mm = pe.matmul(ps[:, bank, 256 * (sb % 2):256 * (sb % 2) + 256], ktok[0:n, sb, :],
                                           vtok[0:n, sb, :], start=(sb % 2 == 0), stop=True, skip_group_check=True)
                        mm.then_inc(pe_done, st.done("pe", f"gla kv {h}"))
                    if s == "p o":
                        pe.wait_ge(dve_done, A("dve", f"gla state {h}"))
                        for vt in range(2):
                            for sb in range(6):
                                a, n = SUPER[sb]
                                if n == 128:
                                    dst = ps[:, (M_, O_)[vt], a:a + n]
                                else:
                                    dst = ps[:, T1, 48 * vt + a - SEQ:48 * vt + a - SEQ + n]
                                first = (sb == 1) or (vt == 0 and sb == 0)
                                pe.matmul(dst, vtok[0:n, sb, 128 * vt:128 * vt + 128], amat[0:n, a:a + n],
                                          start=first, stop=(sb == 0), skip_group_check=True)
                                if sb == 0:
                                    continue
                                mm = pe.matmul(dst, state[:, STATE_IN[sb], 128 * vt:128 * vt + 128],
                                               qe[:, a:a + n], start=False, stop=True, skip_group_check=True)
                        mm.then_inc(pe_done, st.done("pe", f"gla o {h}"))
                    if s == "p ms":
                        pe.wait_ge(dve_done, A("dve", f"gla sum {h}"))
                        pe.wait_ge(act_done, A("act", f"gla z {h + 1}" if h + 1 < C_HEADS else "prep a 0"))
                        for hf in range(2):
                            mm = pe.matmul(ps[:, S0 + hf, 0:HALF], c_("ones_v"), gsq[:, 0, H[hf]], start=True, stop=True)
                        mm.then_inc(pe_done, st.done("pe", f"gla ms {h}"))

                def prep_a(s):
                    if s in ("square", "load"):
                        return
                    pair = prep_pair(s).start
                    at_step = PREP_A.index(s)
                    if at_step >= 2:
                        e = prep_evac(PREP_A[at_step - 2])
                        pe.wait_ge(by_name[e], A(e, f"prep a {PREP_A[at_step - 2]}"))
                    if s == 0:
                        pe.wait_ge(dve_done, A("dve", f"gla state {C_HEADS - 1}"))
                    elif s == 1:
                        pe.wait_ge(act_done, A("act", f"gla oevac {C_HEADS - 1}"))
                    elif s == 2:
                        pe.wait_ge(act_done, A("act", f"gla rstd {C_HEADS - 1}"))
                    if s == 0:
                        pe.wait_ge(act_done, A("act", "ckv sq"))
                        for k in range(KL):
                            for hf in range(2):
                                mm = pe.matmul(ps[:, pair + hf, 0:HALF], c_("ones_v"), cksq[:, k, H[hf]],
                                               start=(k == 0), stop=(k == KL - 1))
                    elif s == 1:
                        for hf in range(2):
                            mm = pe.matmul(ps[0:96, pair + hf, 0:HALF], const[0:96, CONST["perm"][0]:CONST["perm"][0] + 96],
                                           kra[0:96, H[hf]], start=True, stop=True)
                    elif s in (2, 3):
                        u = UIDX["qr", s - 2]
                        pe.wait_ge(dve_done, A("dve", f"evac {u} 0 1"))
                        for hf in range(2):
                            mm = pe.matmul(ps[:, pair + hf, 0:HALF], c_("perm"), qr[:, s - 2, H[hf]],
                                           start=True, stop=True)
                    elif s in (4, 5, 6, 7):
                        if s == 4:
                            pe.wait_ge(dve_done, A("dve", "c 1"))
                            pe.wait_ge(a_loaded["w_uk"], 16)
                        for hf in range(2):
                            for k in range(KL):
                                mm = pe.matmul(ps[:, pair + hf, 0:HALF], wuk[:, k, 128 * (s - 4):128 * (s - 4) + 128],
                                               ckv[:, k, H[hf]], start=(k == 0), stop=(k == KL - 1))
                    elif s in (8, 9):
                        pe.wait_ge(a_loaded["a_ckv"], 16)
                        for i in range(2):
                            n = 2 * (s - 8) + i
                            for k in range(KL):
                                mm = pe.matmul(ps[:, pair + i, 0:CKEYS], wuk[:, k, 128 * n:128 * n + 128],
                                               cct[:, k, :], start=(k == 0), stop=(k == KL - 1))
                    else:
                        pe.wait_ge(a_loaded["w_uv"], 16)
                        for i, (src, a, n, _) in enumerate(VA_TILES[s - 10]):
                            for k in range(KL):
                                mm = pe.matmul(ps[0:n, pair + i, 0:512], src[:, k, a:a + n], wuv[:, k, :],
                                               start=(k == 0), stop=(k == KL - 1))
                    mm.then_inc(pe_done, st.done("pe", f"prep a {s}"))

                def scores(br, j):
                    _, t, i = JOBS[br][j]
                    if br == "a":
                        if j >= 1:
                            pe.wait_ge(dve_done, A("dve", f"a shift {j - 1}"))
                        if j == 0:
                            pe.wait_ge(a_loaded["a_kr"], 16)
                            for e, name in PREP_A_OVER:
                                pe.wait_ge({"act": act_done, "dve": dve_done, "pool": pool_done}[e], A(e, name))
                        for a in range(2):
                            h = 2 * t + a
                            r64, r32 = slice(64 * a, 64 * a + 64), slice(32 * (h % 4), 32 * (h % 4) + 32)
                            if i < 4:
                                qc, nk = slice(128 * i, 128 * i + 128), 128 * (i + 1)
                                pe.matmul(ps[:, S0 + a, 0:nk], qn[r64, t, qc], kn[r64, t, 0:nk], start=True, stop=False,
                                          skip_group_check=True)
                                pe.matmul(ps[:, S0 + a, 0:nk], qrot[r32, h // 4, qc], krot[r32, 0:nk], start=False, stop=True,
                                          skip_group_check=True)
                                mdst = ps[:, S0 + a, nk:nk + META] if i < 3 else ps[:, M_, 16 * a:16 * a + 16]
                                pe.matmul(mdst, qn[r64, t, qc], kn[r64, t, META0:META0 + META],
                                          start=(i == 3 and a == 0), stop=False, skip_group_check=True)
                                mm = pe.matmul(mdst, qr[r32, h // 4, qc],
                                               krot[r32, META0:META0 + META], start=False, stop=True, skip_group_check=True)
                                if i == 3 and a == 0:
                                    mm.then_inc(pe_done, st.done("pe"))
                                    pe.wait_ge(pe_done, st.count["pe"])
                            else:
                                qc = slice(META0, T)
                                for c0, n, key in ((0, CKEYS, kn_c[r64, t, :]), (CKEYS, MIXED, kn[r64, t, META0:T])):
                                    pe.matmul(ps[0:MIXED, S0 + a, c0:c0 + n], qn[r64, t, qc], key, start=(c0 == 0), stop=False,
                                              skip_group_check=True)
                                for c0, n, key, rope in ((0, PAST, kr_c[r32, 0:PAST], qrot), (288, DEC, krot[r32, SAMP0:T], qrot),
                                                         (256, META, kr_c[r32, PAST:CKEYS], qr),
                                                         (272, META, krot[r32, META0:SAMP0], qr)):
                                    mm = pe.matmul(ps[0:MIXED, S0 + a, c0:c0 + n], rope[r32, h // 4, qc], key, start=False,
                                                   stop=True, skip_group_check=True)
                    else:
                        if j >= 1:
                            pe.wait_ge(dve_done, A("dve", f"b bias {j - 1}"))
                        else:
                            pe.wait_ge(act_done, A("act", "b vtok"))
                            pe.wait_ge(dve_done, A("dve", "b vtok"))
                            pe.wait_ge(dve_done, A("dve", f"evac {UIDX['qb', 3]} 0 1"))
                            pe.wait_ge(b_loaded, 48)
                        r64 = slice(64 * t, 64 * t + 64)
                        for g in range(B_G):
                            if i < 4:
                                c0 = 208 * (g % 2)
                                qc = slice(128 * i, 128 * i + 128)
                                parts = [(0, 192, kb[r64, 128 * i - 64:128 * i + 128])] if i > 0 else [(64, 128, kb[r64, qc])]
                                parts.append((192, META, kb[r64, META0:SAMP0]))
                                rows = P
                            else:
                                c0 = 192 * (g % 2)
                                qc = slice(META0, T)
                                parts = [(0, WIN + META, kb_c[r64, :]), (WIN + META, MIXED, kb[r64, META0:T])]
                                rows = MIXED
                            for n_, (o, w, key) in enumerate(parts):
                                mm = pe.matmul(ps[0:rows, S0 + g // 2, c0 + o:c0 + o + w], qb[r64, g, qc], key,
                                               start=(g % 2 == 0 and n_ == 0), stop=True, skip_group_check=True)
                    mm.then_inc(pe_done, st.done("pe", f"{br} scores {j}"))

                def turn(br, j):
                    _, t, i = JOBS[br][j]
                    pe.wait_ge(pool_done, A("pool", f"{br} prob {j}"))
                    if j >= 1:
                        pe.wait_ge(dve_done, A("dve", f"{br} turned {j - 1}"))
                    if j >= 2:
                        pe.wait_ge(dve_done, A("dve", f"{br} o {j - 2}"))
                    nk = key_count(br, i)
                    pb = prob_view(br, j)
                    if br == "a":
                        for a in range(2):
                            if i < 4:
                                for kt in range(i + 1):
                                    pe.transpose(ps[:, T0 + a, 128 * kt:128 * kt + 128], pb[:, a, 128 * kt:128 * kt + 128],
                                                 c_("ident"))
                                mm = pe.transpose(ps[0:META, O_, 256 + 128 * a:384 + 128 * a],
                                                  pb[:, a, nk - META:nk], c_("ident"))
                            else:
                                idn = const[0:MIXED, 0:MIXED]
                                for n_, (c0, w) in enumerate(((0, 128), (128, 128), (CKEYS, MIXED), (PAST, META))):
                                    mm = pe.transpose(ps[0:w, T0 + a, 48 * n_:48 * n_ + 48], pb[0:MIXED, a, c0:c0 + w], idn)
                    else:
                        for g in range(B_G):
                            if i < 4:
                                o = 0 if i > 0 else -64
                                c = slice(128 * g, 128 * g + 128)
                                if i > 0:
                                    pe.transpose(ps[0:64, T1, c], pb[:, g, 0:64], c_("ident"))
                                pe.transpose(ps[:, T0, c], pb[:, g, 64 + o:192 + o], c_("ident"))
                                mm = pe.matmul(ps[64:80, T1, c], pb[:, g, 192 + o:208 + o], c_("ident"), start=True, stop=True,
                                               skip_group_check=True)
                            else:
                                idn = const[0:MIXED, 0:MIXED]
                                c = slice(48 * g, 48 * g + 48)
                                pe.transpose(ps[:, T0, c], pb[0:MIXED, g, 0:WIN], idn)
                                pe.transpose(ps[0:MIXED, T1, c], pb[0:MIXED, g, 144:192], idn)
                                mm = pe.transpose(ps[0:META, M_, c], pb[0:MIXED, g, 128:144], idn)
                    mm.then_inc(pe_done, st.done("pe", f"{br} turn {j}"))

                def values(br, j):
                    _, t, i = JOBS[br][j]
                    pe.wait_ge(dve_done, A("dve", f"{br} turned {j}"))
                    if j >= 1:
                        pe.wait_ge(dve_done, A("dve", f"{br} o {j - 1}"))
                    if br == "a":
                        for a in range(2):
                            hc = slice(64 * (2 * t + a), 64 * (2 * t + a) + 64)
                            if i < 4:
                                dst = ps[64 * a:64 * a + 64, O_, 0:128]
                                for kt in range(i + 1):
                                    pe.matmul(dst, va[:, kt, hc], ptf[:, a, 128 * kt:128 * kt + 128],
                                              start=(kt == 0), stop=False)
                                mm = pe.matmul(dst, va_mix[0:META, hc], ptm[:, 128 * a:128 * a + 128], start=False, stop=True)
                            else:
                                dst = ps[64 * a:64 * a + 64, O_, 0:MIXED]
                                pe.matmul(dst, va_c[:, 0, hc], ptf[:, a, 0:48], start=True, stop=False)
                                pe.matmul(dst, va_c[:, 1, hc], ptf[:, a, 48:96], start=False, stop=False)
                                pe.matmul(dst, va_mix[:, hc], ptf[0:MIXED, a, 96:144], start=False, stop=False)
                                mm = pe.matmul(dst, va_cm[:, hc], ptf[0:META, a, 144:192], start=False, stop=True)
                    else:
                        hc = slice(64 * t, 64 * t + 64)
                        if i < 4:
                            dst = ps[64 * t:64 * t + 64, O_, 0:512]
                            pe.matmul(dst, v_own[:, i, hc], ptf[:, 0, :], start=True, stop=False)
                            r = slice(0 if i > 0 else 64, 80)
                            mm = pe.matmul(dst, v_prev[r, max(i - 1, 0), hc], ptf[r, 1, :], start=False, stop=True)
                        else:
                            dst = ps[64 * t:64 * t + 64, O_, 0:192]
                            pe.matmul(dst, vb_c[:, hc], ptf[:, 0, 0:192], start=True, stop=False)
                            pe.matmul(dst, v_mix[:, hc], ptf[0:MIXED, 1, 0:192], start=False, stop=False)
                            mm = pe.matmul(dst, vb_cm[:, hc], ptm[:, 0:192], start=False, stop=True)
                    mm.then_inc(pe_done, st.done("pe", f"{br} values {j}"))

                def prep_b(s):
                    if s == 0:
                        pe.wait_ge(act_done, A("act", f"evac {UIDX['vb', 0]} 0 1"))
                        pe.wait_ge(dve_done, A("dve", f"a o {len(jobs) - 1}"))
                        for i in range(4):
                            pe.transpose(ps[:, T0, 128 * i:128 * i + 128], vb[:, 128 * i:128 * i + 128], c_("ident"))
                        for i in range(1, 4):
                            pe.transpose(ps[0:64, T1, 128 * i - 128:128 * i], vb[:, 128 * i - 64:128 * i], c_("ident"))
                        for i in range(3):
                            pe.matmul(ps[64:80, T1, 128 * i:128 * i + 128], vb[:, META0:SAMP0], c_("ident"), start=True, stop=True,
                                      skip_group_check=True)
                        mm = pe.transpose(ps[0:MIXED, M_, 0:128], vb[:, META0:T], c_("ident"))
                        mm.then_inc(pe_done, st.done("pe", "b vtok"))

                for step in order:
                    if step[0] == "dense":
                        dense_unit(step[1])
                    elif step[0] == "norm":
                        norm(step[1])
                    elif step[0] == "mean":
                        mean(step[1])
                    elif step[0] == "gla":
                        gla(step[1], step[2])
                    elif step[0] == "prep_a":
                        prep_a(step[1])
                    elif step[0] == "prep_b":
                        prep_b(step[1])
                    elif step[0] == "att":
                        br, j = step[1], step[2]
                        n = len(JOBS[br])
                        if j < n:
                            scores(br, j)
                        if 1 <= j <= n:
                            turn(br, j - 1)
                        if j >= 2:
                            values(br, j - 2)

            @block.scalar
            def _(act):
                def store(dst, src, e, name):
                    act.wait_ge({"act": act_done, "dve": dve_done}[e], A(e, name))
                    act.dma_start(dst, src).then_inc(stored, 16)
                    count["stored"] += 16

                count = {"stored": 0}

                def w_hi(u):
                    slot = u % WSLOTS
                    if u >= WSLOTS:
                        act.wait_ge(w_loaded[slot], 16 * (u // WSLOTS))
                    elif u == 2:
                        act.wait_ge(w2_first, 16)
                    act.activation(whi[slot][:, :], wraw[slot][:, :], ACT.Copy).then_inc(act_done, st.done("act", f"w hi {u}"))

                def round_tile(dst, src, wait, name):
                    act.wait_ge(*wait)
                    act.activation(dst, src, ACT.Copy).then_inc(act_done, st.done("act", name))

                def link(ins, name=None):
                    ins.then_inc(act_done, st.done("act", name))
                    act.wait_ge(act_done, st.count["act"])

                def evac(u):
                    kind, n = UNITS[u]
                    if kind.startswith("gate"):
                        act.wait_ge(*sig_free(kind[-1], n))
                        for hf in range(2):
                            s = sig[:, n % 2, H[hf]]
                            act.wait_ge(pe_done, A("pe", f"half {u} 0 {hf}"))
                            link(act.activation(s, dps[bank_of[u, 0, hf]][:, 0:HALF], ACT.Abs))
                            link(act.activation(s, s, ACT.Exp, scale=-1.0))
                            act.activation(s, s, ACT.Ln, bias=1.0).then_inc(act_done, st.done("act", f"gate ln {u} {hf}"))
                            act.wait_ge(dve_done, A("dve", f"evac {u} 0 {hf}"))
                            act.activation(s, s, ACT.Exp).then_inc(act_done, st.done("act", f"sig {u} {hf}"))
                        return
                    if kind == "ff2" and summed(u):
                        for hf in range(2):
                            if n == 24 and hf == 0:
                                act.wait_ge(pe_done, A("pe", f"dense {UIDX['ff2', 23]}"))
                            act.wait_ge(dve_done, A("dve", f"evac {u} 0 {hf}"))
                            square(u, hf, facc[:, n - 24, H[hf]])
                    if evac_engine(kind) != "act":
                        return
                    for hf in range(2):
                        src = dps[bank_of[u, 0, hf]][:, 0:HALF]
                        act.wait_ge(pe_done, A("pe", f"half {u} 0 {hf}"))
                        if kind == "ck":
                            if hf == 0 and n >= 2:
                                act.wait_ge(dve_done, A("dve", f"gla kend {n - 2}"))
                            ins = act.activation(cproj[n % 2][:, 1, H[hf]], src, ACT.Copy)
                        elif kind == "cg":
                            h, i = n // 2, n % 2
                            if hf == 0 and h >= 2:
                                act.wait_ge(dve_done, A("dve", f"gla silu {h - 2}"))
                            ins = act.activation(cproj[h % 2][:, 4 + i, H[hf]], src, ACT.Copy)
                        elif kind == "vb":
                            if hf == 0:
                                act.wait_ge(dve_done, A("dve", f"a o {len(jobs) - 1}"))
                                act.wait_ge(pe_done, A("pe", f"a values {len(jobs) - 1}"))
                            ins = act.activation(vb[:, H[hf]], src, ACT.Copy)
                        elif kind == "out":
                            if hf == 0 and n == 0:
                                act.wait_ge(pe_done, A("pe", f"dense {UIDX['up_c', KD - 1]}"))
                            square(u, hf, src)
                            ins = act.activation(mix[:, n, H[hf]], src, ACT.Copy)
                        elif kind == "ff1":
                            g = n // 8
                            if hf == 0:
                                if g >= 2 and n % 8 == 0:
                                    act.wait_ge(pe_done, A("pe", f"dense {UIDX['ff2', 8 * (g - 2) + 7]}"))
                                if g == 0 and n == 0:
                                    act.wait_ge(dve_done, A("dve", "h raw pre_mlp 7"))
                                    act.wait_ge(pe_done, A("pe", "ms pre_mlp"))
                                if g == 1 and n == 8:
                                    act.wait_ge(pe_done, A("pe", f"dense {UIDX['up_b', 6]}"))
                            ins = act.activation(hid[g % 2][0][:, n % 8, H[hf]], src, ACT.Relu)
                        ins.then_inc(act_done, st.done("act", f"evac {u} 0 {hf}"))

                def after_evac(u):
                    kind, n = UNITS[u]
                    if kind == "ff1":
                        g = n // 8
                        round_tile(hid[g % 2][2][:, n % 8, :], hid[g % 2][0][:, n % 8, :],
                                   (dve_done, A("dve", f"hid {n}")), f"hid hi {n}")

                def square(u, hf, src):
                    which, n = summed(u)
                    if n >= 3:
                        act.wait_ge(dve_done, A("dve", f"sum {which} {n - 2} {hf}"))
                    dst = sqsum if n == 0 else sqpart[n % 2]
                    act.activation(dst[:, H[hf]], src, ACT.Square).then_inc(act_done, st.done("act", f"sq {which} {n} {hf}"))

                def to_rstd(which, pair):
                    act.wait_ge(pe_done, A("pe", f"ms {which}"))
                    link(act.activation(rstd[:, :].rearrange("p (a n) -> p a n", a=2), ps[:, pair, 0:HALF], ACT.Ln,
                                        bias=eps[:, 0:1]))
                    act.activation(rstd[:, :], rstd[:, :], ACT.Exp, scale=-0.5).then_inc(act_done, st.done("act", f"rstd {which}"))

                def norm(which):
                    to_rstd(which, PAIRS[0])

                def ahead_hi(slot):
                    act.wait_ge(w_ahead[slot], 16)
                    act.activation(whi[slot][:, :], wraw[slot][:, :], ACT.Copy).then_inc(act_done, st.done("act", f"ahead hi {slot}"))

                def mean(which):
                    after = "post_mix" if which == "pre_mlp" else "post_mlp"
                    for k in range(KD):
                        e = x_engine(k)
                        act.wait_ge(by_name[e], A(e, f"x {after} {k}"))
                        act.activation(sq[:, k, :], x[:, k, :], ACT.Square).then_inc(act_done, st.done("act", f"sq {which} {k}"))
                        if which == "next" and k in (1, 4):
                            ahead_hi(1 if k == 1 else 0)
                    to_rstd(which, PAIRS[1])
                    if which == "next":
                        act.wait_ge(act_done, st.count["act"])

                def tokens(which):
                    name = "h" if which == "pre_mix" else "h2"
                    if which == "pre_mix":
                        act.dma_start(io["x_spill"], x[:, :, :]).then_inc(spilled, 16)
                    for k in range(KD):
                        round_tile(h_hi[:, k, :], h_raw[:, k, :], (dve_done, A("dve", f"h raw {which} {k}")), f"{name} hi {k}")

                def gla(h, s):
                    pr = cproj[h % 2]
                    if s == "v decay":
                        if h > 0:
                            act.wait_ge(dve_done, A("dve", f"gla state {h - 1}"))
                            act.wait_ge(pe_done, A("pe", f"gla o {h - 1}"))
                            act.wait_ge(pe_done, A("pe", f"gla diag {h - 1} 15"))
                        act.dma_start(state[:, 6, :], io["state"][bass.ds(l * C_HEADS + h, 1), :, :].rearrange("a p n -> (a p) n")).then_inc(state_loaded, 16)
                        act.wait_ge(pe_done, A("pe", f"gla z {h}"))
                        zz = zlog[:, :]
                        link(act.activation(zz.rearrange("p (a n) -> p a n", a=2), ps[:, S0:S1 + 1, 0:HALF], ACT.Identity,
                                            bias=p_("b_alpha", h)), f"gla z {h}")
                        link(act.activation(ztmp[:, :], zz, ACT.Abs))
                        link(act.activation(ztmp[:, :], ztmp[:, :], ACT.Exp, scale=-1.0))
                        act.activation(ztmp[:, :], ztmp[:, :], ACT.Ln, bias=1.0).then_inc(act_done, st.done("act", f"gla ln {h}"))
                    if s.startswith("v diag"):
                        for j in range(4 * int(s[-1]), 4 * int(s[-1]) + 4):
                            e = ediag_of(j)
                            act.wait_ge(pool_done, A("pool", f"gla d {h} {j}"))
                            act.activation(e, e, ACT.Exp, scale=1.0 / 16).then_inc(act_done, st.done("act", f"gla e {h} {j}"))
                    if s == "v vtok":
                        act.wait_ge(spilled, 16)
                        if h > 0:
                            act.wait_ge(pe_done, A("pe", f"gla o {h - 1}"))
                        for g, pair in enumerate(VTOK_PAIRS):
                            act.wait_ge(pe_done, A("pe", f"gla vtok {h} {g}"))
                            if g < 2:
                                act.activation(vtok[:, pair[0]:pair[0] + 2, :], ps[:, VTOK_BANKS[g], :].rearrange("p (c n) -> p c n", c=2),
                                               ACT.Copy).then_inc(act_done, st.done("act"))
                            else:
                                for c, sb in enumerate(pair):
                                    n = SUPER[sb][1]
                                    act.activation(vtok[0:n, sb, :], ps[0:n, T1, 256 * c:256 * c + 256], ACT.Copy
                                                   ).then_inc(act_done, st.done("act", f"gla vtok {h}" if c == 1 else None))
                    if s == "v farq":
                        act.wait_ge(pool_done, A("pool", f"gla far q {h}"))
                        act.activation(qfar[:, :], qfar[:, :], ACT.Exp, scale=1.0 / 16).then_inc(act_done, st.done("act"))
                        act.activation(qfar_s[:, :], qfar_s[:, :], ACT.Exp, scale=1.0 / 16).then_inc(act_done, st.done("act"))
                        act.activation(kfar_s[:, :], kfar_s[:, :], ACT.Exp, scale=1.0 / 16).then_inc(act_done, st.done("act", f"gla far q {h}"))
                    if s == "v far":
                        for i in range(7, 0, -1):
                            act.wait_ge(pool_done, A("pool", f"gla far {h} {i}"))
                            kf = kfar_of(i)
                            act.activation(kf, kf, ACT.Exp, scale=1.0 / 16).then_inc(act_done, st.done("act", f"gla far {h} {i}"))
                    if s == "v kend":
                        act.wait_ge(dve_done, A("dve", f"gla scan {h}"))
                        if h > 0:
                            act.wait_ge(dve_done, A("dve", f"gla state {h - 1}"))
                        act.activation(ebl[:, :], bcum[:, :], ACT.Exp, scale=1.0 / 16).then_inc(act_done, st.done("act", f"gla eb {h}"))
                        act.wait_ge(pool_done, A("pool", f"gla kend {h}"))
                        act.activation(kend[:, :], kend[:, :], ACT.Exp, scale=1.0 / 16).then_inc(act_done, st.done("act", f"gla kend {h}"))
                    if s == "v ktok":
                        for g in range(2):
                            bank = (M_, O_)[g]
                            act.wait_ge(pe_done, A("pe", f"gla ktok {h} {g}"))
                            for i in range(3):
                                n = SUPER[3 * g + i][1]
                                ins = act.activation(ktok[0:n, 3 * g + i, :], ps[0:n, bank, 128 * i:128 * i + 128], ACT.Copy)
                                ins.then_inc(act_done, st.done("act", f"gla ktok {h} {g}" if i == 2 else None))
                    if s == "v silu":
                        act.wait_ge(act_done, A("act", f"evac {UIDX['cg', 2 * h + 1]} 0 1"))
                        if h >= 1:
                            act.wait_ge(dve_done, A("dve", f"gla out {h - 1} 1"))
                        link(act.activation(gsig[:, :, :], pr[:, 4:6, :], ACT.Abs))
                        link(act.activation(gsig[:, :, :], gsig[:, :, :], ACT.Exp, scale=-1.0))
                        act.activation(gsig[:, :, :], gsig[:, :, :], ACT.Ln, bias=1.0).then_inc(act_done, st.done("act", f"gla gate ln {h}"))
                        act.wait_ge(dve_done, A("dve", f"gla gate {h}"))
                        act.activation(gsig[:, :, :], gsig[:, :, :], ACT.Exp).then_inc(act_done, st.done("act", f"gla gate {h}"))
                    if s == "v o":
                        act.wait_ge(pe_done, A("pe", f"gla o {h}"))
                        act.wait_ge(spilled, 16)
                        if h > 0:
                            act.wait_ge(dve_done, A("dve", f"gla out {h - 1} 1"))
                        act.activation(oh[:, :, 0:SEQ], ps[:, M_::3, :], ACT.Copy).then_inc(act_done, st.done("act"))
                        act.activation(oh[:, :, SEQ:T], ps[:, T1, 0:96].rearrange("p (a n) -> p a n", a=2), ACT.Copy
                                       ).then_inc(act_done, st.done("act", f"gla oevac {h}"))
                        act.wait_ge(act_done, st.count["act"])
                        if h > 0:
                            act.wait_ge(pe_done, A("pe", f"gla ms {h - 1}"))
                        if h == C_HEADS - 1:
                            act.wait_ge(pe_done, A("pe", "prep a 0"))
                        act.activation(gsq[:, :, :], oh[:, :, :], ACT.Square).then_inc(act_done, st.done("act", f"gla sq {h}"))
                    if s == "v out":
                        act.wait_ge(pe_done, A("pe", f"gla ms {h}"))
                        if h == C_HEADS - 1:
                            act.wait_ge(dve_done, A("dve", "c 1"))
                        link(act.activation(rstd[:, :].rearrange("p (a n) -> p a n", a=2), ps[:, S0:S1 + 1, 0:HALF], ACT.Ln,
                                            bias=eps[:, 0:1]))
                        act.activation(rstd[:, :], rstd[:, :], ACT.Exp, scale=-0.5).then_inc(act_done, st.done("act", f"gla rstd {h}"))
                        for which, slot in (("p_state", 5), ("s_state", 7)):
                            act.wait_ge(dve_done, A("dve", f"gla state {h}"))
                            act.dma_start(io[which][bass.ds(l * C_HEADS + h, 1), :, :].rearrange("a p n -> (a p) n"), state[:, slot, :]).then_inc(stored, 16)
                            count["stored"] += 16
                        for i in range(2):
                            k = 2 * h + i
                            round_tile(oc_hi[:, k, :], oc_raw[:, k, :], (dve_done, A("dve", f"gla out {h} {i}")), f"oc hi {k}")

                def prep_a(s):
                    if s == "load":
                        for e, name in (("dve", "gla out 3 1"), ("pe", "gla ms 3"), ("pe", "gla o 3")):
                            act.wait_ge({"dve": dve_done, "pe": pe_done}[e], A(e, name))
                        act.wait_ge(stored, 32 * C_HEADS)
                        for dst, name in ((wuk, "w_uk"), (cct, "a_ckv"), (wuv, "w_uv")):
                            act.dma_start(dst[:, :, :], io[name][bass.ds(l, 1)].rearrange("a (k p) n -> p (a k) n", p=P)
                                          ).then_inc(a_loaded[name], 16)
                        act.dma_start(kr_c[:, :], io["a_kr"][bass.ds(l, 1)].rearrange("a p n -> (a p) n")).then_inc(a_loaded["a_kr"], 16)
                    if s == 2:
                        store(io["c_out"][bass.ds(l, 1)].rearrange("a (k p) n -> p (a k) n", p=P), ckv[:, :, :], "dve", "c 1")
                        store(io["kr_out"][bass.ds(l, 1)].rearrange("a p n -> (a p) n"), krot[0:32, :], "dve", "krot")
                    if s == "square":
                        act.wait_ge(dve_done, A("dve", f"evac {UIDX['ckv', 1]} 0 1"))
                        act.wait_ge(pe_done, A("pe", f"gla ms {C_HEADS - 2}"))
                        act.wait_ge(spilled, 16)
                        act.activation(cksq[:, :, :], ckv[:, :, :], ACT.Square).then_inc(act_done, st.done("act", "ckv sq"))
                    if s == 0:
                        act.wait_ge(pe_done, A("pe", "prep a 0"))
                        link(act.activation(rstd[:, :].rearrange("p (a n) -> p a n", a=2), ps[:, 0:2, 0:HALF], ACT.Ln,
                                            bias=eps[:, 0:1]), "prep a 0")
                        act.activation(rstd[:, :], rstd[:, :], ACT.Exp, scale=-0.5).then_inc(act_done, st.done("act", "c rstd"))
                    if s not in ("square", "load", 0) and prep_evac(s) == "act":
                        act.wait_ge(pe_done, A("pe", f"prep a {s}"))
                        pair = prep_pair(s)
                        if s < 8:
                            act.activation(kn[:, s - 4, :].rearrange("p (a n) -> p a n", a=2), ps[:, pair, 0:HALF], ACT.Copy
                                           ).then_inc(act_done, st.done("act", f"prep a {s}"))
                        elif s < 10:
                            act.activation(kn_c[:, 2 * (s - 8):2 * (s - 8) + 2, :], ps[:, pair, 0:CKEYS], ACT.Copy
                                           ).then_inc(act_done, st.done("act", f"prep a {s}"))
                        else:
                            for i, (_, _, n, dst) in enumerate(VA_TILES[s - 10]):
                                act.activation(dst, ps[0:n, pair.start + i, :], ACT.Copy).then_inc(
                                    act_done, st.done("act", f"prep a {s}" if i == len(VA_TILES[s - 10]) - 1 else None))

                def att(br, j):
                    n = len(JOBS[br])
                    if j < n:
                        _, t, i = JOBS[br][j]
                        pb = prob_view(br, j)
                        nk = key_count(br, i)
                        rows = P if i < 4 else MIXED
                        act.wait_ge(dve_done, A("dve", f"{br} shift {j}"))
                        k = 2 if br == "a" else 4
                        w = nk if br == "a" else nk + 1
                        sc = A_SCALE if br == "a" else B_SCALE
                        for a in range(k):
                            act.activation(pb[0:rows, a, 0:w], pb[0:rows, a, 0:w], ACT.Exp, scale=sc,
                                           accum_out=stat[0:rows, j % 2, 8 + a:9 + a]
                                           ).then_inc(act_done, st.done("act", f"{br} exp {j}" if a == k - 1 else None))
                    if br == "a" and j >= 6 and (j - 6) % 5 == 0:
                        t = (j - 6) // 5
                        if t == 0:
                            act.wait_ge(pe_done, A("pe", "prep a 13"))
                            act.wait_ge(stored, 32 * C_HEADS + 32)
                        round_tile(oa_hi[:, t, :], oa_raw[:, t, :], (dve_done, A("dve", f"a o {5 * t + 4}")), f"oa hi {t}")
                    if br == "b" and j >= 7:
                        i = j - 7
                        round_tile(ob_hi[:, :, BLOCKS[i]], ob_raw[:, :, BLOCKS[i]], (dve_done, A("dve", f"b o {j - 2}")), f"ob hi {i}")

                for step in order:
                    if step[0] == "dense":
                        evac(step[1])
                        after_evac(step[1])
                        if step[1] + 2 < NU:
                            w_hi(step[1] + 2)
                    elif step[0] == "norm":
                        norm(step[1])
                    elif step[0] == "mean":
                        mean(step[1])
                    elif step[0] == "tokens":
                        tokens(step[1])
                    elif step[0] == "gla":
                        gla(step[1], step[2])
                    elif step[0] == "prep_a":
                        prep_a(step[1])
                    elif step[0] == "prep_b":
                        if step[1] == 0:
                            act.wait_ge(pe_done, A("pe", f"a values {len(jobs) - 1}"))
                            for dst, name in ((kb_c, "b_k"), (vb_c, "b_v"), (vb_cm, "b_vm")):
                                act.dma_start(dst[:, :], io[name][bass.ds(l, 1)].rearrange("a p n -> (a p) n")).then_inc(b_loaded, 16)
                            for name, src in (("kw_out", "b_kw"), ("vw_out", "b_vw")):
                                act.dma_start(io[name][bass.ds(l, 1)].rearrange("a p n -> (a p) n")[:, 0:WIN - DEC],
                                               io[src][bass.ds(l, 1)].rearrange("a p n -> (a p) n")[:, DEC:WIN]).then_inc(stored, 16)
                                count["stored"] += 16
                            store(io["kw_out"][bass.ds(l, 1)].rearrange("a p n -> (a p) n")[:, WIN - DEC:WIN], kb[:, SAMP0:T], "dve", f"evac {UIDX['kb', 0]} 0 1")
                            store(io["vw_out"][bass.ds(l, 1)].rearrange("a p n -> (a p) n")[:, WIN - DEC:WIN], vb[:, SAMP0:T], "act", f"evac {UIDX['vb', 0]} 0 1")
                            store(io["kb_out"][bass.ds(l, 1)].rearrange("a p n -> (a p) n"), kb[:, 384:T], "dve", f"evac {UIDX['kb', 0]} 0 1")
                            store(io["vb_out"][bass.ds(l, 1)].rearrange("a p n -> (a p) n"), vb[:, 384:T], "act", f"evac {UIDX['vb', 0]} 0 1")
                        if step[1] == 1:
                            act.wait_ge(pe_done, A("pe", "b vtok"))
                            act.activation(v_own[:, :, :].rearrange("p a n -> p (a n)"), ps[:, T0, :], ACT.Copy).then_inc(act_done, st.done("act", "b vtok"))
                    elif step[0] == "att":
                        att(step[1], step[2])
                    elif step[0] == "split_y":
                        act.wait_ge(pe_done, A("pe", f"dense {UIDX['gate_b', 7]}"))
                        for k in Y_SPLIT[step[1]]:
                            e = y_engine("b", k)
                            round_tile(h_hi[:, k, :], y[:, k, :], (by_name[e], A(e, f"y b {k}")), f"y hi {k}")
                        if step[1] == 1:
                            act.wait_ge(pool_done, A("pool", "y lo 5"))
                            act.wait_ge(dve_done, A("dve", f"y lo {KD - 1}"))
                            act.wait_ge(spilled, 16)
                            act.dma_start(x[:, :, :], io["x_spill"]).then_inc(x_back, 16)

                act.wait_ge(stored, count["stored"])

            @block.vector
            def _(dve):
                def link(ins, name=None):
                    ins.then_inc(dve_done, st.done("dve", name))
                    dve.wait_ge(dve_done, st.count["dve"])

                def add_square(u, hf):
                    which, n = summed(u)
                    dve.wait_ge(act_done, A("act", f"sq {which} {n} {hf}"))
                    if n >= 2:
                        dve.wait_ge(dve_done, A("dve", f"sum {which} {n - 1} {hf}"))
                    if n >= 1:
                        dve.tensor_tensor(sqsum[:, H[hf]], sqsum[:, H[hf]], sqpart[n % 2][:, H[hf]], ALU.add
                                          ).then_inc(dve_done, st.done("dve", f"sum {which} {n} {hf}"))

                def evac(u, outs=None):
                    kind, n = UNITS[u]
                    if kind == "out":
                        for hf in range(2):
                            add_square(u, hf)
                    if kind == "ff1":
                        t = hid[n // 8 % 2][0][:, n % 8, :]
                        dve.wait_ge(act_done, A("act", f"evac {u} 0 1"))
                        dve.tensor_tensor(t, t, t, ALU.mult).then_inc(dve_done, st.done("dve", f"hid {n}"))
                    if evac_engine(kind) != "dve":
                        return
                    for o in (range(outs_of(kind)[0]) if outs is None else outs):
                        for hf in range(2):
                            src = dps[bank_of[u, o, hf]][:, 0:HALF]
                            dve.wait_ge(pe_done, A("pe", f"half {u} {o} {hf}"))
                            c = H[hf]
                            if kind.startswith("gate"):
                                dve.wait_ge(act_done, A("act", f"gate ln {u} {hf}"))
                                s = sig[:, n % 2, c]
                                ins = dve.scalar_tensor_tensor(s, src, 0.0, s, ALU.min, ALU.subtract)
                            elif kind == "kralr":
                                ins = dve.tensor_copy(kra[0:112, c], src[0:112, :])
                            elif kind == "cq":
                                if hf == 0 and n >= 2:
                                    dve.wait_ge(dve_done, A("dve", f"gla qe {n - 2}"))
                                ins = dve.tensor_scalar(cproj[n % 2][:, 0, c], src, float(C_DK ** -0.5), None, ALU.mult)
                            elif kind == "cv":
                                h, i = n // 2, n % 2
                                if hf == 0 and h >= 2:
                                    dve.wait_ge(pe_done, A("pe", f"gla vtok {h - 2} 2"))
                                ins = dve.tensor_copy(cproj[h % 2][:, 2 + i, c], src)
                            elif kind in ("ckv", "qr", "qn"):
                                if hf == 0:
                                    dve.wait_ge(pe_done, A("pe", f"gla ms {C_HEADS - 1 if kind == 'qr' else C_HEADS - 2}"))
                                dst = {"ckv": ckv, "qr": qr, "qn": qn}[kind]
                                ins = dve.tensor_copy(dst[:, n, c], src)
                            elif kind == "kb":
                                if hf == 0:
                                    dve.wait_ge(pe_done, A("pe", f"a values {len(jobs) - 1}"))
                                    dve.wait_ge(stored, 32 * C_HEADS + 32)
                                ins = dve.tensor_copy(kb[:, c], src)
                            elif kind == "qb":
                                ins = dve.tensor_copy(qb[:, n, c], src)
                            elif kind == "up_c":
                                if n == 0 and hf == 0:
                                    dve.wait_ge(pe_done, A("pe", f"gla ms {C_HEADS - 1}"))
                                dve.wait_ge(act_done, A("act", f"sig {u - 1} {hf}"))
                                ins = dve.tensor_tensor(y[:, n, c], sig[:, n % 2, c], src, ALU.mult)
                            elif kind in ("up_a", "up_b"):
                                dve.wait_ge(act_done, A("act", f"sig {UIDX['gate_' + kind[-1], n + o]} {hf}"))
                                ins = dve.tensor_tensor(sig[:, o, c], sig[:, o, c], src, ALU.mult)
                            elif kind == "ff2":
                                g, m = n // 8, n % 8
                                if g == 0:
                                    if m == 0 and hf == 0:
                                        dve.wait_ge(stored, 32 * C_HEADS + 32 + 96)
                                    ins = dve.tensor_copy(facc[:, m, c], src)
                                else:
                                    if hf == 0:
                                        dve.wait_ge(dve_done, A("dve", f"evac {UIDX['ff2', n - 8]} 0 1"))
                                    ins = dve.tensor_tensor(facc[:, m, c], facc[:, m, c], src, ALU.add)
                            ins.then_inc(dve_done, st.done("dve", f"evac {u} {o} {hf}"))
                            if summed(u):
                                add_square(u, hf)
                    for o in range(outs_of(kind)[0] if outs != [0] else 0):
                        if kind in ("up_a", "up_b") and y_engine(kind[-1], n + o) == "dve":
                            dve.wait_ge(dve_done, A("dve", f"evac {u} {o} 1"))
                            dve.wait_ge(pool_done, A("pool", f"y a {n + o}"))
                            dve.tensor_tensor(y[:, n + o, :], y[:, n + o, :], sig[:, o, :], ALU.add
                                              ).then_inc(dve_done, st.done("dve", f"y b {n + o}"))

                def norm(which):
                    src = norm_src[which]
                    dve.wait_ge(act_done, A("act", f"rstd {which}"))
                    if which == "post_mix":
                        dve.wait_ge(x_back, 16)
                        for hf in range(2):
                            dve.wait_ge(act_done, A("act", f"evac {UIDX['out', 7]} 0 {hf}"))
                    for k in range(KD):
                        t = src[:, k, :]
                        dve.scalar_tensor_tensor(t, t, p_("g_" + which, k), rstd[:, :], ALU.mult, ALU.mult
                                                 ).then_inc(dve_done, st.done("dve", f"nrm {which} {k}"))
                        if x_engine(k) == "dve":
                            dve.wait_ge(dve_done, A("dve", f"nrm {which} {k}"))
                            dve.tensor_tensor(x[:, k, :], x[:, k, :], t, ALU.add).then_inc(dve_done, st.done("dve", f"x {which} {k}"))

                def tokens(which):
                    name = "h" if which == "pre_mix" else "h2"
                    if which == "pre_mlp":
                        dve.wait_ge(act_done, A("act", f"rstd {which}"))
                        dve.wait_ge(pe_done, A("pe", f"dense {UIDX['out', KD - 1]}"))
                    def lo(k):
                        dve.wait_ge(act_done, A("act", f"{name} hi {k}"))
                        dve.tensor_tensor(h_lo[:, k, :], h_raw[:, k, :], h_hi[:, k, :].bitcast(F32), ALU.subtract
                                          ).then_inc(dve_done, st.done("dve", f"{name} lo {k}"))
                    for k in range(KD):
                        g = g_pre_mix[:, k:k + 1] if which == "pre_mix" else p_("g_" + which, k)
                        if which == "pre_mlp":
                            e = x_engine(k)
                            dve.wait_ge(by_name[e], A(e, f"x post_mix {k}"))
                        dve.scalar_tensor_tensor(h_raw[:, k, :], x[:, k, :], g, rstd[:, :], ALU.mult, ALU.mult
                                                 ).then_inc(dve_done, st.done("dve", f"h raw {which} {k}"))
                        if k > 0 and lo_engine(name, k - 1) == "dve":
                            lo(k - 1)
                    lo(KD - 1)

                def gla(h, s):
                    pr = cproj[h % 2]
                    q, kk = pr[:, 0, :], pr[:, 1, :]
                    q3 = q.rearrange("p (b t) -> p b t", t=BLK)
                    k3 = kk.rearrange("p (b t) -> p b t", t=BLK)
                    if s == "v decay":
                        dve.wait_ge(act_done, A("act", f"gla ln {h}"))
                        if h > 0:
                            dve.wait_ge(act_done, A("act", f"gla eb {h - 1}"))
                            dve.wait_ge(pool_done, A("pool", f"gla kend {h - 1}"))
                        link(dve.scalar_tensor_tensor(lsig[:, :], zlog[:, :], 0.0, ztmp[:, :], ALU.min, ALU.subtract), f"gla lg {h}")
                        for a, n in SUPER:
                            dve.tensor_tensor_scan(bcum[:, a:a + n], c_("ones")[:, 0:n], lsig[:, a:a + n], 0.0, ALU.mult, ALU.add
                                                   ).then_inc(dve_done, st.done("dve", f"gla scan {h}" if a == SAMP0 else None))
                    if s.startswith("v diag"):
                        for j in range(4 * int(s[-1]), 4 * int(s[-1]) + 4):
                            w = BLK - j
                            e = ediag_of(j).rearrange("p (b t) -> p b t", t=w)
                            dve.wait_ge(act_done, A("act", f"gla e {h} {j}"))
                            if j == 0:
                                dve.wait_ge(act_done, A("act", f"evac {UIDX['ck', h]} 0 1"))
                            link(dve.tensor_tensor(e, e, k3[:, :, j:j + 1].to_broadcast([P, NBLK, w]), ALU.mult))
                            dve.tensor_tensor(e, e, q3[:, :, j:], ALU.mult).then_inc(dve_done, st.done("dve", f"gla e {h} {j}"))
                    if s == "v farq":
                        dve.wait_ge(act_done, A("act", f"gla far q {h}"))
                        qf = qfar[:, :].rearrange("p (b i t) -> p b i t", b=4, t=BLK)
                        q4 = q[:, 0:SEQ].rearrange("p (b i t) -> p b i t", b=4, t=BLK)[:, :, 1:, :]
                        dve.tensor_tensor(qf, qf, q4, ALU.mult).then_inc(dve_done, st.done("dve"))
                        dve.tensor_tensor(qfar_s[:, :], qfar_s[:, :], q[:, SAMP0 + BLK:T], ALU.mult).then_inc(dve_done, st.done("dve"))
                        dve.tensor_tensor(kfar_s[:, :], kfar_s[:, :], kk[:, SAMP0:SAMP0 + BLK], ALU.mult).then_inc(dve_done, st.done("dve", f"gla far s {h}"))
                    if s == "v far":
                        for i in range(7, 0, -1):
                            dve.wait_ge(act_done, A("act", f"gla far {h} {i}"))
                            kf = kfar_of(i).rearrange("p (b s) -> p b s", b=4)
                            k4 = kk[:, 0:SEQ].rearrange("p (b s) -> p b s", b=4)[:, :, 0:16 * i]
                            dve.tensor_tensor(kf, kf, k4, ALU.mult).then_inc(dve_done, st.done("dve", f"gla far {h} {i}"))
                    if s == "v kend":
                        dve.wait_ge(act_done, A("act", f"gla kend {h}"))
                        dve.tensor_tensor(kend[:, :], kend[:, :], kk, ALU.mult).then_inc(dve_done, st.done("dve", f"gla kend {h}"))
                        dve.wait_ge(act_done, A("act", f"gla eb {h}"))
                        if h > 0:
                            dve.wait_ge(pe_done, A("pe", f"gla o {h - 1}"))
                        else:
                            dve.wait_ge(spilled, 16)
                        dve.tensor_tensor(qe[:, :], ebl[:, :], q, ALU.mult).then_inc(dve_done, st.done("dve", f"gla qe {h}"))
                    if s == "v amat":
                        if h > 0:
                            dve.wait_ge(pe_done, A("pe", f"gla o {h - 1}"))
                        dve.wait_ge(pe_done, A("pe", f"gla diag {h} 15"))
                        dve.wait_ge(pe_done, A("pe", f"gla far {h} 1"))
                        half = BLK * DIAG_SPLIT
                        bm = c_("blockmask").rearrange("p (a t) -> p a t", a=1).to_broadcast([P, 2, 128])
                        for i, bank in enumerate((S0, S1)):
                            dve.tensor_tensor(amat[:, half * i:half * i + half].rearrange("p (b t) -> p b t", b=2),
                                              ps[:, bank, 0:half].rearrange("p (b t) -> p b t", b=2), bm, ALU.mult
                                              ).then_inc(dve_done, st.done("dve"))
                        dve.tensor_copy(amat[0:META, META0:SAMP0], ps[0:META, S1, half:half + META]).then_inc(dve_done, st.done("dve"))
                        link(dve.tensor_tensor(amat[0:DEC, SAMP0:T], ps[0:DEC, S1, half + META:half + META + DEC],
                                               c_("blockmask", DEC)[:, 0:DEC], ALU.mult))
                        am = amat[:, 0:SEQ].rearrange("p (b i t) -> p b i t", b=4, t=BLK)
                        far = ps[:, T0, :].rearrange("p (b i t) -> p b i t", b=4, t=BLK)
                        for i in range(1, 8):
                            rows = slice(0, 16 * i)
                            dve.tensor_tensor(am[rows, :, i, :], am[rows, :, i, :], far[rows, :, i, :], ALU.add).then_inc(dve_done, st.done("dve"))
                        last = slice(SAMP0 + BLK, T)
                        dve.tensor_tensor(amat[0:BLK, last], amat[0:BLK, last], ps[0:BLK, T1, 0:BLK], ALU.add
                                          ).then_inc(dve_done, st.done("dve", f"gla amat {h}"))
                    if s == "v silu":
                        dve.wait_ge(act_done, A("act", f"gla gate ln {h}"))
                        dve.scalar_tensor_tensor(gsig[:, :, :], pr[:, 4:6, :], 0.0, gsig[:, :, :], ALU.min, ALU.subtract
                                                 ).then_inc(dve_done, st.done("dve", f"gla gate {h}"))
                        dve.wait_ge(act_done, A("act", f"gla gate {h}"))
                        dve.tensor_tensor(gsig[:, :, :], gsig[:, :, :], pr[:, 4:6, :], ALU.mult).then_inc(dve_done, st.done("dve", f"gla silu {h}"))
                    if s == "v state":
                        dve.wait_ge(pe_done, A("pe", f"gla kv {h}"))
                        dve.wait_ge(pool_done, A("pool", "gla zero"))
                        dve.wait_ge(state_loaded, 16 * (h + 1))
                        if h > 0:
                            dve.wait_ge(stored, 32 * h)
                        for sb in range(6):
                            a, n = SUPER[sb]
                            bank = (S0, S1, T0)[sb // 2]
                            kv = ps[:, bank, 256 * (sb % 2):256 * (sb % 2) + 256]
                            link(dve.scalar_tensor_tensor(state[:, STATE_OUT[sb], :], state[:, STATE_IN[sb], :],
                                                          ebl[:, a + n - 1:a + n], kv, ALU.mult, ALU.add),
                                 f"gla state {h}" if sb == 5 else None)
                    if s == "v o":
                        dve.wait_ge(act_done, A("act", f"gla sq {h}"))
                        dve.tensor_tensor(gsq[:, 0, :], gsq[:, 0, :], gsq[:, 1, :], ALU.add).then_inc(dve_done, st.done("dve", f"gla sum {h}"))
                    if s == "v out":
                        dve.wait_ge(act_done, A("act", f"gla rstd {h}"))
                        for i in range(2):
                            link(dve.scalar_tensor_tensor(oh[:, i, :], oh[:, i, :], p_("g_gla", i), rstd[:, :], ALU.mult, ALU.mult))
                            dve.tensor_tensor(oc_raw[:, 2 * h + i, :], oh[:, i, :], gsig[:, i, :], ALU.mult
                                              ).then_inc(dve_done, st.done("dve", f"gla out {h} {i}"))
                        for k in range(2 * h, 2 * h + 2):
                            dve.wait_ge(act_done, A("act", f"oc hi {k}"))
                            dve.tensor_tensor(oc_lo[:, k, :], oc_raw[:, k, :], oc_hi[:, k, :].bitcast(F32), ALU.subtract
                                              ).then_inc(dve_done, st.done("dve", f"oc lo {k}"))

                def rotate(dst, raw, pair, rows, name, last):
                    c2 = c_("cos", rows).rearrange("p (a n) -> p a n", a=2)
                    s2 = c_("sin", rows).rearrange("p (a n) -> p a n", a=2)
                    t = rtmp[0:rows, :].rearrange("p (a n) -> p a n", a=2)
                    dve.tensor_tensor(dst.rearrange("p (a n) -> p a n", a=2), raw.rearrange("p (a n) -> p a n", a=2), c2, ALU.mult).then_inc(dve_done, st.done("dve"))
                    dve.tensor_tensor(t, ps[0:rows, pair, 0:HALF], s2, ALU.mult).then_inc(dve_done, st.done("dve", name))
                    dve.wait_ge(dve_done, st.count["dve"])
                    link(dve.tensor_tensor(dst, dst, rtmp[0:rows, :], ALU.add), last)

                def prep_a(s):
                    if s in ("square", "load"):
                        return
                    if s == 0:
                        dve.wait_ge(act_done, A("act", "c rstd"))
                        for k in range(KL):
                            dve.scalar_tensor_tensor(ckv[:, k, :], ckv[:, k, :], p_("g_kv", k), rstd[:, :], ALU.mult, ALU.mult
                                                     ).then_inc(dve_done, st.done("dve", f"c {k}"))
                    if s == 1:
                        dve.wait_ge(stored, 32 * C_HEADS)
                        dve.wait_ge(pe_done, A("pe", "prep a 1"))
                        rotate(krot[0:96, :], kra[0:96, :], prep_pair(1), 96, "prep a 1", None)
                        dve.tensor_copy(krot[96:128, :], krot[0:32, :]).then_inc(dve_done, st.done("dve", "krot"))
                    if s in (2, 3):
                        dve.wait_ge(pe_done, A("pe", f"prep a {s}"))
                        rotate(qrot[:, s - 2, :], qr[:, s - 2, :], prep_pair(s), P, f"prep a {s}", f"qrot {s - 2}")
                    if s >= 4 and prep_evac(s) == "dve":
                        pair = prep_pair(s)
                        dve.wait_ge(pe_done, A("pe", f"prep a {s}"))
                        if s < 8:
                            dve.tensor_copy(kn[:, s - 4, :].rearrange("p (a n) -> p a n", a=2), ps[:, pair, 0:HALF]
                                            ).then_inc(dve_done, st.done("dve", f"prep a {s}"))
                        elif s < 10:
                            dve.tensor_copy(kn_c[:, 2 * (s - 8):2 * (s - 8) + 2, :], ps[:, pair, 0:CKEYS]
                                            ).then_inc(dve_done, st.done("dve", f"prep a {s}"))
                        else:
                            for i, (_, _, n, dst) in enumerate(VA_TILES[s - 10]):
                                dve.tensor_copy(dst, ps[0:n, pair.start + i, :]).then_inc(dve_done, st.done("dve", f"prep a {s}" if i == len(VA_TILES[s - 10]) - 1 else None))

                def att(br, j, up):
                    n = len(JOBS[br])
                    if j < n:
                        _, t, i = JOBS[br][j]
                        pb = prob_view(br, j)
                        nk = key_count(br, i)
                        k = 2 if br == "a" else 4
                        rows = P if i < 4 else MIXED
                        sm = stat[0:rows, j % 2, :]
                        dve.wait_ge(pe_done, A("pe", f"{br} scores {j}"))
                        if j >= 2:
                            dve.wait_ge(pe_done, A("pe", f"{br} turn {j - 2}"))
                            dve.wait_ge(pool_done, A("pool", f"{br} prob {j - 2}"))
                        elif br == "b":
                            dve.wait_ge(pe_done, A("pe", f"a turn {len(jobs) - 1}"))
                        if br == "a" and i < 4:
                            nf = 128 * (i + 1)
                            link(dve.memset(ps[0:CHUNK, S0:S1 + 1, nf - CHUNK:nf], NEG))
                        if br == "a" and i < 3:
                            link(dve.tensor_reduce(sm[:, 4:6], ps[:, S0:S1 + 1, 0:nk], AX.X, ALU.max))
                            mx = sm[:, 4:6].rearrange("p (a n) -> p a n", n=1)
                            dve.tensor_tensor(pb[:, :, :], ps[:, S0:S1 + 1, 0:nk], mx.to_broadcast([P, 2, nk]), ALU.subtract
                                              ).then_inc(dve_done, st.done("dve", f"a shift {j}"))
                        elif br == "a" and i == 3:
                            nf = nk - META
                            mt = ps[0:rows, M_, 0:32].rearrange("p (a n) -> p a n", a=2)
                            dve.tensor_reduce(sm[:, 0:2], ps[:, S0:S1 + 1, 0:nf], AX.X, ALU.max).then_inc(dve_done, st.done("dve"))
                            link(dve.tensor_reduce(sm[:, 2:4], mt, AX.X, ALU.max))
                            link(dve.tensor_tensor(sm[:, 4:6], sm[:, 0:2], sm[:, 2:4], ALU.max))
                            mx = sm[:, 4:6].rearrange("p (a n) -> p a n", n=1)
                            dve.tensor_tensor(pb[:, :, 0:nf], ps[:, S0:S1 + 1, 0:nf], mx.to_broadcast([P, 2, nf]), ALU.subtract).then_inc(dve_done, st.done("dve"))
                            dve.tensor_tensor(pb[:, :, nf:nk], mt, mx.to_broadcast([P, 2, META]), ALU.subtract
                                              ).then_inc(dve_done, st.done("dve", f"a shift {j}"))
                        elif br == "a":
                            ms = c_("mask_s", MIXED).rearrange("p (a n) -> p a n", a=1).to_broadcast([MIXED, 2, 320])
                            link(dve.tensor_tensor(pb[0:rows, :, :], ps[0:rows, S0:S1 + 1, 0:320], ms, ALU.add))
                            link(dve.tensor_reduce(sm[:, 4:6], pb[0:rows, :, :], AX.X, ALU.max))
                            mx = sm[:, 4:6].rearrange("p (a n) -> p a n", n=1)
                            dve.tensor_tensor(pb[0:rows, :, :], pb[0:rows, :, :], mx.to_broadcast([rows, 2, 320]), ALU.subtract
                                              ).then_inc(dve_done, st.done("dve", f"a shift {j}"))
                        else:
                            for g in range(4):
                                if i < 4:
                                    src = ps[:, S0 + g // 2, 208 * (g % 2) + 208 - nk:208 * (g % 2) + 208]
                                    dist = c_("dist")[:, 208 - nk:208]
                                else:
                                    src = ps[0:rows, S0 + g // 2, 192 * (g % 2):192 * (g % 2) + 192]
                                    dist = c_("dist_s", rows)
                                slope = 2.0 ** -(4 * t + g + 1)
                                dve.scalar_tensor_tensor(pb[0:rows, g, 0:nk], dist, -slope / B_SCALE, src, ALU.mult, ALU.add
                                                         ).then_inc(dve_done, st.done("dve", f"b bias {j}" if g == 3 else None))
                            link(dve.tensor_scalar(pb[0:rows, :, nk], p_("sinks", 4 * t, 4, rows), 1.0 / B_SCALE, None, ALU.mult))
                            link(dve.tensor_reduce(sm[:, 4:8], pb[0:rows, :, :], AX.X, ALU.max))
                            mx = sm[:, 4:8].rearrange("p (a n) -> p a n", n=1)
                            dve.tensor_tensor(pb[0:rows, :, :], pb[0:rows, :, :], mx.to_broadcast([rows, 4, nk + 1]), ALU.subtract
                                              ).then_inc(dve_done, st.done("dve", f"b shift {j}"))
                    if up is not None:
                        evac(up, [0])
                    if 1 <= j <= n:
                        jj = j - 1
                        _, t, i = JOBS[br][jj]
                        if jj >= 1:
                            dve.wait_ge(pe_done, A("pe", f"{br} values {jj - 1}"))
                        dve.wait_ge(pe_done, A("pe", f"{br} turn {jj}"))
                        if br == "a":
                            if i < 4:
                                nf = 128 * (i + 1)
                                dve.tensor_copy(ptf[:, :, 0:nf], ps[:, T0:T1 + 1, 0:nf]).then_inc(dve_done, st.done("dve"))
                                dve.tensor_copy(ptm[:, 0:256], ps[0:META, O_, 256:512]).then_inc(dve_done, st.done("dve", f"a turned {jj}"))
                            else:
                                dve.tensor_copy(ptf[:, :, 0:96], ps[:, T0:T1 + 1, 0:96]).then_inc(dve_done, st.done("dve"))
                                dve.tensor_copy(ptf[0:MIXED, :, 96:144], ps[0:MIXED, T0:T1 + 1, 96:144]).then_inc(dve_done, st.done("dve"))
                                dve.tensor_copy(ptf[0:META, :, 144:192], ps[0:META, T0:T1 + 1, 144:192]).then_inc(dve_done, st.done("dve", f"a turned {jj}"))
                        elif i < 4:
                            dve.tensor_copy(ptf[:, 0, :], ps[:, T0, :]).then_inc(dve_done, st.done("dve"))
                            r = slice(0 if i > 0 else 64, 80)
                            dve.tensor_copy(ptf[r, 1, :], ps[r, T1, :]).then_inc(dve_done, st.done("dve", f"b turned {jj}"))
                        else:
                            dve.tensor_copy(ptf[:, 0, 0:192], ps[:, T0, 0:192]).then_inc(dve_done, st.done("dve"))
                            dve.tensor_copy(ptf[0:MIXED, 1, 0:192], ps[0:MIXED, T1, 0:192]).then_inc(dve_done, st.done("dve"))
                            dve.tensor_copy(ptm[:, 0:192], ps[0:META, M_, 0:192]).then_inc(dve_done, st.done("dve", f"b turned {jj}"))
                    if j >= 2:
                        jj = j - 2
                        _, t, i = JOBS[br][jj]
                        dve.wait_ge(pe_done, A("pe", f"{br} values {jj}"))
                        qc = slice(128 * i, 128 * i + 128) if i < 4 else slice(META0, T)
                        w = 128 if i < 4 else MIXED
                        if br == "a":
                            dve.tensor_copy(oa_raw[:, t, qc], ps[:, O_, 0:w]).then_inc(dve_done, st.done("dve", f"a o {jj}"))
                        else:
                            r = slice(64 * t, 64 * t + 64)
                            dve.tensor_copy(ob_raw[r, :, qc], ps[r, O_, 0:4 * w].rearrange("p (g n) -> p g n", g=4)
                                            ).then_inc(dve_done, st.done("dve", f"b o {jj}"))
                    if j < n:
                        k = 2 if br == "a" else 4
                        sm = stat[0:P if JOBS[br][j][2] < 4 else MIXED, j % 2, :]
                        dve.wait_ge(act_done, A("act", f"{br} exp {j}"))
                        dve.reciprocal(sm[:, 12:12 + k], sm[:, 8:8 + k]).then_inc(dve_done, st.done("dve", f"{br} rsum {j}"))

                for at_step, step in enumerate(order):
                    if step[0] == "dense":
                        early = order[at_step - 1][0] == "att" and UNITS[step[1]][0] in ("up_a", "up_b")
                        evac(step[1], [1] if early else None)
                    elif step[0] == "norm":
                        norm(step[1])
                    elif step[0] == "tokens":
                        tokens(step[1])
                    elif step[0] == "gla":
                        gla(step[1], step[2])
                    elif step[0] == "prep_a":
                        prep_a(step[1])
                    elif step[0] == "prep_b":
                        if step[1] == 1:
                            dve.wait_ge(pe_done, A("pe", "b vtok"))
                            dve.tensor_copy(v_prev[:, :, :].rearrange("p a n -> p (a n)"), ps[0:80, T1, 0:384]).then_inc(dve_done, st.done("dve"))
                            dve.tensor_copy(v_mix[:, :], ps[0:MIXED, M_, 0:128]).then_inc(dve_done, st.done("dve", "b vtok"))
                    elif step[0] == "att":
                        after = order[at_step + 1]
                        early = after[0] == "dense" and UNITS[after[1]][0] in ("up_a", "up_b")
                        att(step[1], step[2], after[1] if early else None)
                    elif step[0] == "split_y":
                        for k in Y_SPLIT[step[1]]:
                            if lo_engine("y", k) == "dve":
                                dve.wait_ge(act_done, A("act", f"y hi {k}"))
                                dve.tensor_tensor(h_lo[:, k, :], y[:, k, :], h_hi[:, k, :].bitcast(F32), ALU.subtract
                                                  ).then_inc(dve_done, st.done("dve", f"y lo {k}"))

            @block.gpsimd
            def _(pool):
                def link(ins, name=None):
                    ins.then_inc(pool_done, st.done("pool", name))
                    pool.wait_ge(pool_done, st.count["pool"])

                def w_lo(u):
                    slot = u % WSLOTS
                    pool.wait_ge(act_done, A("act", f"w hi {u}"))
                    pool.tensor_tensor(wlo[slot][:, :], wraw[slot][:, :], whi[slot][:, :].bitcast(F32), ALU.subtract
                                       ).then_inc(pool_done, st.done("pool", f"w lo {u}"))

                def lo_tile(lo, raw, hi, name, hname):
                    pool.wait_ge(act_done, A("act", hname))
                    pool.tensor_tensor(lo, raw, hi.bitcast(F32), ALU.subtract).then_inc(pool_done, st.done("pool", name))

                def evac(u):
                    kind, n = UNITS[u]
                    if kind == "ff1":
                        s = hid[n // 8 % 2]
                        lo_tile(s[1][:, n % 8, :], s[0][:, n % 8, :], s[2][:, n % 8, :], f"hid lo {n}", f"hid hi {n}")
                    if kind in ("up_a", "up_b"):
                        for o in range(2):
                            if y_engine(kind[-1], n + o) != "pool":
                                continue
                            pool.wait_ge(dve_done, A("dve", f"evac {u} {o} 1"))
                            pool.tensor_tensor(y[:, n + o, :], y[:, n + o, :], sig[:, o, :], ALU.add
                                               ).then_inc(pool_done, st.done("pool", f"y {kind[-1]} {n + o}"))

                def norm(which):
                    for k in range(KD):
                        if x_engine(k) == "pool":
                            pool.wait_ge(dve_done, A("dve", f"nrm {which} {k}"))
                            if k == 1 and which == "post_mix":
                                pool.wait_ge(x_back, 16)
                            pool.tensor_tensor(x[:, k, :], x[:, k, :], norm_src[which][:, k, :], ALU.add
                                               ).then_inc(pool_done, st.done("pool", f"x {which} {k}"))

                def mean(which):
                    if which == "next":
                        for slot in (1, 0):
                            lo_tile(wlo[slot][:, :], wraw[slot][:, :], whi[slot][:, :], f"ahead lo {slot}", f"ahead hi {slot}")
                        pool.wait_ge(pool_done, st.count["pool"])

                def gla(h, s):
                    b3 = bcum[:, :].rearrange("p (b t) -> p b t", t=BLK)
                    if s == "v decay":
                        if h > 0:
                            pool.wait_ge(dve_done, A("dve", f"gla state {h - 1}"))
                            pool.wait_ge(pe_done, A("pe", f"gla o {h - 1}"))
                        if h == 0:
                            link(pool.memset(state[:, 0, :], 0.0), "gla zero")
                    if s.startswith("v diag"):
                        for j in range(4 * int(s[-1]), 4 * int(s[-1]) + 4):
                            w = BLK - j
                            e = ediag_of(j).rearrange("p (b t) -> p b t", t=w)
                            if j == 0:
                                pool.wait_ge(dve_done, A("dve", f"gla scan {h}"))
                            pool.tensor_tensor(e, b3[:, :, j:], b3[:, :, j:j + 1].to_broadcast([P, NBLK, w]), ALU.subtract
                                               ).then_inc(pool_done, st.done("pool", f"gla d {h} {j}"))
                    if s == "v farq":
                        if h > 0:
                            pool.wait_ge(pe_done, A("pe", f"gla far {h - 1} 1"))
                        b4 = bcum[:, 0:SEQ].rearrange("p (b i t) -> p b i t", b=4, t=BLK)
                        qf = qfar[:, :].rearrange("p (b i t) -> p b i t", b=4, t=BLK)
                        for b in range(4):
                            pool.tensor_tensor(qf[:, b], b4[:, b, 1:, :], b4[:, b, 0:7, 15:16].to_broadcast([P, 7, BLK]), ALU.subtract
                                               ).then_inc(pool_done, st.done("pool"))
                        ref = bcum[:, SAMP0 + 15:SAMP0 + 16].to_broadcast([P, BLK])
                        pool.tensor_tensor(qfar_s[:, :], bcum[:, SAMP0 + BLK:T], ref, ALU.subtract).then_inc(pool_done, st.done("pool"))
                        pool.tensor_tensor(kfar_s[:, :], ref, bcum[:, SAMP0:SAMP0 + BLK], ALU.subtract).then_inc(pool_done, st.done("pool", f"gla far q {h}"))
                    if s == "v far":
                        b4 = bcum[:, 0:SEQ].rearrange("p (b s) -> p b s", b=4)
                        for i in range(7, 0, -1):
                            kf = kfar_of(i).rearrange("p (b s) -> p b s", b=4)
                            pool.tensor_tensor(kf, b4[:, :, 16 * i - 1:16 * i].to_broadcast([P, 4, 16 * i]), b4[:, :, 0:16 * i], ALU.subtract
                                               ).then_inc(pool_done, st.done("pool", f"gla far {h} {i}"))
                    if s == "v kend":
                        pool.wait_ge(dve_done, A("dve", f"gla lg {h}"))
                        if h > 0:
                            pool.wait_ge(pe_done, A("pe", f"gla ktok {h - 1} 1"))
                        for i, (a, n) in enumerate(SUPER):
                            pool.tensor_tensor(kend[:, a:a + n], bcum[:, a + n - 1:a + n].to_broadcast([P, n]), bcum[:, a:a + n], ALU.subtract
                                               ).then_inc(pool_done, st.done("pool", f"gla kend {h}" if i == 5 else None))
                def att(br, j):
                    n = len(JOBS[br])
                    if j < n:
                        _, t, i = JOBS[br][j]
                        pb = prob_view(br, j)
                        k = 2 if br == "a" else 4
                        rows = P if i < 4 else MIXED
                        w = pb.shape[2]
                        pool.wait_ge(dve_done, A("dve", f"{br} rsum {j}"))
                        rs = stat[0:rows, j % 2, 12:12 + k].rearrange("p (a n) -> p a n", n=1).to_broadcast([rows, k, w])
                        pool.tensor_tensor(pb[0:rows, :, :], pb[0:rows, :, :], rs, ALU.mult).then_inc(pool_done, st.done("pool", f"{br} prob {j}"))
                    if br == "a" and j >= 6 and (j - 6) % 5 == 0:
                        t = (j - 6) // 5
                        lo_tile(oa_lo[:, t, :], oa_raw[:, t, :], oa_hi[:, t, :], f"oa lo {t}", f"oa hi {t}")
                    if br == "b" and j >= 7:
                        i = j - 7
                        lo_tile(ob_lo[:, :, BLOCKS[i]], ob_raw[:, :, BLOCKS[i]], ob_hi[:, :, BLOCKS[i]], f"ob lo {i}", f"ob hi {i}")

                for step in order:
                    if step[0] == "dense":
                        evac(step[1])
                        if step[1] + 2 < NU:
                            w_lo(step[1] + 2)
                    elif step[0] == "norm":
                        norm(step[1])
                    elif step[0] == "mean":
                        mean(step[1])
                    elif step[0] == "tokens":
                        name = "h" if step[1] == "pre_mix" else "h2"
                        for k in range(KD):
                            if lo_engine(name, k) == "pool":
                                lo_tile(h_lo[:, k, :], h_raw[:, k, :], h_hi[:, k, :], f"{name} lo {k}", f"{name} hi {k}")
                    elif step[0] == "gla":
                        gla(step[1], step[2])
                    elif step[0] == "att":
                        att(step[1], step[2])
                    elif step[0] == "split_y":
                        for k in Y_SPLIT[step[1]]:
                            if lo_engine("y", k) == "pool":
                                lo_tile(h_lo[:, k, :], y[:, k, :], h_hi[:, k, :], f"y lo {k}", f"y hi {k}")
        with nc.Fori(0, DEPTH) as l:
            with nc.Block() as block:
                layer(l, block)
            for s_ in block_sems:
                nc.sync.sem_clear(s_)
            nc.all_engine_barrier()

        with nc.Block() as block:
            @block.sync
            def _(sp):
                sp.dma_start(io["y_out"].rearrange("(k p) t -> p k t", p=P), x[:, :, :]).then_inc(last_stored, 16)
                sp.wait_ge(last_stored, 16)
    return st.seen


def shape_constants():
    c = np.zeros((P, NCONST), np.float32)

    def put(name, value, rows=P):
        a, w = CONST[name]
        c[0:rows, a:a + w] = value

    put("ident", np.eye(P))
    put("ones_d", 1.0 / D)
    put("ones_v", 1.0 / C_DV)
    perm = np.zeros((P, P))
    for j in range(P):
        if j % A_ROPE < A_ROPE // 2:
            perm[j + A_ROPE // 2, j] = -1.0
        else:
            perm[j - A_ROPE // 2, j] = 1.0
    put("perm", perm)
    put("selrep", (np.arange(144) % BLK == BLK - 1).astype(np.float32)[None])
    blk = np.arange(P) // BLK
    put("blockmask", (blk[:, None] == blk[None, :]).astype(np.float32))
    half = A_ROPE // 2
    inv = np.float32(10000.0) ** (-np.arange(half, dtype=np.float32) / np.float32(half))
    pos = np.concatenate([np.arange(SEQ), np.zeros(META), PAST + np.arange(DEC)]).astype(np.float32)
    ang = pos[None, :] * inv[np.arange(P) % half][:, None].astype(np.float32)
    put("cos", np.cos(ang.astype(np.float32)))
    put("sin", np.sin(ang.astype(np.float32)))
    far = 1e34
    r = np.arange(P)[:, None]
    prev, own = np.arange(-CHUNK, 0)[None], np.arange(P)[None]
    put("dist", np.concatenate([np.where(r < CHUNK, np.abs(r - prev), far),
                                np.where(own // CHUNK <= r // CHUNK, np.abs(r - own), far), np.zeros((P, META))], 1))
    d = np.full((MIXED, 192), far)
    q = PAST + np.arange(DEC)[:, None]
    k = PAST - WIN + np.arange(WIN + DEC)[None]
    seen = (k // CHUNK <= q // CHUNK) & (k // CHUNK > q // CHUNK - WIN // CHUNK)
    dist = np.where(seen, np.abs(q - k), far)
    d[META:, 0:WIN], d[META:, WIN + MIXED - DEC + META:] = dist[:, 0:WIN], dist[:, WIN:]
    d[META:, WIN:WIN + META] = 0.0
    d[0:META, WIN + META:WIN + 2 * META] = 0.0
    put("dist_s", d, MIXED)
    m = np.full((MIXED, 320), NEG)
    m[META:, 0:CKEYS] = 0.0
    m[META:, CKEYS + META:] = 0.0
    m[0:META, CKEYS:CKEYS + META] = 0.0
    put("mask_s", m, MIXED)
    put("ones", 1.0)
    put("eps", EPS)
    return c


def pack_units(i, l):
    w_in = i["w_in"][l]
    sizes = [512, 256, 256, 32, 512, 128, 128, 512, 512, 1024, 16, 1024, 3072]
    edge = np.concatenate([[0], np.cumsum(sizes)])
    part = {n: w_in[:, edge[j]:edge[j + 1]] for j, n in enumerate(
        ("qn", "qr", "ckv", "kr", "qb", "kb", "vb", "cq", "ck", "cv", "alr", "cg", "gate"))}
    qb = part["qb"].reshape(D, B_KV, B_G, B_HD).transpose(0, 2, 1, 3).reshape(D, -1)
    up_b = i["w_up_b"][l].reshape(B_KV, B_G, B_HD, D).transpose(1, 0, 2, 3).reshape(-1, D)
    out = np.empty((NU, P, 1024), np.float32)
    for u, (kind, n) in enumerate(UNITS):
        c = slice(128 * n, 128 * n + 128)
        if kind == "kralr":
            m = np.concatenate([part["kr"]] * 3 + [part["alr"], np.zeros((D, 16), np.float32)], 1)
        elif kind == "qb":
            m = qb[:, c]
        elif kind.startswith("gate"):
            b = "abc".index(kind[-1])
            m = part["gate"][:, D * b + 128 * n:D * b + 128 * n + 128]
        elif kind == "up_c":
            m = i["w_up_c"][l][:, c]
        elif kind in ("up_a", "up_b"):
            m = (i["w_up_a"][l] if kind == "up_a" else up_b)[:, 128 * n:128 * n + 256]
        elif kind == "out":
            m = i["w_out"][l][:, c]
        elif kind == "ff1":
            m = i["w_ff1"][l][:, c]
        elif kind == "ff2":
            g, t = n // 8, n % 8
            m = i["w_ff2"][l][D * g:D * g + D, 128 * t:128 * t + 128]
        else:
            m = part[kind][:, c]
        k = m.shape[0] // P
        out[u] = m.reshape(k, P, m.shape[1]).transpose(1, 0, 2).reshape(P, 1024)
    return out


def pack_params(i, l):
    p = np.zeros((P, NPARAM), np.float32)

    def put(name, v):
        a, w = PARAM[name]
        p[:, a:a + w] = v

    for name in ("g_post_mix", "g_pre_mlp", "g_post_mlp", "g_kv", "g_gla", "b_alpha"):
        put(name, i[name][l].reshape(-1, P).T)
    put("sinks", np.repeat(i["b_sinks"][l][None], P, 0))
    return p


OUTPUTS = {"y_out": (D, T), "c_out": (DEPTH, LORA, T), "kr_out": (DEPTH, A_ROPE, T),
           "kb_out": (DEPTH, P, T - 384), "vb_out": (DEPTH, P, T - 384),
           "kw_out": (DEPTH, P, WIN), "vw_out": (DEPTH, P, WIN),
           "p_state": (DEPTH * C_HEADS, C_DK, C_DV), "s_state": (DEPTH * C_HEADS, C_DK, C_DV)}


def kernel(**inputs):
    import concourse.bacc as bacc
    from concourse.bass_utils import run_bass_kernel_spmd

    i = {k: np.asarray(v) for k, v in inputs.items()}
    two = range(DEPTH)
    t = lambda a: np.ascontiguousarray(np.swapaxes(a, -1, -2))
    a_ckv = np.concatenate([i["cache_A_ckv"][:, 0], i["cache_A_meta_ckv"][:, 0]], 1)
    a_kr = np.concatenate([i["cache_A_krope"][:, 0], i["cache_A_meta_krope"][:, 0]], 1)
    b_k = i["cache_B_k"][:, 0].reshape(DEPTH, WIN, P)
    b_v = i["cache_B_v"][:, 0].reshape(DEPTH, WIN, P)
    b_mk = i["cache_B_meta_k"][:, 0].reshape(DEPTH, META, P)
    arrays = {
        "x": t(np.concatenate([i["x_prompt"][0], i["meta_tokens"], i["x_sample"][0]], 0)),
        "const": shape_constants(),
        "w": np.concatenate([pack_units(i, l) for l in two] + [np.zeros((WSLOTS, P, 1024), np.float32)]),
        "g_pre_mix": np.concatenate([i["g_pre_mix"].reshape(DEPTH, KD, P).transpose(0, 2, 1), np.zeros((1, P, KD), np.float32)]),
        "par": np.stack([pack_params(i, l) for l in two]),
        "w_alpha": i["w_alpha"], "w_uk": i["w_uk"].reshape(DEPTH, LORA, 512), "w_uv": i["w_uv"].reshape(DEPTH, LORA, 512),
        "a_ckv": t(a_ckv), "a_kr": np.tile(t(a_kr), (1, 4, 1)),
        "b_k": t(np.concatenate([b_k, b_mk], 1)), "b_v": b_v,
        "b_vm": i["cache_B_meta_v"][:, 0].reshape(DEPTH, META, P),
        "b_kw": t(b_k), "b_vw": t(b_v),
        "state": i["state_C"][:, 0].reshape(DEPTH * C_HEADS, C_DK, C_DV),
    }
    arrays = {k: np.ascontiguousarray(v) for k, v in arrays.items()}

    def program(known):
        nc = bacc.Bacc("TRN2", target_bir_lowering=False, num_devices=1)
        io = {k: nc.dram_tensor("in_" + k, v.shape, F32, kind="ExternalInput").ap() for k, v in arrays.items()}
        io.update({k: nc.dram_tensor("out_" + k, v, F32, kind="ExternalOutput").ap() for k, v in OUTPUTS.items()})
        io["x_spill"] = nc.dram_tensor("x_spill", (P, KD, T), F32, kind="Internal").ap()
        return nc, build(nc, io, known)

    _, known = program(None)
    nc, _ = program(known)
    r = run_bass_kernel_spmd(nc, [{"in_" + k: v for k, v in arrays.items()}], core_ids=[0]).results[0]
    o = {k: r["out_" + k] for k in OUTPUTS}

    y = t(o["y_out"])
    c, kr = t(o["c_out"]), t(o["kr_out"])
    kb, vb, kw, vw = t(o["kb_out"]), t(o["vb_out"]), t(o["kw_out"]), t(o["vw_out"])
    f, m, s = slice(0, SEQ), slice(META0, SAMP0), slice(SAMP0, T)
    heads = lambda a: a.reshape(DEPTH, 1, -1, B_KV, B_HD)
    states = lambda a: a.reshape(DEPTH, 1, C_HEADS, C_DK, C_DV)
    return (y[None, f], y[None, s], c[:, None, f], kr[:, None, f], c[:, None, m], kr[:, None, m],
            heads(kb[:, 0:128]), heads(vb[:, 0:128]), heads(kb[:, 128:144]), heads(vb[:, 128:144]),
            states(o["p_state"]), c[:, None, s], kr[:, None, s], heads(kw), heads(vw), states(o["s_state"]))
```
